# Optimizing a Trainium2 kernel written in Bass

```python
import math
import jax, jax.numpy as jnp
from jax import lax
import numpy as np

D_MODEL = 1024
BATCH = 1
SEQ = 512
DEPTH = 1

N_HEADS = 8
HEAD_DIM = 64
V_DIM = 2 * HEAD_DIM
QK_WIDTH = N_HEADS * 2 * HEAD_DIM
ATTN_WIDTH = N_HEADS * V_DIM
LRU_WIDTH = D_MODEL
LRU_BLOCKS = 8
LRU_BLOCK = LRU_WIDTH // LRU_BLOCKS
CONV_WIDTH = 4
LRU_C = 8.0
D_FF = 4 * D_MODEL
N_BUCKETS = 32
MAX_DISTANCE = 128
Q_BLOCK = 128
EPS = 1e-6
IN_WIDTH = 3 * QK_WIDTH // 2 * 0 + QK_WIDTH + QK_WIDTH + ATTN_WIDTH + 2 * LRU_WIDTH + 2 * D_MODEL


def rmsnorm(x, g):
    x32 = x.astype(jnp.float32)
    y = x32 * lax.rsqrt(jnp.mean(jnp.square(x32), axis=-1, keepdims=True) + EPS)
    return (y * g.astype(jnp.float32)).astype(x.dtype)

def rel_bucket(n):
    max_exact = N_BUCKETS // 2
    n = jnp.maximum(n, 0)
    nf = jnp.maximum(n, 1).astype(jnp.float32)
    large = max_exact + (jnp.log(nf / max_exact) / math.log(MAX_DISTANCE / max_exact)
                         * (N_BUCKETS - max_exact)).astype(jnp.int32)
    large = jnp.minimum(large, N_BUCKETS - 1)
    return jnp.where(n < max_exact, n, large)

def diff_attention(q, k, v, q_g, k_g, rel_bias, lam, subln_g, lambda_init):
    B, S = q.shape[0], q.shape[1]
    q = rmsnorm(q, q_g)
    k = rmsnorm(k, k_g)
    nb = S // Q_BLOCK
    qb = jnp.transpose(q.reshape(B, nb, Q_BLOCK, N_HEADS, 2, HEAD_DIM), (1, 0, 2, 3, 4, 5))
    k_pos = jnp.arange(S, dtype=jnp.int32)
    scale = HEAD_DIM ** -0.5
    bias_tab = rel_bias.astype(jnp.float32)

    def one_block(args):
        q_blk, blk = args
        q_pos = blk * Q_BLOCK + jnp.arange(Q_BLOCK, dtype=jnp.int32)
        rel = q_pos[:, None] - k_pos[None, :]
        bias = jnp.transpose(bias_tab[rel_bucket(rel)], (2, 0, 1))
        logits = jnp.einsum('bqhcd,bkhcd->bhcqk', q_blk, k).astype(jnp.float32) * scale
        logits = logits + bias[None, :, None]
        logits = jnp.where(rel >= 0, logits, -jnp.inf)
        p = jax.nn.softmax(logits, axis=-1)
        attn = p[:, :, 0] - lam * p[:, :, 1]
        return jnp.einsum('bhqk,bkhe->bqhe', attn.astype(v.dtype), v)

    out = lax.map(one_block, (qb, jnp.arange(nb, dtype=jnp.int32)))
    out = jnp.transpose(out, (1, 0, 2, 3, 4)).reshape(B, S, N_HEADS, V_DIM)
    out = rmsnorm(out, subln_g) * (1.0 - lambda_init)
    return out.reshape(B, S, ATTN_WIDTH)

def rg_lru_branch(xr, gr, conv_w, conv_b, w_a, b_a, w_x, b_x, lru_lambda):
    B, S, W = xr.shape
    gate = jax.nn.gelu(gr)
    xpad = jnp.pad(xr, ((0, 0), (CONV_WIDTH - 1, 0), (0, 0)))
    xc = conv_b
    for tap in range(CONV_WIDTH):
        xc = xc + xpad[:, tap:tap + S] * conv_w[tap]
    xblk = xc.reshape(B, S, LRU_BLOCKS, LRU_BLOCK)
    r = jax.nn.sigmoid(jnp.einsum('bsne,nef->bsnf', xblk, w_a) + b_a).reshape(B, S, W)
    i = jax.nn.sigmoid(jnp.einsum('bsne,nef->bsnf', xblk, w_x) + b_x).reshape(B, S, W)
    log_a = -LRU_C * r.astype(jnp.float32) * jax.nn.softplus(-lru_lambda.astype(jnp.float32))
    a = jnp.exp(log_a)
    mult = jnp.sqrt(-jnp.expm1(2.0 * log_a))
    b = mult * (i * xc).astype(jnp.float32)

    def combine(c1, c2):
        a1, b1 = c1
        a2, b2 = c2
        return a1 * a2, a2 * b1 + b2

    _, h = lax.associative_scan(combine, (a, b), axis=1)
    return (h.astype(xr.dtype)) * gate

def first_inputs(seed: int = 0) -> dict:
    key = jax.random.key(seed)
    ks = jax.random.split(key, 24)
    f32 = jnp.float32
    nrm = lambda k, shape, scale: jax.random.normal(k, shape, f32) * scale
    gain = lambda k, shape: 1.0 + 0.05 * jax.random.normal(k, shape, f32)
    x = jax.random.normal(ks[0], (BATCH, SEQ, D_MODEL), f32)
    u = jax.random.uniform(ks[15], (DEPTH, LRU_WIDTH), f32, minval=0.9, maxval=0.999)
    a0 = u ** (1.0 / LRU_C)
    lru_lambda = jnp.log(a0) - jnp.log1p(-a0)
    return {
        'x': x,
        'norm_mix_g': gain(ks[1], (DEPTH, D_MODEL)),
        'w_in': nrm(ks[2], (DEPTH, D_MODEL, IN_WIDTH), D_MODEL ** -0.5),
        'q_norm_g': gain(ks[3], (DEPTH, HEAD_DIM)),
        'k_norm_g': gain(ks[4], (DEPTH, HEAD_DIM)),
        'lambda_q1': nrm(ks[5], (DEPTH, HEAD_DIM), 0.1),
        'lambda_k1': nrm(ks[6], (DEPTH, HEAD_DIM), 0.1),
        'lambda_q2': nrm(ks[7], (DEPTH, HEAD_DIM), 0.1),
        'lambda_k2': nrm(ks[8], (DEPTH, HEAD_DIM), 0.1),
        'subln_g': gain(ks[9], (DEPTH, V_DIM)),
        'conv_w': nrm(ks[10], (DEPTH, CONV_WIDTH, LRU_WIDTH), CONV_WIDTH ** -0.5),
        'conv_b': nrm(ks[11], (DEPTH, LRU_WIDTH), 0.02),
        'w_rg_a': nrm(ks[12], (DEPTH, LRU_BLOCKS, LRU_BLOCK, LRU_BLOCK), LRU_BLOCK ** -0.5),
        'b_rg_a': nrm(ks[13], (DEPTH, LRU_BLOCKS, LRU_BLOCK), 0.02),
        'w_rg_x': nrm(ks[14], (DEPTH, LRU_BLOCKS, LRU_BLOCK, LRU_BLOCK), LRU_BLOCK ** -0.5),
        'b_rg_x': nrm(ks[16], (DEPTH, LRU_BLOCKS, LRU_BLOCK), 0.02),
        'lru_lambda': lru_lambda,
        'w_proj_attn': nrm(ks[17], (DEPTH, ATTN_WIDTH, D_MODEL), ATTN_WIDTH ** -0.5),
        'w_proj_rnn': nrm(ks[18], (DEPTH, LRU_WIDTH, D_MODEL), LRU_WIDTH ** -0.5),
        'w_out': nrm(ks[19], (DEPTH, D_MODEL, D_MODEL), D_MODEL ** -0.5),
        'norm_mlp_g': gain(ks[20], (DEPTH, D_MODEL)),
        'w_up': nrm(ks[21], (DEPTH, D_MODEL, D_FF), D_MODEL ** -0.5),
        'w_down': nrm(ks[22], (DEPTH, D_FF, D_MODEL), D_FF ** -0.5),
        'rel_bias': nrm(ks[23], (N_BUCKETS, N_HEADS), 0.5),
    }

def first_block(x, norm_mix_g, w_in, q_norm_g, k_norm_g, lambda_q1, lambda_k1, lambda_q2, lambda_k2,
              subln_g, conv_w, conv_b, w_rg_a, b_rg_a, w_rg_x, b_rg_x, lru_lambda,
              w_proj_attn, w_proj_rnn, w_out, norm_mlp_g, w_up, w_down, rel_bias):
    B, S, _ = x.shape
    offs = np.cumsum([QK_WIDTH, QK_WIDTH, ATTN_WIDTH, LRU_WIDTH, LRU_WIDTH, D_MODEL]).tolist()
    for l in range(DEPTH):
        lambda_init = 0.8 - 0.6 * math.exp(-0.3 * l)
        h = rmsnorm(x, norm_mix_g[l])
        proj = jnp.einsum('bsd,de->bse', h, w_in[l])
        q, k, v, xr, gr, g_attn, g_rnn = jnp.split(proj, offs, axis=-1)
        q = q.reshape(B, S, N_HEADS, 2, HEAD_DIM)
        k = k.reshape(B, S, N_HEADS, 2, HEAD_DIM)
        v = v.reshape(B, S, N_HEADS, V_DIM)
        lam = (jnp.exp(jnp.sum(lambda_q1[l].astype(jnp.float32) * lambda_k1[l].astype(jnp.float32)))
               - jnp.exp(jnp.sum(lambda_q2[l].astype(jnp.float32) * lambda_k2[l].astype(jnp.float32)))
               + lambda_init)
        attn_out = diff_attention(q, k, v, q_norm_g[l], k_norm_g[l], rel_bias, lam, subln_g[l], lambda_init)
        rnn_out = rg_lru_branch(xr, gr, conv_w[l], conv_b[l], w_rg_a[l], b_rg_a[l],
                                w_rg_x[l], b_rg_x[l], lru_lambda[l])
        y_attn = jnp.einsum('bse,ed->bsd', attn_out, w_proj_attn[l])
        y_rnn = jnp.einsum('bse,ed->bsd', rnn_out, w_proj_rnn[l])
        merged = jax.nn.sigmoid(g_attn) * y_attn + jax.nn.sigmoid(g_rnn) * y_rnn
        x = x + jnp.einsum('bsd,de->bse', merged, w_out[l])
        h2 = rmsnorm(x, norm_mlp_g[l])
        up = jnp.square(jax.nn.relu(jnp.einsum('bsd,df->bsf', h2, w_up[l])))
        x = x + jnp.einsum('bsf,fd->bsd', up, w_down[l])
    return x


N_NSA_HEADS = 8
N_NSA_KV = 2
NSA_GROUP = N_NSA_HEADS // N_NSA_KV
N_FOX_HEADS = 8
D_NSA = N_NSA_HEADS * HEAD_DIM
D_FOX = N_FOX_HEADS * HEAD_DIM
D_MIX = D_NSA + D_FOX
D_KV = N_NSA_KV * HEAD_DIM
D_PROJ = D_NSA + 6 * D_KV + 3 * N_NSA_HEADS + 3 * D_FOX + N_FOX_HEADS
CMP_BLOCK = 32
CMP_STRIDE = 16
CMP_HIDDEN = 128
SEL_BLOCK = 64
SEL_TOPK = 16
WINDOW = 512
N_EXPERTS = 32
TOP_K = 4
D_FF_2 = D_MODEL
SWIGLU_LIMIT = 7.0
SWIGLU_ALPHA = 1.702
PLE_DIM = 256
NEG = -1e30
FORCED_SCORE = 1e9


def rmsnorm_2(x, g):
    xf = x.astype(jnp.float32)
    y = xf * lax.rsqrt(jnp.mean(xf * xf, axis=-1, keepdims=True) + EPS)
    return (y * g.astype(jnp.float32)).astype(x.dtype)

def masked_softmax(logits, mask):
    logits = jnp.where(mask, logits.astype(jnp.float32), NEG)
    m = jnp.max(logits, axis=-1, keepdims=True)
    e = jnp.exp(logits - m) * mask
    return e / jnp.maximum(jnp.sum(e, axis=-1, keepdims=True), 1e-30)

def alibi_slopes(n):
    return jnp.exp2(-8.0 * jnp.arange(1, n + 1, dtype=jnp.float32) / n)

def proj_split_points():
    sizes = [D_NSA, D_KV, D_KV, D_KV, D_KV, D_KV, D_KV, 3 * N_NSA_HEADS,
             D_FOX, D_FOX, D_FOX, N_FOX_HEADS]
    pts, acc = [], 0
    for s in sizes[:-1]:
        acc += s
        pts.append(acc)
    return pts

def compress(kv, w1, w2, pe):
    B, T, G, Dh = kv.shape
    nc = (T - CMP_BLOCK) // CMP_STRIDE + 1
    idx = jnp.arange(nc)[:, None] * CMP_STRIDE + jnp.arange(CMP_BLOCK)[None, :]
    blocks = kv[:, idx] + pe[None, None, :, None, :]
    blocks = jnp.swapaxes(blocks, 2, 3).reshape(B, nc, G, CMP_BLOCK * Dh)
    return jax.nn.gelu(blocks @ w1) @ w2

def nsa_attention(q, k_c, v_c, k_s, v_s, k_w, v_w, gate_logits, slopes):
    B, T, H, Dh = q.shape
    G = k_s.shape[2]
    R = H // G
    scale = Dh ** -0.5
    nc = k_c.shape[1]
    ns = T // SEL_BLOCK
    topk = min(SEL_TOPK, ns)
    cmp_start = jnp.arange(nc) * CMP_STRIDE
    cmp_end = cmp_start + CMP_BLOCK - 1
    sel_start = jnp.arange(ns) * SEL_BLOCK
    overlap = ((cmp_start[:, None] < sel_start[None, :] + SEL_BLOCK)
               & (cmp_end[:, None] >= sel_start[None, :])).astype(jnp.float32)
    ks_blocks = k_s.reshape(B, ns, SEL_BLOCK, G, Dh).transpose(0, 3, 1, 2, 4)
    vs_blocks = v_s.reshape(B, ns, SEL_BLOCK, G, Dh).transpose(0, 3, 1, 2, 4)
    pad = jnp.zeros((B, WINDOW, G, Dh), k_w.dtype)
    kw_pad = jnp.concatenate([pad, k_w], axis=1)
    vw_pad = jnp.concatenate([pad, v_w], axis=1)
    qg = q.reshape(B, T, G, R, Dh)
    gates = jax.nn.sigmoid(gate_logits.reshape(B, T, G, R, 3))
    sl = slopes.reshape(G, R)
    b_ix = jnp.arange(B)[:, None, None, None]
    g_ix = jnp.arange(G)[None, None, :, None]
    j_sel = jnp.arange(ns)
    l_sel = jnp.arange(SEL_BLOCK)

    def block(start):
        qb = lax.dynamic_slice_in_dim(qg, start, Q_BLOCK, 1)
        gb = lax.dynamic_slice_in_dim(gates, start, Q_BLOCK, 1)
        t = start + jnp.arange(Q_BLOCK)
        lc = jnp.einsum('bqgrd,bcgd->bqgrc', qb, k_c).astype(jnp.float32) * scale
        dist_c = (t[:, None] - cmp_end[None, :]).astype(jnp.float32)
        lc = lc - sl[None, None, :, :, None] * dist_c[None, :, None, None, :]
        mask_c = (cmp_end[None, :] <= t[:, None])[None, :, None, None, :]
        p_c = masked_softmax(lc, mask_c)
        o_c = jnp.einsum('bqgrc,bcgd->bqgrd', p_c.astype(v_c.dtype), v_c)
        imp = jnp.einsum('bqgrc,cn->bqgn', p_c, overlap)
        cur = t // SEL_BLOCK
        valid = j_sel[None, :] <= cur[:, None]
        forced = valid & ((j_sel[None, :] == 0) | (j_sel[None, :] == cur[:, None])
                          | (j_sel[None, :] == cur[:, None] - 1))
        score = jnp.where(forced[None, :, None, :], FORCED_SCORE,
                          jnp.where(valid[None, :, None, :], imp, -1.0))
        _, idx = lax.top_k(score, topk)
        ks = ks_blocks[b_ix, g_ix, idx]
        vs = vs_blocks[b_ix, g_ix, idx]
        ls = jnp.einsum('bqgrd,bqgkld->bqgrkl', qb, ks).astype(jnp.float32) * scale
        pos = idx[..., None] * SEL_BLOCK + l_sel
        dist_s = (t[None, :, None, None, None] - pos)[:, :, :, None]
        ls = ls - sl[None, None, :, :, None, None] * dist_s.astype(jnp.float32)
        mask_s = jnp.broadcast_to(dist_s >= 0, ls.shape)
        flat = (B, Q_BLOCK, G, R, topk * SEL_BLOCK)
        p_s = masked_softmax(ls.reshape(flat), mask_s.reshape(flat)).reshape(ls.shape)
        o_s = jnp.einsum('bqgrkl,bqgkld->bqgrd', p_s.astype(vs.dtype), vs)
        kw = lax.dynamic_slice_in_dim(kw_pad, start, Q_BLOCK + WINDOW, 1)
        vw = lax.dynamic_slice_in_dim(vw_pad, start, Q_BLOCK + WINDOW, 1)
        s = start - WINDOW + jnp.arange(Q_BLOCK + WINDOW)
        dist_w = t[:, None] - s[None, :]
        lw = jnp.einsum('bqgrd,bsgd->bqgrs', qb, kw).astype(jnp.float32) * scale
        lw = lw - sl[None, None, :, :, None] * dist_w.astype(jnp.float32)[None, :, None, None, :]
        mask_w = ((dist_w >= 0) & (dist_w < WINDOW) & (s[None, :] >= 0))[None, :, None, None, :]
        p_w = masked_softmax(lw, mask_w)
        o_w = jnp.einsum('bqgrs,bsgd->bqgrd', p_w.astype(vw.dtype), vw)
        o = gb[..., 0:1] * o_c + gb[..., 1:2] * o_s + gb[..., 2:3] * o_w
        return o.reshape(B, Q_BLOCK, H * Dh)

    starts = jnp.arange(T // Q_BLOCK) * Q_BLOCK
    out = lax.map(block, starts)
    return out.transpose(1, 0, 2, 3).reshape(B, T, H * Dh)

def fox_attention(q, k, v, f_logit):
    B, T, H, Dh = q.shape
    scale = Dh ** -0.5
    c = jnp.cumsum(jax.nn.log_sigmoid(f_logit.astype(jnp.float32)), axis=1).transpose(0, 2, 1)
    kpos = jnp.arange(T)

    def block(start):
        qb = lax.dynamic_slice_in_dim(q, start, Q_BLOCK, 1)
        cb = lax.dynamic_slice_in_dim(c, start, Q_BLOCK, 2)
        t = start + jnp.arange(Q_BLOCK)
        l = jnp.einsum('bqhd,bshd->bhqs', qb, k).astype(jnp.float32) * scale
        l = l + (cb[..., None] - c[:, :, None, :])
        mask = (kpos[None, :] <= t[:, None])[None, None]
        pr = masked_softmax(l, mask)
        o = jnp.einsum('bhqs,bshd->bqhd', pr.astype(v.dtype), v)
        return o.reshape(B, Q_BLOCK, H * Dh)

    starts = jnp.arange(T // Q_BLOCK) * Q_BLOCK
    out = lax.map(block, starts)
    return out.transpose(1, 0, 2, 3).reshape(B, T, H * Dh)

def moe(x, w_router, b_router, w_up, b_up, w_down, b_down):
    B, T, D = x.shape
    xf = x.reshape(-1, D)
    n = xf.shape[0]
    logits = (xf @ w_router + b_router).astype(jnp.float32)
    top_v, top_i = lax.top_k(logits, TOP_K)
    w = jax.nn.softmax(top_v, axis=-1)
    flat_e = top_i.reshape(-1)
    order = jnp.argsort(flat_e)
    sorted_e = flat_e[order]
    tok = order // TOP_K
    sizes = jnp.bincount(flat_e, length=N_EXPERTS).astype(jnp.int32)
    xs = xf[tok]
    h = lax.ragged_dot(xs, w_up, sizes) + b_up[sorted_e]
    g, lin = jnp.split(h, 2, axis=-1)
    g = jnp.minimum(g, SWIGLU_LIMIT)
    lin = jnp.clip(lin, -SWIGLU_LIMIT, SWIGLU_LIMIT)
    act = g * jax.nn.sigmoid(SWIGLU_ALPHA * g) * (lin + 1.0)
    y = lax.ragged_dot(act, w_down, sizes) + b_down[sorted_e]
    y = y * w.reshape(-1)[order][:, None].astype(y.dtype)
    return jax.ops.segment_sum(y, tok, num_segments=n).reshape(B, T, D)

def second_inputs(seed: int = 0) -> dict:
    key = jax.random.key(seed)
    ks = jax.random.split(key, 32)
    L, D, E, F = DEPTH, D_MODEL, N_EXPERTS, D_FF_2
    nrm = lambda k, shape, fan: jax.random.normal(k, shape, jnp.float32) * (fan ** -0.5)
    gain = lambda k, shape: 1.0 + 0.02 * jax.random.normal(k, shape, jnp.float32)
    small = lambda k, shape, s: s * jax.random.normal(k, shape, jnp.float32)
    return {
        "x": jax.random.normal(ks[0], (BATCH, SEQ, D), jnp.float32),
        "p": jax.random.normal(ks[1], (L, BATCH, SEQ, PLE_DIM), jnp.float32),
        "ln1": gain(ks[2], (L, D)),
        "w_in": nrm(ks[3], (L, D, D_PROJ), D),
        "b_fg": jax.random.uniform(ks[4], (L, N_FOX_HEADS), jnp.float32, 1.0, 5.0),
        "w_cmp1_k": nrm(ks[5], (L, CMP_BLOCK * HEAD_DIM, CMP_HIDDEN), CMP_BLOCK * HEAD_DIM),
        "w_cmp2_k": nrm(ks[6], (L, CMP_HIDDEN, HEAD_DIM), CMP_HIDDEN),
        "pe_cmp_k": small(ks[7], (L, CMP_BLOCK, HEAD_DIM), 0.1),
        "w_cmp1_v": nrm(ks[8], (L, CMP_BLOCK * HEAD_DIM, CMP_HIDDEN), CMP_BLOCK * HEAD_DIM),
        "w_cmp2_v": nrm(ks[9], (L, CMP_HIDDEN, HEAD_DIM), CMP_HIDDEN),
        "pe_cmp_v": small(ks[10], (L, CMP_BLOCK, HEAD_DIM), 0.1),
        "gn_nsa": gain(ks[11], (L, D_NSA)),
        "gn_fox": gain(ks[12], (L, D_FOX)),
        "w_out": nrm(ks[13], (L, D_MIX, D), D_MIX),
        "ln2": gain(ks[14], (L, D)),
        "w_router": nrm(ks[15], (L, D, E), D),
        "b_router": small(ks[16], (L, E), 0.01),
        "w_up": nrm(ks[17], (L, E, D, 2 * F), D),
        "b_up": small(ks[18], (L, E, 2 * F), 0.01),
        "w_down": nrm(ks[19], (L, E, F, D), F),
        "b_down": small(ks[20], (L, E, D), 0.01),
        "ln_ple": gain(ks[21], (L, D)),
        "w_ple": nrm(ks[22], (L, PLE_DIM, D), PLE_DIM),
        "w_ple_gate": nrm(ks[23], (L, D, D), D),
        "ln_f": gain(ks[24], (D,)),
    }

def second_block(x, p, ln1, w_in, b_fg, w_cmp1_k, w_cmp2_k, pe_cmp_k, w_cmp1_v, w_cmp2_v,
              pe_cmp_v, gn_nsa, gn_fox, w_out, ln2, w_router, b_router, w_up, b_up,
              w_down, b_down, ln_ple, w_ple, w_ple_gate, ln_f):
    B, T, _ = x.shape
    G, Dh = N_NSA_KV, HEAD_DIM
    slopes = alibi_slopes(N_NSA_HEADS)
    pts = proj_split_points()
    h = x
    for i in range(DEPTH):
        u = rmsnorm_2(h, ln1[i])
        proj = u @ w_in[i]
        (q_n, k_c, v_c, k_s, v_s, k_w, v_w, g_n,
         q_f, k_f, v_f, f_f) = jnp.split(proj, pts, axis=-1)
        kc = compress(k_c.reshape(B, T, G, Dh), w_cmp1_k[i], w_cmp2_k[i], pe_cmp_k[i])
        vc = compress(v_c.reshape(B, T, G, Dh), w_cmp1_v[i], w_cmp2_v[i], pe_cmp_v[i])
        o_nsa = nsa_attention(q_n.reshape(B, T, N_NSA_HEADS, Dh), kc, vc,
                              k_s.reshape(B, T, G, Dh), v_s.reshape(B, T, G, Dh),
                              k_w.reshape(B, T, G, Dh), v_w.reshape(B, T, G, Dh),
                              g_n.reshape(B, T, N_NSA_HEADS, 3), slopes)
        o_fox = fox_attention(q_f.reshape(B, T, N_FOX_HEADS, Dh),
                              k_f.reshape(B, T, N_FOX_HEADS, Dh),
                              v_f.reshape(B, T, N_FOX_HEADS, Dh),
                              f_f + b_fg[i])
        mix = jnp.concatenate([rmsnorm_2(o_nsa, gn_nsa[i]), rmsnorm_2(o_fox, gn_fox[i])], axis=-1)
        h = h + mix @ w_out[i]
        h = h + moe(rmsnorm_2(h, ln2[i]), w_router[i], b_router[i], w_up[i], b_up[i],
                    w_down[i], b_down[i])
        h = h + (p[i] @ w_ple[i]) * jax.nn.sigmoid(rmsnorm_2(h, ln_ple[i]) @ w_ple_gate[i])
    return rmsnorm_2(h, ln_f)


def setup_inputs(seed=0):
    out = dict(first_inputs(seed))
    for name, value in second_inputs(seed + 1).items():
        if name != "x":
            out[name + "_2"] = value
    return out


def reference(
    x, norm_mix_g, w_in, q_norm_g, k_norm_g, lambda_q1, lambda_k1, lambda_q2, lambda_k2,
    subln_g, conv_w, conv_b, w_rg_a, b_rg_a, w_rg_x, b_rg_x, lru_lambda, w_proj_attn,
    w_proj_rnn, w_out, norm_mlp_g, w_up, w_down, rel_bias, p_2, ln1_2, w_in_2, b_fg_2,
    w_cmp1_k_2, w_cmp2_k_2, pe_cmp_k_2, w_cmp1_v_2, w_cmp2_v_2, pe_cmp_v_2, gn_nsa_2, gn_fox_2,
    w_out_2, ln2_2, w_router_2, b_router_2, w_up_2, b_up_2, w_down_2, b_down_2, ln_ple_2,
    w_ple_2, w_ple_gate_2, ln_f_2,
):
    x = first_block(
        x, norm_mix_g, w_in, q_norm_g, k_norm_g, lambda_q1, lambda_k1, lambda_q2, lambda_k2,
        subln_g, conv_w, conv_b, w_rg_a, b_rg_a, w_rg_x, b_rg_x, lru_lambda, w_proj_attn,
        w_proj_rnn, w_out, norm_mlp_g, w_up, w_down, rel_bias,
    )
    return second_block(
        x, p_2, ln1_2, w_in_2, b_fg_2, w_cmp1_k_2, w_cmp2_k_2, pe_cmp_k_2, w_cmp1_v_2,
        w_cmp2_v_2, pe_cmp_v_2, gn_nsa_2, gn_fox_2, w_out_2, ln2_2, w_router_2, b_router_2,
        w_up_2, b_up_2, w_down_2, b_down_2, ln_ple_2, w_ple_2, w_ple_gate_2, ln_f_2,
    )


_drawn_inputs = setup_inputs


def setup_inputs(seed=0):
    import zlib

    import numpy as np

    out = dict(_drawn_inputs(seed))
    spreads = {}
    factors = {'lambda_q1': 130.727,
     'b_rg_a': 8.0,
     'b_rg_x': 8.0,
     'ln1_2': 2.77,
     'pe_cmp_k_2': 5.148,
     'gn_nsa_2': 12.923,
     'gn_fox_2': 12.805,
     'b_router_2': 14.208,
     'b_up_2': 37.777,
     'b_down_2': 116.098,
     'ln_ple_2': 200.0,
     'ln_f_2': 22.443,
     'pe_cmp_v_2': 4.031,
     'ln2_2': 4.626}
    for name, (base, spread) in spreads.items():
        noise = np.random.default_rng([zlib.crc32(name.encode()), seed]).standard_normal(out[name].shape)
        drawn = base * np.exp(spread * noise) if base else spread * noise
        out[name] = __import__('jax').numpy.asarray(drawn.astype(out[name].dtype))
    for name, factor in factors.items():
        out[name] = (out[name] * factor).astype(out[name].dtype)
    return out
```

```python
import math
from contextlib import ExitStack

import concourse.bass as bass
from concourse import mybir

F32 = mybir.dt.float32
BF16 = mybir.dt.bfloat16
F32R = mybir.dt.float32r
I32 = mybir.dt.int32
U32 = mybir.dt.uint32
ALU = mybir.AluOpType
ACT = mybir.ActivationFunctionType
AX = mybir.AxisListType

P = 128
SEQ = 512
TT = SEQ // P
D = 1024
KT = D // P
HEADS = 8
BUCKETS = 32
FF = 4096
EXPERTS = 32
TOPK = 4
EPS = 1e-6
NEG = -1e30
CMP_STRIDE = 16
CMP_BLOCK = 32
NCMP = (SEQ - CMP_BLOCK) // CMP_STRIDE + 1
HD = 64
SHEAR = 384
ITEMS = SEQ * TOPK // P + EXPERTS - 1

VECS = [("norm_mix_g", 8), ("norm_mlp_g", 8), ("conv_w", 32), ("conv_b", 8), ("b_rg_a", 8), ("b_rg_x", 8),
        ("lru_lambda", 8), ("ln1_2", 8), ("ln2_2", 8), ("ln_ple_2", 8), ("gn_nsa_2", 4), ("gn_fox_2", 4),
        ("subln_g", 1)]
VAT = {}
_r = 0
for _n, _k in VECS:
    VAT[_n] = _r
    _r += _k
VAT["q_norm_g"], VAT["k_norm_g"] = _r, _r + 1
NVEC = _r + 2


class Link:

    def __init__(self, eng, sem, base=0):
        self.eng, self.sem, self.base, self.n = eng, sem, base, 0

    def __call__(self, ins):
        ins.then_inc(self.sem, 1)
        self.n += 1
        self.eng.wait_ge(self.sem, self.base + self.n)
        return self

    def turn(self, base, i, per):
        self.base, self.n = base + i * per, 0


def held(eng, carrier, sem, value):
    eng.wait_ge(sem, value)
    if carrier is not None and not isinstance(value, int):
        eng.sem_inc(carrier, 1)


class PhaseSems:

    def __init__(self, nc):
        self.nc, self.all = nc, []

    def __call__(self, name):
        self.all.append(self.nc.alloc_semaphore(name=name))
        return self.all[-1]

    def over(self):
        self.nc.clear_and_free_semaphores(self.all)
        self.nc.all_engine_barrier()


class Gemm:

    def __init__(self, nc, sem, sb, ps):
        self.nc = nc
        self.loaded = [sem("weights_loaded0"), sem("weights_loaded1")]
        self.product = sem("product_ready")
        self.drained = [sem(f"bank_drained{j}") for j in range(4)]
        self.carrier = {e: sem(f"carrier_{e}") for e in ("sp", "pe", "act", "dve", "pool")}
        self.ring = sb("weight_ring", [P, 2, 8, 512])
        self.bank = ps
        self.done = 0
        self.early = 0

    def loads(self, sp, p, pair, pieces):
        for b in range(2):
            if not isinstance(pair, int) or pair > 0:
                held(sp, None, self.product, 4 * (2 * pair + b - 1))
            for dst, src in pieces(p, b):
                sp.dma_start(dst, src).then_inc(self.loaded[b], 16)

    def sp(self, sp, pairs, pieces):
        start = 0
        if self.done == 0:
            self.loads(sp, 0, 0, pieces)
            start = 1
        if start < pairs:
            with sp.Fori(start, pairs) as p:
                self.loads(sp, p, p + self.done, pieces)

    def pe_pair(self, pe, pair, operands, start=True, stop=True, width=512):
        for b in range(2):
            held(pe, None, self.loaded[b], 32 * (pair + 1))
            for j in range(4):
                if start and (not isinstance(pair, int) or pair > 0):
                    held(pe, None, self.drained[j], 2 * (pair - 1) + b + 1)
                for k in range(8):
                    lhsT, rhs = operands(self.ring, b, j, k)
                    mm = pe.matmul(self.bank[4 * b + j][:, 0:width if not callable(width) else width(b)], lhsT, rhs,
                                   start=start and k == 0, stop=stop and k == 7)
                mm.then_inc(self.product, 1)

    def pe(self, pe, pairs, operands):
        start = 0
        if self.done == 0:
            self.pe_pair(pe, 0, operands)
            start = 1
        if start < pairs:
            with pe.Fori(start, pairs) as p:
                self.pe_pair(pe, p + self.done, operands)

    def drain(self, eng, who, pairs, js, evac):
        with eng.Fori(0, pairs) as p:
            for b in range(2):
                for j in js:
                    held(eng, self.carrier[who], self.product, 4 * (2 * (p + self.done) + b) + j + 1)
                    evac(eng, p, b, j, self.bank[4 * b + j]).then_inc(self.drained[j], 1)


def cols_of(ring, xT):
    return lambda r, b, j, k: (ring[:, b, k, j * P:(j + 1) * P], xT[:, k, :])


def rows_of(ring, xT, width=lambda b: 512):
    return lambda r, b, j, k: (xT[:, k, j * P:(j + 1) * P], ring[:, b, k, 0:width(b)])


def block_pieces(ring, w, col0=0, row0=0):
    def pieces(p, b):
        src = w[row0:row0 + D, bass.ds(p * 1024 + (col0 + b * 512), 512)].rearrange("(k q) n -> q k n", q=P)
        return [(ring[:, b, 0:4, :], src[:, 0:4, :]), (ring[:, b, 4:8, :], src[:, 4:8, :])]
    return pieces


def norm_to_cols(nc, name, sem, sb, bank, ident, x, g_at, vecT, hT, h=None, width=D, width_at=0, keep=None):
    kt = width // P
    with ExitStack() as st:
        sq = st.enter_context(nc.sbuf_tensor(name + "_sq", [P, width], F32))
        rows = keep if keep is not None else st.enter_context(nc.sbuf_tensor(name + "_rows", [P, TT, width], F32))
        stat = st.enter_context(nc.sbuf_tensor(name + "_stat", [P, 4, TT], F32))
        summed, act_link, rooted, scaled, turned, emptied = (
            sem(f"{name}_{s}") for s in ("squares_summed", "act_link", "rooted", "scaled", "turned", "emptied"))
        dve_link, dve_emptied = sem(name + "_dve_link"), sem(name + "_dve_emptied")
        with nc.Block() as block:
            @block.scalar
            def _(act):
                link = Link(act, act_link)
                for t in range(TT):
                    link(act.activation(sq[:, :], x[:, t, width_at:width_at + width], ACT.Square,
                                        accum_out=stat[:, 0, t:t + 1]))
                act.wait_ge(dve_link, 1)
                act.activation(stat[:, 2, :], stat[:, 1, :], ACT.Sqrt).then_inc(rooted, 1)
                for j in range(0, kt, 2):
                    act.wait_ge(turned, j + 1)
                    act.activation(hT[:, j, :], bank[j % 8][:, :], ACT.Copy,
                                   scale=vecT[:, g_at + j:g_at + j + 1]).then_inc(emptied, 1)

            @block.vector
            def _(dve):
                link = Link(dve, dve_link)
                dve.wait_ge(act_link, TT)
                link(dve.tensor_scalar(stat[:, 1, :], stat[:, 0, :], 1.0 / width, EPS, ALU.mult, ALU.add))
                dve.wait_ge(rooted, 1)
                link(dve.reciprocal(stat[:, 3, :], stat[:, 2, :]))
                for t in range(TT):
                    dve.tensor_scalar(rows[:, t, 0:width], x[:, t, width_at:width_at + width], stat[:, 3, t:t + 1],
                                      None, ALU.mult).then_inc(scaled, 1)
                for j in range(1, kt, 2):
                    dve.wait_ge(turned, j + 1)
                    dve.tensor_scalar(hT[:, j, :], bank[j % 8][:, :], vecT[:, g_at + j:g_at + j + 1], None,
                                      ALU.mult).then_inc(dve_emptied, 1)

            @block.tensor
            def _(pe):
                pe.wait_ge(scaled, TT)
                for j in range(kt):
                    for t in range(TT):
                        mm = pe.transpose(bank[j % 8][:, t * P:(t + 1) * P], rows[:, t, j * P:(j + 1) * P], ident[:, :])
                    mm.then_inc(turned, 1)


def log1p_steps(dve, link, out, e, s, s2):
    link(dve.tensor_scalar(s2, e, 2.0, None, ALU.add))
    link(dve.reciprocal(s, s2))
    link(dve.tensor_tensor(s, s, e, ALU.mult))
    link(dve.tensor_tensor(s2, s, s, ALU.mult))
    link(dve.tensor_scalar(out, s2, 1.0 / 17, None, ALU.mult))
    for k in range(7, 0, -1):
        link(dve.scalar_tensor_tensor(out, out, 1.0 / (2 * k + 1), s2, ALU.add, ALU.mult))
    link(dve.scalar_tensor_tensor(out, out, 1.0, s, ALU.add, ALU.mult))
    link(dve.tensor_scalar(out, out, 2.0, None, ALU.mult))


def transpose_rows(nc, name, sem, bank, ident, x, tiles, outT, scale_at=None):
    turned, act_emptied, dve_emptied = sem(name + "_turned"), sem(name + "_act_emptied"), sem(name + "_dve_emptied")
    with nc.Block() as block:
        @block.tensor
        def _(pe):
            for j in range(tiles):
                for t in range(TT):
                    mm = pe.transpose(bank[j][:, t * P:(t + 1) * P], x[:, t, j * P:(j + 1) * P], ident[:, :])
                mm.then_inc(turned, 1)

        @block.scalar
        def _(act):
            for j in range(0, tiles, 2):
                act.wait_ge(turned, j + 1)
                act.activation(outT[:, j, :], bank[j][:, :], ACT.Copy, scale=scale_at(j)).then_inc(act_emptied, 1)

        @block.vector
        def _(dve):
            for j in range(1, tiles, 2):
                dve.wait_ge(turned, j + 1)
                dve.tensor_scalar(outT[:, j, :], bank[j][:, :], scale_at(j), None, ALU.mult).then_inc(dve_emptied, 1)


def lru(nc, sem, bank, vecT, XG, w_a_dram, w_x_dram, rnnT):
    sem = PhaseSems(nc)
    with ExitStack() as st:
        def sb(name, shape):
            return st.enter_context(nc.sbuf_tensor(name, shape, F32))
        wa, wx = sb("lru_wa", [P, KT, P]), sb("lru_wx", [P, KT, P])
        xc, r, i = sb("lru_xc", [P, KT, SEQ]), sb("lru_r", [P, KT, SEQ]), sb("lru_i", [P, KT, SEQ])
        sp_t = sb("lru_softplus", [P, 5, KT])
        xr, gr, a = XG[:, 0], XG[:, 1], XG[:, 0]
        names = ("weights", "abs", "exp", "softplus", "convolved", "gate_product", "gate_ready", "input_gated",
                 "decay_ready", "tanh_ready", "one_minus", "rooted", "scaled", "scanned", "gelu", "out", "act_link", "dve_link")
        s = {n: sem("lru_" + n) for n in names}
        lam = vecT[:, VAT["lru_lambda"]:VAT["lru_lambda"] + KT]
        with nc.Block() as block:
            @block.sync
            def _(sp):
                sp.dma_start(wa[:, :, :], w_a_dram.rearrange("n e f -> e n f")).then_inc(s["weights"], 16)
                sp.dma_start(wx[:, :, :], w_x_dram.rearrange("n e f -> e n f")).then_inc(s["weights"], 16)

            @block.vector
            def _(dve):
                link = Link(dve, s["dve_link"])
                link(dve.tensor_scalar(sp_t[:, 0, :], lam, -1.0, None, ALU.mult))
                dve.tensor_tensor(sp_t[:, 0, :], sp_t[:, 0, :], lam, ALU.min).then_inc(s["abs"], 1)
                dve.wait_ge(s["exp"], 1)
                log1p_steps(dve, link, sp_t[:, 2, :], sp_t[:, 1, :], sp_t[:, 3, :], sp_t[:, 4, :])
                link(dve.tensor_scalar(sp_t[:, 3, :], lam, -1.0, 0.0, ALU.mult, ALU.max))
                link(dve.tensor_tensor(sp_t[:, 2, :], sp_t[:, 2, :], sp_t[:, 3, :], ALU.add))
                link(dve.tensor_scalar(sp_t[:, 2, :], sp_t[:, 2, :], 8.0, None, ALU.mult))
                dve.tensor_scalar(sp_t[:, 3, :], sp_t[:, 2, :], -1.0, None, ALU.mult).then_inc(s["softplus"], 1)
                for n in range(KT):
                    w = lambda tap: vecT[:, VAT["conv_w"] + tap * KT + n:VAT["conv_w"] + tap * KT + n + 1]
                    link(dve.tensor_scalar(xc[:, n, :], xr[:, n, :], w(3),
                                           vecT[:, VAT["conv_b"] + n:VAT["conv_b"] + n + 1], ALU.mult, ALU.add))
                    for tap in (2, 1, 0):
                        back = 3 - tap
                        last = dve.scalar_tensor_tensor(xc[:, n, back:], xr[:, n, 0:SEQ - back], w(tap),
                                                        xc[:, n, back:], ALU.mult, ALU.add)
                        if tap:
                            link(last)
                    last.then_inc(s["convolved"], 1)
                dve.wait_ge(s["convolved"], KT)
                dve.wait_ge(s["gate_ready"], 2 * KT)
                link(dve.tensor_tensor(i[:, :, :], i[:, :, :], xc[:, :, :], ALU.mult))
                dve.wait_ge(s["decay_ready"], KT)
                link(dve.tensor_tensor(xc[:, :, :], a, a, ALU.mult))
                dve.wait_ge(s["tanh_ready"], KT)
                dve.scalar_tensor_tensor(r[:, :, :].rearrange("p n t -> p (n t)"),
                                         xc[:, :, :].rearrange("p n t -> p (n t)"), 1.0,
                                         r[:, :, :].rearrange("p n t -> p (n t)"),
                                         ALU.add, ALU.mult).then_inc(s["one_minus"], 1)
                dve.wait_ge(s["rooted"], 1)
                link(dve.tensor_tensor(i[:, :, :], i[:, :, :], r[:, :, :], ALU.mult))
                for n in range(KT):
                    link(dve.tensor_tensor_scan(xc[:, n, :], a[:, n, :], i[:, n, :], 0.0, ALU.mult, ALU.add))
                dve.wait_ge(s["gelu"], 1)
                dve.tensor_tensor(rnnT[:, :, :], xc[:, :, :], gr, ALU.mult).then_inc(s["out"], 1)

            @block.tensor
            def _(pe):
                pe.wait_ge(s["weights"], 32)
                for n in range(KT):
                    pe.wait_ge(s["convolved"], n + 1)
                    if n >= 4:
                        pe.wait_ge(s["gate_ready"], 2 * (n - 3))
                    pe.matmul(bank[2 * (n % 4)][:, :], wa[:, n, :], xc[:, n, :], start=True, stop=True)\
                      .then_inc(s["gate_product"], 1)
                    pe.matmul(bank[2 * (n % 4) + 1][:, :], wx[:, n, :], xc[:, n, :], start=True, stop=True)\
                      .then_inc(s["gate_product"], 1)

            @block.scalar
            def _(act):
                act.wait_ge(s["abs"], 1)
                act.activation(sp_t[:, 1, :], sp_t[:, 0, :], ACT.Exp).then_inc(s["exp"], 1)
                for n in range(KT):
                    for m, (dst, b) in enumerate(((r, "b_rg_a"), (i, "b_rg_x"))):
                        act.wait_ge(s["gate_product"], 2 * n + m + 1)
                        act.activation(dst[:, n, :], bank[2 * (n % 4) + m][:, :], ACT.Sigmoid,
                                       bias=vecT[:, VAT[b] + n:VAT[b] + n + 1]).then_inc(s["gate_ready"], 1)
                act.wait_ge(s["convolved"], KT)
                act.wait_ge(s["softplus"], 1)
                act.wait_ge(s["gate_ready"], 2 * KT)
                for n in range(KT):
                    act.activation(a[:, n, :], r[:, n, :], ACT.Exp, scale=sp_t[:, 3, n:n + 1])\
                       .then_inc(s["decay_ready"], 1)
                act.wait_ge(s["decay_ready"], KT)
                for n in range(KT):
                    act.activation(r[:, n, :], r[:, n, :], ACT.Tanh, scale=sp_t[:, 2, n:n + 1])\
                       .then_inc(s["tanh_ready"], 1)
                act.wait_ge(s["one_minus"], 1)
                act.activation(r[:, :, :], r[:, :, :], ACT.Sqrt).then_inc(s["rooted"], 1)
                act.activation(gr, gr, ACT.Gelu_apprx_tanh).then_inc(s["gelu"], 1)
    sem.over()


def diff_attention(nc, sem, bank, ident, vecT, QKV, biasE, neg_lam, O):
    sem = PhaseSems(nc)
    with ExitStack() as st:
        def sb(name, shape):
            return st.enter_context(nc.sbuf_tensor(name, shape, F32))
        sq = O
        stat = sb("da_stat", [P, 2, TT, 2 * HEADS])
        rstd = sb("da_rstd", [P, 2, TT, 2 * HEADS])
        stage = sb("da_stage", [P, 2, TT, P])
        qkT = sb("da_qkT", [P, 2, SEQ])
        prob = sb("da_prob", [P, 4, SEQ])
        comb = sb("da_comb", [P, 2, SEQ])
        turned_sb = sb("da_turned", [P, 2, SEQ])
        nmax = sb("da_nmax", [P, 4])
        rsum = sb("da_rsum", [P, 4])
        rinv = sb("da_rinv", [P, 4])
        names = ("squared", "summed", "rooted", "staged", "qk_turned", "qk_ready", "scores_ready", "max_ready",
                 "probs_ready", "combined", "comb_turned", "combT_ready", "pv_ready", "out_stored", "dve_link", "act_link")
        s = {n: sem("da_" + n) for n in names}
        cr = {e: sem("da_carrier_" + e) for e in ("pe", "act", "dve")}
        S = [bank[0], bank[1], bank[2], bank[3]]
        T = [bank[4], bank[5]]
        OB = [bank[6], bank[7]]
        nk = [(q + 1) * P for q in range(TT)]
        with nc.Block() as block:
            @block.vector
            def _(dve):
                link = Link(dve, s["dve_link"])
                for m in range(2):
                    dve.wait_ge(s["squared"], m + 1)
                    dve.tensor_reduce(stat[:, m].rearrange("p t g -> p (t g)"),
                                      sq[:, :, :].rearrange("p t (g d) -> p (t g) d", d=HD), AX.X, ALU.add)\
                       .then_inc(s["summed"], 1)
                dve.wait_ge(s["summed"], 2)
                link(dve.tensor_scalar(stat[:, :, :, :], stat[:, :, :, :], 1.0 / HD, EPS, ALU.mult, ALU.add))
                dve.wait_ge(s["rooted"], 1)
                link(dve.reciprocal(rstd[:, :, :, :], rstd[:, :, :, :]))

                def unit_max(h, q):
                    for c in range(2):
                        u = 8 * h + 2 * q + c
                        dve.wait_ge(s["scores_ready"], u + 2)
                        dve.wait_ge(s["probs_ready"], u + 1)
                        dve.tensor_reduce(nmax[:, (2 * q + c) % 4:(2 * q + c) % 4 + 1], S[(2 * q + c) % 4][:, 0:nk[q]],
                                          AX.X, ALU.max, negate=True).then_inc(s["max_ready"], 1)

                def combine(h, q):
                    w = 4 * h + q
                    a, b = (2 * q) % 4, (2 * q + 1) % 4
                    dve.wait_ge(s["probs_ready"], 4 + 8 * h + 2 * q + 2)
                    link(dve.reciprocal(rinv[:, a:a + 2], rsum[:, a:a + 2]))
                    link(dve.tensor_tensor(rinv[:, b:b + 1], rinv[:, b:b + 1], neg_lam[:, 0:1], ALU.mult))
                    dve.wait_ge(s["comb_turned"], w + 1)
                    link(dve.tensor_scalar(comb[:, q % 2, 0:nk[q]], prob[:, a, 0:nk[q]], rinv[:, a:a + 1], None, ALU.mult))
                    dve.scalar_tensor_tensor(comb[:, q % 2, 0:nk[q]], prob[:, b, 0:nk[q]], rinv[:, b:b + 1],
                                             comb[:, q % 2, 0:nk[q]], ALU.mult, ALU.add).then_inc(s["combined"], 1)

                def store(h, q):
                    w = 4 * h + q
                    held(dve, cr["dve"], s["pv_ready"], 2 + w + 1)
                    dve.tensor_copy(O[:, q, bass.ds(h * P, P)], OB[q % 2][:, 0:P]).then_inc(s["out_stored"], 1)

                with dve.Fori(0, HEADS) as h:
                    link.turn(2, h, TT * 3)
                    for m in range(2):
                        held(dve, cr["dve"], s["qk_turned"], 2 * h + 1)
                        dve.tensor_tensor(stage[:, m].rearrange("p t (c d) -> p t c d", d=HD),
                                          QKV[:, m, :, bass.ds(h * P, P)].rearrange("p t (c d) -> p t c d", d=HD),
                                          rstd[:, m, :, bass.ds(h * 2, 2)].unsqueeze(3).broadcast_to([P, TT, 2, HD]),
                                          ALU.mult).then_inc(s["staged"], 1)
                    unit_max(h, 0)
                    unit_max(h, 1)
                    combine(h, 0)
                    unit_max(h, 2)
                    combine(h, 1)
                    store(h, 0)
                    unit_max(h, 3)
                    combine(h, 2)
                    store(h, 1)
                    combine(h, 3)
                    store(h, 2)
                    store(h, 3)

            @block.tensor
            def _(pe):
                def scores(h, q):
                    for c in range(2):
                        u = 8 * h + 2 * q + c
                        held(pe, None, s["probs_ready"], u + 1)
                        bk = S[(2 * q + c) % 4]
                        r0 = c * HD
                        pe.matmul(bk[:, 0:nk[q]], qkT[r0:r0 + HD, 0, q * P:(q + 1) * P], qkT[r0:r0 + HD, 1, 0:nk[q]],
                                  start=True, stop=False)
                        lo = max(q - 1, 0) * P
                        pe.matmul(bk[:, lo:nk[q]], ident[:, :],
                                  biasE[:, h, (2 * P - (nk[q] - lo)):2 * P],
                                  start=False, stop=True).then_inc(s["scores_ready"], 1)

                def turn(h, q):
                    w = 4 * h + q
                    held(pe, None, s["combined"], 2 + w + 1)
                    held(pe, None, s["combT_ready"], w + 1)
                    for k in range(q + 1):
                        mm = pe.transpose(T[q % 2][:, k * P:(k + 1) * P], comb[:, q % 2, k * P:(k + 1) * P], ident[:, :])
                    mm.then_inc(s["comb_turned"], 1)

                def values(h, q):
                    w = 4 * h + q
                    held(pe, cr["pe"], s["combT_ready"], 2 + w + 1)
                    held(pe, cr["pe"], s["out_stored"], w + 1)
                    for k in range(q + 1):
                        mm = pe.matmul(OB[q % 2][:, 0:P], turned_sb[:, q % 2, k * P:(k + 1) * P],
                                       QKV[:, 2, k, bass.ds(h * P, P)], start=k == 0, stop=k == q)
                    mm.then_inc(s["pv_ready"], 1)

                with pe.Fori(0, HEADS) as h:
                    for m in range(2):
                        held(pe, cr["pe"], s["staged"], 2 * h + m + 1)
                        held(pe, cr["pe"], s["combT_ready"], 4 * h + 2)
                        for t in range(TT):
                            mm = pe.transpose(T[m][:, t * P:(t + 1) * P], stage[:, m, t, :], ident[:, :])
                        mm.then_inc(s["qk_turned"], 1)
                    held(pe, cr["pe"], s["qk_ready"], 2 * h + 2)
                    scores(h, 0)
                    scores(h, 1)
                    turn(h, 0)
                    scores(h, 2)
                    values(h, 0)
                    turn(h, 1)
                    scores(h, 3)
                    values(h, 1)
                    turn(h, 2)
                    values(h, 2)
                    turn(h, 3)
                    values(h, 3)

            @block.scalar
            def _(act):
                act.sem_inc(s["probs_ready"], 4)
                act.sem_inc(s["qk_turned"], 1)
                act.sem_inc(s["scores_ready"], 1)
                act.sem_inc(s["combined"], 2)
                act.sem_inc(s["comb_turned"], 2)
                act.sem_inc(s["combT_ready"], 2)
                act.sem_inc(s["pv_ready"], 2)
                act.sem_inc(s["out_stored"], 2)
                for m in range(2):
                    if m:
                        act.wait_ge(s["summed"], 1)
                    act.activation(sq[:, :, :], QKV[:, m], ACT.Square).then_inc(s["squared"], 1)
                act.wait_ge(s["dve_link"], 1)
                act.activation(rstd[:, :, :, :], stat[:, :, :, :], ACT.Sqrt).then_inc(s["rooted"], 1)

                def exps(h, q):
                    for c in range(2):
                        u = 8 * h + 2 * q + c
                        held(act, None, s["max_ready"], u + 1)
                        held(act, None, s["combined"], 4 * h + q + 1)
                        sl = (2 * q + c) % 4
                        act.activation(prob[:, sl, 0:nk[q]], S[sl][:, 0:nk[q]], ACT.Exp, bias=nmax[:, sl:sl + 1],
                                       accum_out=rsum[:, sl:sl + 1]).then_inc(s["probs_ready"], 1)

                def keep(h, q):
                    w = 4 * h + q
                    held(act, None, s["comb_turned"], 2 + w + 1)
                    held(act, None, s["pv_ready"], w + 1)
                    act.activation(turned_sb[:, q % 2, 0:nk[q]], T[q % 2][:, 0:nk[q]], ACT.Copy)\
                       .then_inc(s["combT_ready"], 1)

                with act.Fori(0, HEADS) as h:
                    for m, g in enumerate(("q_norm_g", "k_norm_g")):
                        held(act, None, s["qk_turned"], 2 * h + m + 2)
                        held(act, None, s["scores_ready"], 8 * h + 1)
                        act.activation(qkT[:, m, :], T[m][:, :], ACT.Copy, scale=vecT[:, VAT[g]:VAT[g] + 1])\
                           .then_inc(s["qk_ready"], 1)
                    exps(h, 0)
                    exps(h, 1)
                    keep(h, 0)
                    exps(h, 2)
                    keep(h, 1)
                    exps(h, 3)
                    keep(h, 2)
                    keep(h, 3)
    sem.over()


def attention(nc, name, sem, bank, ident, q_of, k_of, nk, mask_of, v_of, O, out_at, gate_of, row_scale, add):
    sem = PhaseSems(nc)
    with ExitStack() as st:
        def sb(n, shape):
            return st.enter_context(nc.sbuf_tensor(f"{name}_{n}", shape, F32))
        q65 = sb("q", [HD + 1, 2, SEQ])
        ones = sb("ones", [HD + 1, SEQ])
        prob = sb("prob", [P, 4, SEQ])
        kept = sb("kept", [P, 2, SEQ])
        nmax, rsum, rinv = sb("nmax", [P, 4]), sb("rsum", [P, 4]), sb("rinv", [P, 4])
        S, T, OB = bank[0:4], bank[4:6], bank[6:8]
        s = {n: sem(f"{name}_{n}") for n in ("staged", "rowed", "scores", "maxed", "probs", "turned", "kept", "pv",
                                              "stored", "link", "ones")}
        cr = {e: sem(f"{name}_carrier_{e}") for e in ("pe", "act", "dve")}
        nkt = [-(-n // P) for n in nk]
        units = [(par, q) for par in range(2) for q in range(TT)]
        rows = min(P, nk[0])
        with nc.Block() as block:
            def turns(eng, body):
                with eng.Fori(0, 2) as g:
                    with eng.Fori(0, 2) as hh:
                        body(g, 2 * g + hh)

            @block.vector
            def _(dve):
                link = Link(dve, s["link"])
                dve.memset(q65[HD:HD + 1, :, :], 1.0).then_inc(s["ones"], 1)
                dve.memset(ones[:, :], 1.0).then_inc(s["ones"], 1)

                def body(g, hp):
                    link.turn(0, hp, 2 * len(units))

                    def top(m):
                        par, q = units[m]
                        held(dve, None, s["scores"], 5 + 8 * hp + m + 1)
                        dve.wait_ge(s["probs"], 8 * hp + m + 1)
                        dve.tensor_reduce(nmax[:, m % 4:m % 4 + 1], S[m % 4][:, 0:nk[q]], AX.X, ALU.max, negate=True)\
                           .then_inc(s["maxed"], 1)

                    def scale(m):
                        par, q = units[m]
                        held(dve, None, s["probs"], 4 + 8 * hp + m + 1)
                        link(dve.reciprocal(rinv[:, m % 4:m % 4 + 1], rsum[:, m % 4:m % 4 + 1]))
                        if gate_of:
                            link(dve.tensor_tensor(rinv[:, m % 4:m % 4 + 1], rinv[:, m % 4:m % 4 + 1],
                                                   gate_of(q, 2 * hp + par), ALU.mult))
                        else:
                            link(dve.tensor_copy(rinv[:, m % 4:m % 4 + 1], rinv[:, m % 4:m % 4 + 1]))

                    def store(m):
                        par, q = units[m]
                        dst = O[:, q, bass.ds(hp * P + (out_at + par * HD), HD)]
                        held(dve, cr["dve"], s["pv"], 2 + 8 * hp + m + 1)
                        r = rinv[:, m % 4:m % 4 + 1]
                        if add:
                            ins = dve.scalar_tensor_tensor(dst, OB[m % 2][:, 0:HD], r, dst, ALU.mult, ALU.add)
                        else:
                            ins = dve.tensor_scalar(dst, OB[m % 2][:, 0:HD], r, None, ALU.mult)
                        ins.then_inc(s["stored"], 1)

                    n = len(units)
                    for m in range(n + 3):
                        if m < n:
                            top(m)
                        if 0 <= m - 1 < n:
                            scale(m - 1)
                        if 0 <= m - 3 < n:
                            store(m - 3)
                turns(dve, body)

            @block.tensor
            def _(pe):
                def body(g, hp):
                    def scores(m):
                        par, q = units[m]
                        if q == 0:
                            held(pe, None, s["staged"], 2 * hp + par + 1)
                            if row_scale:
                                held(pe, None, s["rowed"], 2 * hp + par + 1)
                        held(pe, None, s["probs"], 8 * hp + m + 1)
                        pe.matmul(S[m % 4][:, 0:nk[q]], q65[:, par, q * P:(q + 1) * P], k_of(g, hp, par, nk[q]),
                                  start=True, stop=False)
                        (lo, hi), mask = mask_of(q)
                        pe.matmul(S[m % 4][:, lo:hi], ident[:, :], mask, start=False, stop=True).then_inc(s["scores"], 1)

                    def turn(m):
                        par, q = units[m]
                        held(pe, None, s["probs"], 4 + 8 * hp + m + 1)
                        held(pe, None, s["kept"], 8 * hp + m + 1)
                        for k in range(nkt[q]):
                            mm = pe.transpose(T[m % 2][0:rows, k * P:(k + 1) * P], prob[:, m % 4, k * P:k * P + rows],
                                              ident[:, :])
                        mm.then_inc(s["turned"], 1)

                    def values(m):
                        par, q = units[m]
                        held(pe, cr["pe"], s["kept"], 2 + 8 * hp + m + 1)
                        held(pe, cr["pe"], s["stored"], 8 * hp + m + 1)
                        for k in range(nkt[q]):
                            mm = pe.matmul(OB[m % 2][:, 0:HD], kept[0:rows, m % 2, k * P:(k + 1) * P],
                                           v_of(g, hp, par, k), start=k == 0, stop=k == nkt[q] - 1)
                        mm.then_inc(s["pv"], 1)

                    n = len(units)
                    for m in range(n + 3):
                        if m < n:
                            scores(m)
                        if 0 <= m - 2 < n:
                            turn(m - 2)
                        if 0 <= m - 3 < n:
                            values(m - 3)
                pe.wait_ge(s["ones"], 2)
                turns(pe, body)

            @block.scalar
            def _(act):
                act.sem_inc(s["scores"], 5)
                act.sem_inc(s["probs"], 4)
                act.sem_inc(s["turned"], 4)
                act.sem_inc(s["kept"], 2)
                act.sem_inc(s["pv"], 2)
                act.sem_inc(s["stored"], 2)
                act.wait_ge(s["ones"], 2)

                def body(g, hp):
                    for par in range(2):
                        held(act, cr["act"], s["scores"], 8 * hp + 4 * par + 1)
                        act.activation(q65[0:HD, par, :], q_of(hp, par), ACT.Copy, scale=HD ** -0.5)\
                           .then_inc(s["staged"], 1)
                        if row_scale:
                            act.activation(q65[HD:HD + 1, par, :], ones[HD:HD + 1, :], ACT.Copy,
                                           scale=row_scale(2 * hp + par)).then_inc(s["rowed"], 1)

                    def exp(m):
                        par, q = units[m]
                        held(act, None, s["maxed"], 8 * hp + m + 1)
                        held(act, None, s["turned"], 8 * hp + m + 1)
                        act.activation(prob[:, m % 4, 0:nk[q]], S[m % 4][:, 0:nk[q]], ACT.Exp, bias=nmax[:, m % 4:m % 4 + 1],
                                       accum_out=rsum[:, m % 4:m % 4 + 1]).then_inc(s["probs"], 1)

                    def keep(m):
                        par, q = units[m]
                        held(act, None, s["turned"], 4 + 8 * hp + m + 1)
                        held(act, None, s["pv"], 8 * hp + m + 1)
                        act.activation(kept[0:rows, m % 2, 0:nkt[q] * P], T[m % 2][0:rows, 0:nkt[q] * P], ACT.Copy)\
                           .then_inc(s["kept"], 1)

                    n = len(units)
                    for m in range(n + 2):
                        if m < n:
                            exp(m)
                        if 0 <= m - 2 < n:
                            keep(m - 2)
                turns(act, body)
    sem.over()


def second_layer(nc, A, outer, sem, sb, bank, ident, vecT, x, hT, gemm, out_rows, out_written, stop):
    ring = gemm.ring
    w_in = A["w_in_2"][0]

    def finish(rows):
        with nc.Block() as block:
            @block.sync
            def _(sp):
                sp.dma_start(out_rows, rows).then_inc(out_written, 16)
                sp.wait_ge(out_written, 16)

    norm_to_cols(nc, "ln1", sem, sb, bank, ident, x, VAT["ln1_2"], vecT, hT)

    mix = ExitStack()
    O = mix.enter_context(nc.sbuf_tensor("mix_out", [P, TT, D], F32))
    with ExitStack() as st:
        def tb(name, shape, dt=F32):
            return st.enter_context(nc.sbuf_tensor(name, shape, dt))
        T4 = tb("projT", [P, 4, 4, SEQ])
        R2 = tb("proj_rows", [P, 2, TT, 512])
        NG = 2 * P + 24
        wf = tb("w_forget", [P, KT, HEADS])
        bf = tb("b_forget", [HEADS, 1])
        fz = tb("forget", [HEADS, 6, SEQ])
        kN = tb("nsa_keys", [HD + 1, 4, SEQ])
        kF = tb("fox_keys", [HD + 1, HEADS, SEQ])
        kC = tb("cmp_keys", [HD + 1, 2, NCMP])
        vC = tb("cmp_values", [NCMP, 2, HD])
        pos_i = tb("positions_int", [1, SEQ], I32)
        pos_f = tb("positions", [1, SEQ])
        mask = tb("causal_mask", [P, P])
        cmask = tb("cmp_mask", [P, TT, NCMP])
        slopes = tb("slopes", [HD + 1, HEADS])
        valid = tb("first_rows_valid", [P, 1])

        cols_src = [[(0, 256), (256, 512)], [(512, 896), (1024, 1152)], [(1304, 1560), (1560, 1816)],
                    [(1816, 2072), (2072, 2328)]]
        rows_src = [[(2328, 2584), (2584, 2840)], [(896, 1024), (1152, 1304)]]

        def pieces_of(src):
            def pieces(p, b):
                got, at = [], 0
                for lo, hi in src[2 * p + b]:
                    got.append((ring[:, b, :, at:at + hi - lo], w_in[:, lo:hi].rearrange("(k q) n -> q k n", q=P)))
                    at += hi - lo
                return got
            return pieces

        f_loaded, f_product, f_biased, f_abs, f_exp, f_link, cum_ready, cum_moved = (
            sem("forget_" + n) for n in ("loaded", "product", "biased", "abs", "exp", "link", "cum_ready", "cum_moved"))
        with nc.Block() as block:
            @block.sync
            def _(sp):
                sp.dma_start(wf[:, :, :], w_in[:, 2840:2848].rearrange("(k q) n -> q k n", q=P)).then_inc(f_loaded, 16)
                sp.dma_start(bf[:, :], A["b_fg_2"].rearrange("l h -> h l")).then_inc(f_loaded, 16)
                for p in range(2):
                    gemm.loads(sp, p, gemm.done + p, pieces_of(cols_src))
                gemm.loads(sp, 0, gemm.done + 2, pieces_of(rows_src))

            @block.tensor
            def _(pe):
                gemm.pe(pe, 2, cols_of(ring, hT))
                gemm.pe_pair(pe, gemm.done + 2, rows_of(ring, hT, lambda b: (512, NG)[b]), width=lambda b: (512, NG)[b])

            def evac(copy):
                def one(eng, p, b, j, bk):
                    return copy(eng, T4[:, 2 * p + b, j, :], bk[:, :])
                return one

            def drain(eng, who, js, copy):
                gemm.drain(eng, who, 2, js, evac(copy))
                for b in range(2):
                    for j in js:
                        w = (512, NG)[b]
                        eng.wait_ge(gemm.product, 4 * (2 * (gemm.done + 2) + b) + j + 1)
                        copy(eng, R2[:, b, j, 0:w], gemm.bank[4 * b + j][:, 0:w]).then_inc(gemm.drained[j], 1)

            @block.scalar
            def _(act):
                drain(act, "act", (0, 2), lambda e, d, s_: e.activation(d, s_, ACT.Copy))

            @block.vector
            def _(dve):
                drain(dve, "dve", (1, 3), lambda e, d, s_: e.tensor_copy(d, s_))
        gemm.done += 3

        prep = ExitStack()
        pb = lambda name, shape: prep.enter_context(nc.sbuf_tensor(name, shape, F32))
        w1 = pb("cmp_w1", [P, 2, CMP_BLOCK, P])
        w2 = pb("cmp_w2", [P, 2, HD])
        pe_rows = pb("cmp_pe", [CMP_BLOCK, 2, HD])
        peT = pb("cmp_peT", [HD, 2, CMP_BLOCK])
        hconst = pb("cmp_const", [P, 2])
        hid = pb("cmp_hidden", [P, 4, NCMP])
        names = ("w_loaded", "pool_step", "iota_done", "pos_ready", "pos_moved", "keys_copied", "gates_ready", "dve_link",
                 "pe_turned", "peT_ready", "const_product", "const_ready", "hid_product", "hid_ready", "out_product", "out_ready")
        s = {n: sem("prep_" + n) for n in names}
        with nc.Block() as block:
            @block.sync
            def _(sp):
                for i, n in enumerate(("k", "v")):
                    src = A[f"w_cmp1_{n}_2"][0].rearrange("(l d) h -> d l h", d=HD)
                    for half in range(2):
                        sp.dma_start(w1[half * HD:(half + 1) * HD, i], src).then_inc(s["w_loaded"], 16)
                    sp.dma_start(w2[:, i, :], A[f"w_cmp2_{n}_2"][0]).then_inc(s["w_loaded"], 16)
                    sp.dma_start(pe_rows[:, i, :], A[f"pe_cmp_{n}_2"][0]).then_inc(s["w_loaded"], 16)
                sp.wait_ge(s["pos_ready"], 1)
                for i in range(4):
                    sp.dma_start(kN[HD:HD + 1, i, :], pos_f[0:1, :]).then_inc(s["pos_moved"], 16)
                ends = pos_f[0:1, CMP_BLOCK - 1:CMP_BLOCK + CMP_STRIDE * (NCMP - 1):CMP_STRIDE]
                with nc.allow_non_contiguous_dma(reason="31 positions"):
                    for g in range(2):
                        sp.dma_start(kC[HD:HD + 1, g, :], ends).then_inc(s["pos_moved"], 16)
                sp.wait_ge(cum_ready, 1)
                sp.dma_start(kF[HD:HD + 1, :, :], fz[:, 5, :]).then_inc(cum_moved, 16)
                sp.wait_ge(s["pos_moved"], 16 * 6)
                sp.wait_ge(cum_moved, 16)

            @block.gpsimd
            def _(pool):
                link = Link(pool, s["pool_step"])
                pool.iota(pos_i[:, :], pattern=[[1, SEQ]], base=0, channel_multiplier=0).then_inc(s["iota_done"], 1)
                link(pool.memset(mask[:, :], 0.0))
                link(pool.memset(cmask[:, :, :], 0.0))
                link(pool.memset(valid[:, :], 1.0))
                for h in range(HEADS):
                    link(pool.memset(slopes[:, h:h + 1], 2.0 ** (-8.0 * (h + 1) / HEADS)))
                link(pool.affine_select(out=mask[:, :], in_=mask[:, :], compare_op=ALU.is_ge, fill=NEG, base=0,
                                        pattern=[[-1, P]], channel_multiplier=1))
                for t in range(TT):
                    link(pool.affine_select(out=cmask[:, t, :], in_=cmask[:, t, :], compare_op=ALU.is_ge, fill=NEG,
                                            base=t * P - (CMP_BLOCK - 1), pattern=[[-CMP_STRIDE, NCMP]],
                                            channel_multiplier=1))
                link(pool.affine_select(out=valid[:, :], in_=valid[:, :], compare_op=ALU.is_ge, fill=0.0,
                                        base=-(CMP_BLOCK - 1), pattern=[[0, 1]], channel_multiplier=1))

            @block.tensor
            def _(pe):
                pe.wait_ge(f_loaded, 32)
                for k in range(KT):
                    mm = pe.matmul(bank[0][0:HEADS, :], wf[:, k, :], hT[:, k, :], start=k == 0, stop=k == KT - 1)
                mm.then_inc(f_product, 1)
                pe.wait_ge(s["w_loaded"], 16 * 8)
                for i in range(2):
                    pe.transpose(bank[1][0:HD, i * CMP_BLOCK:(i + 1) * CMP_BLOCK], pe_rows[:, i, :],
                                 ident[0:CMP_BLOCK, 0:CMP_BLOCK]).then_inc(s["pe_turned"], 1)
                pe.wait_ge(s["peT_ready"], 1)
                for i in range(2):
                    for l in range(CMP_BLOCK):
                        mm = pe.matmul(bank[2][:, i:i + 1], w1[0:HD, i, l, :], peT[:, i, l:l + 1],
                                       start=l == 0, stop=l == CMP_BLOCK - 1)
                    mm.then_inc(s["const_product"], 1)
                for i in range(2):
                    for g in range(2):
                        lo = g * HD
                        for l in range(CMP_BLOCK):
                            mm = pe.matmul(bank[3 + 2 * i + g][:, 0:NCMP], w1[lo:lo + HD, i, l, :],
                                           T4[lo:lo + HD, 1, i, l:l + CMP_STRIDE * (NCMP - 1) + 1:CMP_STRIDE],
                                           start=l == 0, stop=l == CMP_BLOCK - 1)
                        mm.then_inc(s["hid_product"], 1)
                pe.wait_ge(s["hid_ready"], 4)
                for g in range(2):
                    pe.matmul(bank[7][0:HD, g * 64:g * 64 + NCMP], w2[:, 0, :], hid[:, g, :], start=True, stop=True)\
                      .then_inc(s["out_product"], 1)
                for g in range(2):
                    pe.matmul(bank[1][0:NCMP, 256 + g * 64:256 + (g + 1) * 64], hid[:, 2 + g, :], w2[:, 1, :],
                              start=True, stop=True).then_inc(s["out_product"], 1)

            @block.scalar
            def _(act):
                act.wait_ge(f_abs, 1)
                act.activation(fz[:, 2, :], fz[:, 1, :], ACT.Exp).then_inc(f_exp, 1)
                for h in range(HEADS):
                    hp, par = h // 2, h % 2
                    act.activation(kF[0:HD, h, :], T4[par * HD:(par + 1) * HD, 3, hp, :], ACT.Copy)\
                       .then_inc(s["keys_copied"], 1)
                for i in range(2):
                    for g in range(2):
                        act.activation(kN[0:HD, 2 * i + g, :], T4[g * HD:(g + 1) * HD, 1, 2 + i, :], ACT.Copy)\
                           .then_inc(s["keys_copied"], 1)
                act.activation(R2[:, 1, :, 2 * P:NG], R2[:, 1, :, 2 * P:NG], ACT.Sigmoid).then_inc(s["gates_ready"], 1)
                act.wait_ge(s["const_ready"], 1)
                for i in range(4):
                    act.wait_ge(s["hid_product"], i + 1)
                    act.activation(hid[:, i, :], bank[3 + i][:, 0:NCMP], ACT.Gelu_apprx_tanh,
                                   bias=hconst[:, i // 2:i // 2 + 1]).then_inc(s["hid_ready"], 1)
                act.wait_ge(s["out_product"], 4)
                for g in range(2):
                    act.activation(kC[0:HD, g, :], bank[7][0:HD, g * 64:g * 64 + NCMP], ACT.Copy)\
                       .then_inc(s["out_ready"], 1)
                for g in range(2):
                    act.activation(vC[:, g, :], bank[1][0:NCMP, 256 + g * 64:256 + (g + 1) * 64], ACT.Copy)\
                       .then_inc(s["out_ready"], 1)

            @block.vector
            def _(dve):
                link = Link(dve, s["dve_link"])
                dve.wait_ge(s["iota_done"], 1)
                dve.tensor_copy(pos_f[:, :], pos_i[:, :]).then_inc(s["pos_ready"], 1)
                dve.wait_ge(f_product, 1)
                link(dve.tensor_scalar(fz[:, 0, :], bank[0][0:HEADS, :], bf[:, 0:1], None, ALU.add))
                link(dve.tensor_scalar(fz[:, 1, :], fz[:, 0, :], -1.0, None, ALU.mult))
                dve.tensor_tensor(fz[:, 1, :], fz[:, 1, :], fz[:, 0, :], ALU.min).then_inc(f_abs, 1)
                dve.wait_ge(f_exp, 1)
                log1p_steps(dve, link, fz[:, 5, :], fz[:, 2, :], fz[:, 3, :], fz[:, 4, :])
                link(dve.tensor_scalar(fz[:, 1, :], fz[:, 0, :], -1.0, 0.0, ALU.mult, ALU.max))
                link(dve.tensor_tensor(fz[:, 1, :], fz[:, 1, :], fz[:, 5, :], ALU.add))
                link(dve.memset(fz[:, 2, :], 1.0))
                dve.tensor_tensor_scan(fz[:, 5, :], fz[:, 2, :], fz[:, 1, :], 0.0, ALU.mult, ALU.add)\
                   .then_inc(cum_ready, 1)
                dve.wait_ge(s["pe_turned"], 2)
                dve.tensor_copy(peT[:, :, :], bank[1][0:HD, 0:2 * CMP_BLOCK].rearrange("d (i l) -> d i l", i=2))\
                   .then_inc(s["peT_ready"], 1)
                dve.wait_ge(s["const_product"], 2)
                dve.tensor_copy(hconst[:, :], bank[2][:, 0:2]).then_inc(s["const_ready"], 1)
                dve.wait_ge(s["gates_ready"], 1)
                dve.wait_ge(s["pool_step"], 3 + HEADS + 1 + TT + 1)
                dve.tensor_scalar(R2[:, 1, 0, 2 * P:NG:3], R2[:, 1, 0, 2 * P:NG:3], valid[:, 0:1], None, ALU.mult)\
                   .then_inc(s["gates_ready"], 1)

        prep.close()

        gate = lambda br: (lambda q, h: R2[:, 1, q, bass.ds(h * 3 + (2 * P + br), 1)])
        q_from = lambda i: (lambda hp, par: T4[par * HD:(par + 1) * HD, i, hp, :])
        slope = lambda h: slopes[HD:HD + 1, bass.ds(h, 1)]
        full = [(q + 1) * P for q in range(TT)]
        causal = lambda q: ((q * P, (q + 1) * P), mask[:, :])
        attention(nc, "cmp", sem, bank, ident, q_from(0), lambda g, hp, par, n: kC[:, g, 0:n], [NCMP] * TT,
                  lambda q: ((0, NCMP), cmask[:, q, :]), lambda g, hp, par, k: vC[:, g, :], O, 0, gate(0), slope, False)
        attention(nc, "sel", sem, bank, ident, q_from(0), lambda g, hp, par, n: kN[:, g, 0:n], full, causal,
                  lambda g, hp, par, k: R2[:, 1, k, bass.ds(g * HD, HD)], O, 0, gate(1), slope, True)
        attention(nc, "win", sem, bank, ident, q_from(0), lambda g, hp, par, n: kN[:, 2 + g, 0:n], full, causal,
                  lambda g, hp, par, k: R2[:, 1, k, bass.ds(g * HD + P, HD)], O, 0, gate(2), slope, True)
        attention(nc, "fox", sem, bank, ident, q_from(2), lambda g, hp, par, n: kF[:, hp * 2 + par, 0:n], full, causal,
                  lambda g, hp, par, k: R2[:, 0, k, bass.ds(hp * P + par * HD, HD)], O, 4 * P, None, None, False)

    for name, at in (("gn_nsa", 0), ("gn_fox", 4)):
        norm_to_cols(nc, name, sem, sb, bank, ident, O, VAT[name + "_2"], vecT, hT[:, at:at + 4, :], width=4 * P,
                     width_at=at * P)
    mix.close()

    def gemm_phase(pieces, operands, evac, who, engine):
        with nc.Block() as block:
            @block.sync
            def _(sp):
                gemm.sp(sp, 1, pieces)

            @block.tensor
            def _(pe):
                gemm.pe(pe, 1, operands)

            @engine(block)
            def _(eng):
                gemm.drain(eng, who, 1, (0, 1, 2, 3), evac)
        gemm.done += 1
    residual = lambda eng, p, b, j, bk: eng.tensor_tensor(x[:, j, b * 512:(b + 1) * 512], bk[:, :],
                                                         x[:, j, b * 512:(b + 1) * 512], ALU.add)
    gemm_phase(block_pieces(ring, A["w_out_2"][0]), rows_of(ring, hT), residual, "dve", lambda blk: blk.vector)
    if stop == "mix":
        finish(x[:, :, :])
        return
    moe(nc, A, sem, bank, ident, vecT, x, hT, ring, gemm)
    if stop == "moe":
        finish(x[:, :, :])
        return
    last_stage(nc, A, sem, sb, bank, ident, vecT, x, hT, ring, gemm, gemm_phase, out_rows, out_written)


def moe(nc, A, sem_, bank, ident, vecT, x, hT, ring, gemm):
    outer = ExitStack()

    def ob(name, shape, dt=F32):
        return outer.enter_context(nc.sbuf_tensor(name, shape, dt))
    wt = ob("route_weights", [P, TT, TOPK])
    wtT = ob("route_weightsT", [EXPERTS, SEQ])
    slot = ob("route_slots", [P, TT * TOPK], U32)
    out_row = ob("route_out_rows", [P, TT * TOPK], U32)
    work = ob("work_experts", [1, ITEMS], I32)
    total = ob("work_total", [1, 1], I32)

    with ExitStack() as st:
        def tb(name, shape, dt=F32):
            return st.enter_context(nc.sbuf_tensor(name, shape, dt))
        rows = tb("moe_rows", [P, TT, D])
        norm_to_cols(nc, "ln2", sem_, None, bank, ident, x, VAT["ln2_2"], vecT, hT, keep=rows)
        gain = tb("ln2_wide", [P, D])
        sem = PhaseSems(nc)
        wr, br = tb("w_router", [P, KT, EXPERTS]), tb("b_router", [1, EXPERTS])
        ones, tri = tb("ones_square", [P, P]), tb("before", [P, P])
        iota_i, iota = tb("iota_int", [P, EXPERTS], I32), tb("iota", [P, EXPERTS])
        item_i, item = tb("item_int", [1, ITEMS], I32), tb("item", [1, ITEMS])
        tok, zero = tb("token_ids", [P, TT], I32), tb("zero_slots", [P, ITEMS + 1], I32)
        lg, top = tb("logits", [P, TT, EXPERTS]), tb("top_values", [P, TT, 8])
        top_i, top_f = tb("top_index", [P, TT, 8], U32), tb("top_index_float", [P, TT, 8])
        stat = tb("route_stat", [P, 3, TT])
        eq = tb("pick_onehot", [P, TT, TOPK, EXPERTS])
        tmp = tb("pick_tmp", [P, TT, TOPK, EXPERTS])
        chosen, dense = tb("chosen", [P, TT, EXPERTS]), tb("dense_weights", [P, TT, EXPERTS])
        place = tb("places", [P, TT, EXPERTS])
        picks = tb("pick_rows", [P, TT, TOPK])
        line = tb("expert_line", [P, 4, EXPERTS])
        grid = tb("work_grid", [1, ITEMS, EXPERTS])
        found = tb("work_found", [1, ITEMS])
        bu = tb("b_up_rows", [EXPERTS, 2 * D])
        br1, br2 = tb("b_up_rest", [EXPERTS, 2 * D]), tb("b_up_rest2", [EXPERTS, 2 * D])
        parts = tb("b_up_parts", [EXPERTS, 3, 2 * D], BF16)
        names = ("loaded", "bias_loaded", "gain_loaded", "gained", "h2_written", "zero_ready", "zeroed", "pool_link", "iotas", "logits_ready", "dve_link",
                 "tops_negated", "exps_ready", "chosen_ready", "places_ready", "slots_ready", "scattered", "parts_ready",
                 "parts_written", "weights_turned")
        s = {n: sem("route_" + n) for n in names}
        with nc.Block() as block:
            @block.sync
            def _(sp):
                sp.dma_start(wr[:, :, :], A["w_router_2"][0].rearrange("(k q) e -> q k e", q=P)).then_inc(s["loaded"], 16)
                sp.dma_start(br[:, :], A["b_router_2"]).then_inc(s["loaded"], 16)
                sp.dma_start(bu[:, :], A["b_up_2"][0]).then_inc(s["bias_loaded"], 16)
                sp.dma_start(gain[:, :], A["ln2_row"].broadcast_to([P, D])).then_inc(s["gain_loaded"], 16)
                sp.wait_ge(s["gained"], TT)
                sp.dma_start(A["h2_scratch"].rearrange("(t p) d -> p t d", p=P), rows[:, :, :]).then_inc(s["h2_written"], 16)
                sp.wait_ge(s["zero_ready"], 1)
                sp.dma_start(A["slot_tokens"].rearrange("(p c) o -> p (c o)", p=P), zero[:, :]).then_inc(s["zeroed"], 16)
                sp.wait_ge(s["parts_ready"], 1)
                sp.dma_start(A["bias_parts"], parts[:, :, :]).then_inc(s["parts_written"], 16)
                sp.wait_ge(s["parts_written"], 16)
                sp.wait_ge(s["h2_written"], 16)

            @block.gpsimd
            def _(pool):
                pool.memset(zero[:, :], 0).then_inc(s["zero_ready"], 1)
                link = Link(pool, s["pool_link"])
                link(pool.memset(ones[:, :], 1.0))
                link(pool.memset(tri[:, :], 1.0))
                link(pool.affine_select(out=tri[:, :], in_=tri[:, :], compare_op=ALU.is_gt, fill=0.0, base=0,
                                        pattern=[[1, P]], channel_multiplier=-1))
                link(pool.iota(iota_i[:, :], pattern=[[1, EXPERTS]], base=0, channel_multiplier=0))
                link(pool.iota(item_i[:, :], pattern=[[1, ITEMS]], base=0, channel_multiplier=0))
                link(pool.iota(tok[:, :], pattern=[[P, TT]], base=0, channel_multiplier=1))
                pool.wait_ge(s["slots_ready"], 1)
                pool.wait_ge(s["zeroed"], 16)
                for t in range(TT):
                    for k in range(TOPK):
                        j = t * TOPK + k
                        pool.indirect_dma_start(A["slot_tokens"], bass.IndirectOffsetOnAxis(ap=slot[:, j:j + 1], axis=0),
                                                tok[:, t:t + 1], None).then_inc(s["scattered"], 16)
                pool.wait_ge(s["scattered"], 16 * TT * TOPK)

            @block.tensor
            def _(pe):
                pe.wait_ge(s["loaded"], 32)
                pe.wait_ge(s["pool_link"], 3)
                for t in range(TT):
                    for k in range(KT):
                        pe.matmul(bank[t][:, 0:EXPERTS], hT[:, k, t * P:(t + 1) * P], wr[:, k, :], start=k == 0, stop=False)
                    pe.matmul(bank[t][:, 0:EXPERTS], ones[0:1, :], br[:, :], start=False, stop=True)\
                      .then_inc(s["logits_ready"], 1)
                pe.wait_ge(s["chosen_ready"], 1)
                for t in range(TT):
                    for u in range(t):
                        pe.matmul(bank[4][:, t * EXPERTS:(t + 1) * EXPERTS], ones[:, :], chosen[:, u, :], start=u == 0, stop=False)
                    pe.matmul(bank[4][:, t * EXPERTS:(t + 1) * EXPERTS], tri[:, :], chosen[:, t, :], start=t == 0, stop=True)
                for u in range(TT):
                    mm = pe.matmul(bank[5][:, 0:EXPERTS], ones[:, :], chosen[:, u, :], start=u == 0, stop=u == TT - 1)
                mm.then_inc(s["places_ready"], 1)
                for t in range(TT):
                    mm = pe.transpose(bank[6][0:EXPERTS, t * P:(t + 1) * P], dense[:, t, :], ident[:, :])
                mm.then_inc(s["weights_turned"], 1)

            @block.scalar
            def _(act):
                act.wait_ge(s["tops_negated"], 1)
                for t in range(TT):
                    act.activation(wt[:, t, :], top[:, t, 0:TOPK], ACT.Exp, bias=stat[:, 0, t:t + 1],
                                   accum_out=stat[:, 1, t:t + 1]).then_inc(s["exps_ready"], 1)

            @block.vector
            def _(dve):
                link = Link(dve, s["dve_link"])
                dve.wait_ge(s["bias_loaded"], 16)
                dve.wait_ge(s["gain_loaded"], 16)
                for t in range(TT):
                    dve.tensor_tensor(rows[:, t, :], rows[:, t, :], gain[:, :], ALU.mult).then_inc(s["gained"], 1)
                link(dve.tensor_copy(parts[:, 0, :], bu[:, :]))
                link(dve.tensor_tensor(br1[:, :], bu[:, :], parts[:, 0, :], ALU.subtract))
                link(dve.tensor_copy(parts[:, 1, :], br1[:, :]))
                link(dve.tensor_tensor(br2[:, :], br1[:, :], parts[:, 1, :], ALU.subtract))
                dve.tensor_copy(parts[:, 2, :], br2[:, :]).then_inc(s["parts_ready"], 1)
                dve.wait_ge(s["pool_link"], 6)
                link(dve.tensor_copy(iota[:, :], iota_i[:, :]))
                link(dve.tensor_copy(item[:, :], item_i[:, :]))
                for t in range(TT):
                    dve.wait_ge(s["logits_ready"], t + 1)
                    link(dve.tensor_copy(lg[:, t, :], bank[t][:, 0:EXPERTS]))
                    link(dve.max(top[:, t, :], lg[:, t, :]))
                    link(dve.max_index(top_i[:, t, :], top[:, t, :], lg[:, t, :]))
                dve.tensor_scalar(stat[:, 0, :], top[:, :, 0], -1.0, None, ALU.mult).then_inc(s["tops_negated"], 1)
                link(dve.tensor_copy(top_f[:, :, :], top_i[:, :, :]))
                for t in range(TT):
                    link(dve.tensor_tensor(eq[:, t], iota[:, :].unsqueeze(1).broadcast_to([P, TOPK, EXPERTS]),
                                           top_f[:, t, 0:TOPK].unsqueeze(2).broadcast_to([P, TOPK, EXPERTS]), ALU.is_equal))
                link(dve.tensor_reduce(chosen[:, :, :], eq[:, :, :, :].rearrange("p t k e -> p t e k"), AX.X, ALU.add))
                dve.wait_ge(s["exps_ready"], TT)
                link(dve.reciprocal(stat[:, 2, :], stat[:, 1, :]))
                link(dve.tensor_tensor(wt[:, :, :], wt[:, :, :], stat[:, 2, :].unsqueeze(2).broadcast_to([P, TT, TOPK]), ALU.mult))
                for t in range(TT):
                    link(dve.tensor_tensor(tmp[:, t], eq[:, t], wt[:, t, :].unsqueeze(2).broadcast_to([P, TOPK, EXPERTS]), ALU.mult))
                dve.tensor_reduce(dense[:, :, :], tmp[:, :, :, :].rearrange("p t k e -> p t e k"), AX.X, ALU.add)\
                   .then_inc(s["chosen_ready"], 1)
                dve.wait_ge(s["chosen_ready"], 1)
                dve.wait_ge(s["places_ready"], 1)
                link(dve.tensor_copy(line[:, 0, :], bank[5][:, 0:EXPERTS]))
                link(dve.tensor_scalar(line[:, 1, :], line[:, 0, :], 0.0, None, ALU.is_gt))
                for j in range(1, SEQ // P):
                    link(dve.scalar_tensor_tensor(line[:, 1, :], line[:, 0, :], float(j * P), line[:, 1, :], ALU.is_gt, ALU.add))
                link(dve.memset(line[:, 3, :], 1.0))
                link(dve.tensor_tensor_scan(line[:, 2, :], line[:, 3, :], line[:, 1, :], 0.0, ALU.mult, ALU.add))
                link(dve.tensor_tensor(line[:, 3, :], line[:, 2, :], line[:, 1, :], ALU.subtract))
                link(dve.tensor_copy(place[:, :, :], bank[4][:, 0:TT * EXPERTS].rearrange("p (t e) -> p t e", t=TT)))
                link(dve.scalar_tensor_tensor(place[:, :, :], line[:, 3, :].unsqueeze(1).broadcast_to([P, TT, EXPERTS]), float(P),
                                              place[:, :, :], ALU.mult, ALU.add))
                for t in range(TT):
                    link(dve.tensor_tensor(tmp[:, t], eq[:, t], place[:, t, :].unsqueeze(1).broadcast_to([P, TOPK, EXPERTS]), ALU.mult))
                link(dve.tensor_reduce(picks[:, :, :], tmp[:, :, :, :], AX.X, ALU.add))
                dve.tensor_copy(slot[:, :], picks[:, :, :].rearrange("p t k -> p (t k)")).then_inc(s["slots_ready"], 1)
                link(dve.tensor_scalar(out_row[:, :], picks[:, :, :].rearrange("p t k -> p (t k)"), float(P), None, ALU.add))
                link(dve.tensor_tensor(grid[:, :, :], line[0:1, 2, :].unsqueeze(1).broadcast_to([1, ITEMS, EXPERTS]),
                                       item[:, :].unsqueeze(2).broadcast_to([1, ITEMS, EXPERTS]), ALU.is_le))
                link(dve.tensor_reduce(found[:, :], grid[:, :, :], AX.X, ALU.add))
                link(dve.tensor_scalar(work[:, :], found[:, :], float(EXPERTS - 1), None, ALU.min))
                link(dve.tensor_copy(total[:, :], line[0:1, 2, EXPERTS - 1:EXPERTS]))
                dve.wait_ge(s["weights_turned"], 1)
                link(dve.tensor_copy(wtT[:, :], bank[6][0:EXPERTS, :]))
        sem.over()

    with ExitStack() as st:
        def tb(name, shape, dt=F32):
            return st.enter_context(nc.sbuf_tensor(name, shape, dt))
        UNITS, RAW, SPLIT = 12, 6, 4
        ring4 = ring[:, :, :, :].rearrange("p a k n -> p (a k n)").rearrange("p (r n) -> p r n", r=4)
        raw2 = tb("raw_units", [P, 2, 2048])
        raw = [ring4[:, r, :] for r in range(4)] + [raw2[:, r, :] for r in range(2)]
        uh, ul = tb("unit_high", [P, SPLIT, 2048], F32R), tb("unit_low", [P, SPLIT, 2048], F32R)
        index = tb("item_tokens", [P, 1], I32)
        xg = tb("gathered", [P, D])
        xh, xl = tb("gatheredT_high", [P, KT, P], F32R), tb("gatheredT_low", [P, KT, P], F32R)
        biasb, ones3 = tb("bias_row_parts", [3, 2 * D], BF16), tb("ones_three", [3, P], BF16)
        gs, sg, ls = tb("gate_part", [P, D]), tb("gate_sigmoid", [P, D]), tb("linear_part", [P, D])
        at, y = tb("activated", [P, D]), tb("expert_rows", [P, D])
        ah, al = tb("activatedT_high", [P, KT, P], F32R), tb("activatedT_low", [P, KT, P], F32R)
        zero_rows = tb("zero_rows", [P, D])
        sem = PhaseSems(nc)
        raw_loaded = [sem(f"raw_loaded{r}") for r in range(RAW)]
        names = ("ones", "index_loaded", "gathered", "xg_turned", "xg_high", "xg_ready", "bias_loaded", "up_ready",
                 "high_ready", "split_ready", "unit_used", "gate_ready", "sigmoid_ready", "act_ready", "act_turned",
                 "act_high", "actT_ready", "y_kept", "y_written", "dve_link", "counted")
        s = {n: sem("moe_" + n) for n in names}
        carrier = sem("moe_carrier_pool")
        w_up = A["w_up_2"][0].rearrange("e k n -> (e k) n")
        w_down = A["w_down_2"][0].rearrange("e k n -> (e k) n")
        bias_rows = A["bias_parts"].rearrange("e a n -> (e a) n")
        four = lambda bk: bk[:, :].rearrange("p (k t) -> p k t", k=4)
        with nc.Block() as block:
            def items(eng, body, skipped=None):
                n = eng.value_load(total[0:1, 0:1], min_val=1, max_val=ITEMS)
                with eng.Fori(0, ITEMS) as i:
                    with eng.If(i < n):
                        body(i)
                    if skipped:
                        with eng.Else():
                            skipped(i)
                    eng.nop()
                return n

            @block.sync
            def _(sp):
                def body(i):
                    e = sp.value_load(work[0:1, bass.ds(i, 1)], min_val=0, max_val=EXPERTS - 1)
                    for u in range(UNITS):
                        held(sp, None, s["split_ready"], UNITS * i + u + 1)
                        dst = raw[u % RAW].rearrange("p (k n) -> p k n", k=2)
                        if u < 8:
                            c, j = u // 4, u % 4
                            src = w_up[bass.ds(e * D + j * 2 * P, 2 * P), :].rearrange("(k q) (s n) -> q k s n", q=P, s=2)
                            for k in range(2):
                                sp.dma_start(dst[:, k, :].rearrange("p (s n) -> p s n", s=2),
                                             src[:, k, :, c * 512:(c + 1) * 512]).then_inc(raw_loaded[u % RAW], 16)
                        else:
                            src = w_down[bass.ds(e * D + (u - 8) * 2 * P, 2 * P), :].rearrange("(k q) n -> q k n", q=P)
                            for k in range(2):
                                sp.dma_start(dst[:, k, :], src[:, k, :]).then_inc(raw_loaded[u % RAW], 16)
                        if u == 0:
                            held(sp, None, s["up_ready"], 2 * i + 1)
                            sp.dma_start(biasb[:, :], bias_rows[bass.ds(e * 3, 3), :]).then_inc(s["bias_loaded"], 16)
                sp.wait_ge(s["counted"], 2)
                items(sp, body)

            @block.gpsimd
            def _(pool):
                for name, n in (("split_ready", RAW), ("unit_used", SPLIT), ("up_ready", 1), ("act_ready", 2),
                                ("y_kept", 1), ("y_written", 16)):
                    pool.sem_inc(s[name], n)
                pool.sem_inc(s["counted"], 1)

                def gather(i):
                    pool.dma_start(index[:, :], A["slot_tokens"][bass.ds(i * P, P), :]).then_inc(s["index_loaded"], 16)
                    held(pool, carrier, s["index_loaded"], 16 * i + 16)
                    pool.indirect_dma_start(xg[:, :], None, A["h2_scratch"],
                                            bass.IndirectOffsetOnAxis(ap=index[:, 0:1], axis=0)).then_inc(s["gathered"], 16)

                def body(i):
                    held(pool, carrier, s["xg_turned"], i + 1)
                    gather(i + 1)
                gather(0)
                items(pool, body)

            @block.tensor
            def _(pe):
                def three(bk, xs, k, ws, first, last):
                    (h, l), (wh, wl) = xs, ws
                    pe.matmul(bk, h[:, k, :], wh, start=first, stop=False)
                    pe.matmul(bk, h[:, k, :], wl, start=False, stop=False)
                    return pe.matmul(bk, l[:, k, :], wh, start=False, stop=last)

                def turn_rows(i):
                    held(pe, None, s["gathered"], 16 * i + 16)
                    for k in range(KT):
                        mm = pe.transpose(bank[k // 4][:, (k % 4) * P:(k % 4 + 1) * P], xg[:, k * P:(k + 1) * P], ident[:, :])
                    mm.then_inc(s["xg_turned"], 1)

                def turn_act(i, c):
                    held(pe, None, s["act_ready"], 2 + 2 * i + c + 1)
                    for k in range(4):
                        mm = pe.transpose(bank[4 + c][:, k * P:(k + 1) * P], at[:, (4 * c + k) * P:(4 * c + k + 1) * P], ident[:, :])
                    mm.then_inc(s["act_turned"], 1)

                def unit(i, u):
                    held(pe, None, s["split_ready"], RAW + UNITS * i + u + 1)
                    for k in range(2):
                        for h in range(2):
                            at_ = slice(k * 1024 + h * 512, k * 1024 + (h + 1) * 512)
                            ws = (uh[:, u % SPLIT, at_], ul[:, u % SPLIT, at_])
                            if u < 8:
                                c, kk = u // 4, 2 * (u % 4) + k
                                mm = three(bank[2 * c + h][:, :], (xh, xl), kk, ws, kk == 0, False)
                            else:
                                kk = 2 * (u - 8) + k
                                mm = three(bank[6 + h][:, :], (ah, al), kk, ws, kk == 0, kk == KT - 1)
                    mm.then_inc(s["unit_used"], 1)

                def bias(c):
                    for h in range(2):
                        mm = pe.matmul(bank[2 * c + h][:, :], ones3[:, :], biasb[:, h * D + c * 512:h * D + (c + 1) * 512],
                                       start=False, stop=True)
                    mm.then_inc(s["up_ready"], 1)

                def body(i):
                    held(pe, None, s["xg_ready"], 2 * i + 2)
                    for u in range(4):
                        unit(i, u)
                    held(pe, None, s["bias_loaded"], 16 * i + 16)
                    bias(0)
                    held(pe, None, s["act_ready"], 2 * i + 2)
                    for u in range(4, 7):
                        unit(i, u)
                    turn_act(i, 0)
                    unit(i, 7)
                    bias(1)
                    held(pe, None, s["actT_ready"], 2 * i + 1)
                    held(pe, None, s["y_kept"], 2 * i + 1)
                    unit(i, 8)
                    unit(i, 9)
                    turn_act(i, 1)
                    turn_rows(i + 1)
                    held(pe, None, s["actT_ready"], 2 * i + 2)
                    unit(i, 10)
                    unit(i, 11)
                pe.wait_ge(s["ones"], 1)
                pe.wait_ge(s["counted"], 2)
                turn_rows(0)
                items(pe, body)

            @block.vector
            def _(dve):
                dve.memset(ones3[:, :], 1.0).then_inc(s["ones"], 1)
                dve.memset(zero_rows[:, :], 0.0).then_inc(s["counted"], 1)
                link = Link(dve, s["dve_link"])

                def low(i, u):
                    held(dve, None, s["high_ready"], UNITS * i + u + 1)
                    dve.tensor_tensor(ul[:, u % SPLIT, :], raw[u % RAW], uh[:, u % SPLIT, :].bitcast(F32), ALU.subtract)\
                       .then_inc(s["split_ready"], 1)

                def rows_low(i):
                    for c in range(2):
                        held(dve, None, s["xg_high"], 2 * i + c + 1)
                        dve.tensor_tensor(xl[:, 4 * c:4 * c + 4, :], four(bank[c]), xh[:, 4 * c:4 * c + 4, :].bitcast(F32),
                                          ALU.subtract).then_inc(s["xg_ready"], 1)

                def act_low(i, c):
                    held(dve, None, s["act_high"], 2 * i + c + 1)
                    dve.tensor_tensor(al[:, 4 * c:4 * c + 4, :], four(bank[4 + c]), ah[:, 4 * c:4 * c + 4, :].bitcast(F32),
                                      ALU.subtract).then_inc(s["actT_ready"], 1)

                def swiglu(i, c):
                    cols = slice(c * 512, (c + 1) * 512)
                    held(dve, None, s["up_ready"], 1 + 2 * i + c + 1)
                    dve.tensor_scalar(gs[:, cols], bank[2 * c][:, :], 7.0, None, ALU.min).then_inc(s["gate_ready"], 1)
                    link(dve.tensor_scalar(ls[:, cols], bank[2 * c + 1][:, :], 7.0, -7.0, ALU.min, ALU.max))
                    link(dve.scalar_tensor_tensor(ls[:, cols], ls[:, cols], 1.0, gs[:, cols], ALU.add, ALU.mult))
                    held(dve, None, s["sigmoid_ready"], 2 * i + c + 1)
                    dve.tensor_tensor(at[:, cols], ls[:, cols], sg[:, cols], ALU.mult).then_inc(s["act_ready"], 1)

                def body(i):
                    link.turn(0, i, 4)
                    for u in range(8):
                        low(i, u)
                    swiglu(i, 0)
                    for u in range(8, 11):
                        low(i, u)
                    act_low(i, 0)
                    swiglu(i, 1)
                    low(i, 11)
                    act_low(i, 1)
                    rows_low(i + 1)
                dve.wait_ge(s["counted"], 2)
                rows_low(0)
                items(dve, body)

            @block.scalar
            def _(act):
                def high(i, u):
                    r = u % RAW
                    held(act, None, raw_loaded[r], 64 * i + 32 * (u // RAW) + 32)
                    held(act, None, s["unit_used"], UNITS * i + u + 1)
                    act.activation(uh[:, u % SPLIT, :], raw[r], ACT.Copy).then_inc(s["high_ready"], 1)

                def rows_high(i):
                    held(act, None, s["xg_turned"], i + 1)
                    for c in range(2):
                        act.activation(xh[:, 4 * c:4 * c + 4, :], four(bank[c]), ACT.Copy).then_inc(s["xg_high"], 1)

                def act_high(i, c):
                    held(act, None, s["act_turned"], 2 * i + c + 1)
                    act.activation(ah[:, 4 * c:4 * c + 4, :], four(bank[4 + c]), ACT.Copy).then_inc(s["act_high"], 1)

                def sigmoid(i, c):
                    cols = slice(c * 512, (c + 1) * 512)
                    held(act, None, s["gate_ready"], 2 * i + c + 1)
                    act.activation(sg[:, cols], gs[:, cols], ACT.Sigmoid, scale=1.702).then_inc(s["sigmoid_ready"], 1)

                def keep_rows(i):
                    held(act, None, s["unit_used"], SPLIT + UNITS * i)
                    held(act, None, s["y_written"], 16 * i + 16)
                    for n in range(2):
                        act.activation(y[:, n * 512:(n + 1) * 512], bank[6 + n][:, :], ACT.Copy).then_inc(s["y_kept"], 1)
                    held(act, None, s["y_kept"], 1 + 2 * i + 2)
                    act.dma_start(A["expert_out"][bass.ds(i * P, P), :], y[:, :]).then_inc(s["y_written"], 16)

                def body(i):
                    for u in range(4):
                        high(i, u)
                    keep_rows(i)
                    for u in range(4, 8):
                        high(i, u)
                    sigmoid(i, 0)
                    for u in range(8, 11):
                        high(i, u)
                    act_high(i, 0)
                    high(i, 11)
                    sigmoid(i, 1)
                    act_high(i, 1)
                    rows_high(i + 1)

                def skipped(i):
                    act.dma_start(A["expert_out"][bass.ds(i * P + P, P), :], zero_rows[:, :]).then_inc(s["y_written"], 16)
                act.wait_ge(s["counted"], 2)
                for n in range(2):
                    act.activation(bank[6 + n][:, :], zero_rows[:, 0:512], ACT.Copy).then_inc(s["ones"], 1)
                act.wait_ge(s["ones"], 3)
                rows_high(0)
                n = items(act, body, skipped)
                held(act, None, s["unit_used"], n * UNITS + SPLIT)
                act.wait_ge(s["y_written"], ITEMS * 16 + 16)
                for h in range(2):
                    act.activation(y[:, h * 512:(h + 1) * 512], bank[6 + h][:, :], ACT.Copy).then_inc(s["y_kept"], 1)
                held(act, None, s["y_kept"], n * 2 + 3)
                act.dma_start(A["expert_out"][bass.ds(n * P, P), :], y[:, :]).then_inc(s["y_written"], 16)
                act.wait_ge(s["y_written"], ITEMS * 16 + 32)
        sem.over()

    with ExitStack() as st:
        def tb(name, shape, dt=F32):
            return st.enter_context(nc.sbuf_tensor(name, shape, dt))
        back = tb("picked_rows", [P, 4, D])
        bd = tb("b_down", [EXPERTS, D])
        sem = PhaseSems(nc)
        b_loaded, b_product, link_sem, added = (sem("combine_" + n) for n in ("b_loaded", "b_product", "link", "added"))
        fetched = [sem(f"combine_fetched{i}") for i in range(4)]
        with nc.Block() as block:
            @block.sync
            def _(sp):
                sp.dma_start(bd[:, :], A["b_down_2"][0]).then_inc(b_loaded, 16)

            @block.gpsimd
            def _(pool):
                for t in range(TT):
                    for k in range(TOPK):
                        j = t * TOPK + k
                        if j >= 4:
                            pool.wait_ge(added, j - 3)
                        pool.indirect_dma_start(back[:, j % 4, :], None, A["expert_out"],
                                                bass.IndirectOffsetOnAxis(ap=out_row[:, j:j + 1], axis=0))\
                            .then_inc(fetched[j % 4], 16)

            @block.tensor
            def _(pe):
                pe.wait_ge(b_loaded, 16)
                for t in range(TT):
                    for n in range(2):
                        pe.matmul(bank[2 * t + n][:, :], wtT[:, t * P:(t + 1) * P], bd[:, n * 512:(n + 1) * 512],
                                  start=True, stop=True).then_inc(b_product, 1)

            @block.vector
            def _(dve):
                link = Link(dve, link_sem)
                for t in range(TT):
                    for n in range(2):
                        dve.wait_ge(b_product, 2 * t + n + 1)
                        link(dve.tensor_tensor(x[:, t, n * 512:(n + 1) * 512], bank[2 * t + n][:, :],
                                               x[:, t, n * 512:(n + 1) * 512], ALU.add))
                for t in range(TT):
                    for k in range(TOPK):
                        j = t * TOPK + k
                        dve.wait_ge(fetched[j % 4], 16 * (j // 4 + 1))
                        dve.scalar_tensor_tensor(x[:, t, :], back[:, j % 4, :], wt[:, t, k:k + 1], x[:, t, :],
                                                 ALU.mult, ALU.add).then_inc(added, 1)
                        dve.wait_ge(added, j + 1)
        sem.over()
    outer.close()


def last_stage(nc, A, sem, sb, bank, ident, vecT, x, hT, ring, gemm, gemm_phase, out_rows, out_written):
    norm_to_cols(nc, "ple", sem, sb, bank, ident, x, VAT["ln_ple_2"], vecT, hT)
    with ExitStack() as st:
        def tb(name, shape, dt=F32):
            return st.enter_context(nc.sbuf_tensor(name, shape, dt))
        PD = 256
        sg = tb("ple_gate", [P, TT, D])
        gemm_phase(block_pieces(ring, A["w_ple_gate_2"][0]), rows_of(ring, hT),
                   lambda eng, p, b, j, bk: eng.activation(sg[:, j, b * 512:(b + 1) * 512], bk[:, :], ACT.Sigmoid),
                   "act", lambda blk: blk.scalar)
        pr, pT, wp = tb("ple_input", [P, TT, PD]), tb("ple_T", [P, PD // P, SEQ]), tb("w_ple", [P, PD // P, D])
        gf = tb("ln_f", [P, D])
        tmp, stat = tb("ple_tmp", [P, 2, D]), tb("final_stat", [P, 3, TT])
        s = {n: sem("last_" + n) for n in ("loaded", "turned", "kept", "product", "gated", "link", "squared", "rooted", "scaled")}
        with nc.Block() as block:
            @block.sync
            def _(sp):
                sp.dma_start(pr[:, :, :], A["p_2"][0, 0].rearrange("(t q) d -> q t d", q=P)).then_inc(s["loaded"], 16)
                sp.dma_start(wp[:, :, :], A["w_ple_2"][0].rearrange("(k q) n -> q k n", q=P)).then_inc(s["loaded"], 16)
                sp.dma_start(gf[:, :], A["ln_f_2"].unsqueeze(0).broadcast_to([P, D])).then_inc(s["loaded"], 16)
                for t in range(TT):
                    sp.wait_ge(s["scaled"], t + 1)
                    sp.dma_start(out_rows[:, t, :], x[:, t, :]).then_inc(out_written, 16)
                sp.wait_ge(out_written, 16 * TT)

            @block.tensor
            def _(pe):
                pe.wait_ge(s["loaded"], 48)
                for k in range(PD // P):
                    for t in range(TT):
                        mm = pe.transpose(bank[k][:, t * P:(t + 1) * P], pr[:, t, k * P:(k + 1) * P], ident[:, :])
                    mm.then_inc(s["turned"], 1)
                pe.wait_ge(s["kept"], 2)
                for t in range(TT):
                    for n in range(2):
                        for k in range(PD // P):
                            mm = pe.matmul(bank[2 * t + n][:, :], pT[:, k, t * P:(t + 1) * P], wp[:, k, n * 512:(n + 1) * 512],
                                           start=k == 0, stop=k == PD // P - 1)
                        mm.then_inc(s["product"], 1)

            @block.scalar
            def _(act):
                for k in range(2):
                    act.wait_ge(s["turned"], k + 1)
                    act.activation(pT[:, k, :], bank[k][:, :], ACT.Copy).then_inc(s["kept"], 1)
                for t in range(TT):
                    act.wait_ge(s["link"], 4 * t + 4)
                    if t:
                        act.wait_ge(s["squared"], t)
                    act.activation(sg[:, 0, :], x[:, t, :], ACT.Square, accum_out=stat[:, 0, t:t + 1]).then_inc(s["squared"], 1)
                act.wait_ge(s["link"], 4 * TT + 1)
                act.activation(stat[:, 2, :], stat[:, 1, :], ACT.Sqrt).then_inc(s["rooted"], 1)

            @block.vector
            def _(dve):
                link = Link(dve, s["link"])
                for t in range(TT):
                    for n in range(2):
                        dve.wait_ge(s["product"], 2 * t + n + 1)
                        cols = slice(n * 512, (n + 1) * 512)
                        link(dve.tensor_tensor(tmp[:, 0, cols], bank[2 * t + n][:, :], sg[:, t, cols], ALU.mult))
                        link(dve.tensor_tensor(x[:, t, cols], x[:, t, cols], tmp[:, 0, cols], ALU.add))
                dve.wait_ge(s["squared"], TT)
                link(dve.tensor_scalar(stat[:, 1, :], stat[:, 0, :], 1.0 / D, EPS, ALU.mult, ALU.add))
                dve.wait_ge(s["rooted"], 1)
                link(dve.reciprocal(stat[:, 0, :], stat[:, 2, :]))
                for t in range(TT):
                    dve.scalar_tensor_tensor(x[:, t, :], x[:, t, :], stat[:, 0, t:t + 1], gf[:, :], ALU.mult, ALU.mult)\
                       .then_inc(s["scaled"], 1)


def bias_columns():
    import numpy as np
    m = np.zeros((BUCKETS + 1, SHEAR), np.float32)
    half = BUCKETS // 2
    for c in range(SHEAR):
        n = 2 * P - 1 - c
        if n < 0:
            m[BUCKETS, c] = NEG
            continue
        b = n if n < half else min(half + int(math.log(max(n, 1) / half) / math.log(128 / half) * (BUCKETS - half)), BUCKETS - 1)
        m[b, c] += 1.0
        m[BUCKETS - 1, c] -= 1.0
    return m


def build(nc, A, out, stop=None):
    outer = ExitStack()
    with outer:
        def sem(name):
            return outer.enter_context(nc.semaphore(name))

        def sb(name, shape, dt=F32):
            return outer.enter_context(nc.sbuf_tensor(name, shape, dt))

        bank = [outer.enter_context(nc.psum_tensor(f"bank{i}", [P, 512], F32)) for i in range(8)]
        out_rows = out[0].rearrange("(t p) d -> p t d", p=P)

        ident = sb("ident", [P, P])
        vecT = sb("vecT", [P, NVEC])
        x = sb("x_rows", [P, TT, D])
        hT = sb("hT", [P, KT, SEQ])
        gemm = Gemm(nc, sem, sb, bank)
        ring = gemm.ring
        out_written = sem("out_written")

        def finish(rows):
            with nc.Block() as block:
                @block.sync
                def _(sp):
                    sp.dma_start(out_rows, rows).then_inc(out_written, 16)
                    sp.wait_ge(out_written, 16)

        first = ExitStack()
        attnT = first.enter_context(nc.sbuf_tensor("attnT", [P, KT, SEQ], F32))
        rnnT = first.enter_context(nc.sbuf_tensor("rnnT", [P, KT, SEQ], F32))
        biasE = first.enter_context(nc.sbuf_tensor("biasE", [P, HEADS, 2 * P], F32))
        neg_lam = first.enter_context(nc.sbuf_tensor("neg_lam", [P, 1], F32))

        with ExitStack() as st:
            vec = st.enter_context(nc.sbuf_tensor("vec", [NVEC, P], F32))
            lv = st.enter_context(nc.sbuf_tensor("lambda_vectors", [P, 4, HD], F32))
            lp = st.enter_context(nc.sbuf_tensor("lambda_products", [P, 2, HD], F32))
            ls = st.enter_context(nc.sbuf_tensor("lambda_sums", [P, 4], F32))
            rb = st.enter_context(nc.sbuf_tensor("rel_bias", [BUCKETS + 1, HEADS], F32))
            rbb = st.enter_context(nc.sbuf_tensor("rel_bias_wide", [BUCKETS + 1, HEADS, P], F32))
            cols = st.enter_context(nc.sbuf_tensor("bias_columns", [BUCKETS + 1, SHEAR], F32))
            rep = st.enter_context(nc.sbuf_tensor("bias_rows", [P, HEADS, SHEAR], F32))
            zeroed, ident_ready, vec_loaded, x_loaded, lam_loaded, bias_loaded, ones_ready = (
                sem(n) for n in ("zeroed", "ident_ready", "vec_loaded", "x_loaded", "lam_loaded", "bias_loaded", "ones_ready"))
            vec_turned, wide_ready, rows_product, rows_ready, sheared, lam_summed, lam_exp, dve_link, bias_ready = (
                sem("setup_" + n) for n in ("vec_turned", "wide_ready", "rows_product", "rows_ready", "sheared",
                                            "lam_summed", "lam_exp", "dve_link", "bias_ready"))
            flat = A["bias_scratch"]
            nvec_dma = len(VECS) + 4
            with nc.Block() as block:
                @block.sync
                def _(sp):
                    for name, k in VECS:
                        r = VAT[name]
                        src = A[name].rearrange("l ... -> (l ...)") if False else A[name]
                        sp.dma_start(vec[r:r + k, :], src).then_inc(vec_loaded, 16)
                    for name in ("q_norm_g", "k_norm_g"):
                        for half in range(2):
                            sp.dma_start(vec[VAT[name]:VAT[name] + 1, half * HD:(half + 1) * HD], A[name])\
                              .then_inc(vec_loaded, 16)
                    sp.dma_start(x[:, :, :], A["x"][0].rearrange("(t p) d -> p t d", p=P)).then_inc(x_loaded, 16)
                    for i, n in enumerate(("lambda_q1", "lambda_k1", "lambda_q2", "lambda_k2")):
                        sp.dma_start(lv[:, i, :], A[n].broadcast_to([P, HD])).then_inc(lam_loaded, 16)
                    sp.wait_ge(ones_ready, 1)
                    sp.dma_start(rb[0:BUCKETS, :], A["rel_bias"]).then_inc(bias_loaded, 16)
                    sp.dma_start(cols[:, :], A["bias_columns"]).then_inc(bias_loaded, 16)
                    sp.wait_ge(rows_ready, HEADS)
                    sp.dma_start(flat.rearrange("(h p m) -> p h m", h=HEADS, p=P), rep[:, :, :]).then_inc(sheared, 16)
                    sp.wait_ge(sheared, 16)
                    for h in range(HEADS):
                        at = h * P * SHEAR + P - 1
                        sp.dma_start(biasE[:, h, :], flat[at:at + P * (SHEAR - 1)]
                                     .rearrange("(p m) -> p m", p=P)[:, 0:2 * P]).then_inc(bias_ready, 16)
                    sp.wait_ge(bias_ready, 16 * HEADS)
                    sp.wait_ge(x_loaded, 16)

                @block.gpsimd
                def _(pool):
                    pool.memset(ident[:, :], 0.0).then_inc(zeroed, 1)
                    pool.wait_ge(zeroed, 1)
                    pool.affine_select(out=ident[:, :], in_=ident[:, :], compare_op=ALU.not_equal, fill=1.0, base=0,
                                       pattern=[[-1, P]], channel_multiplier=1).then_inc(ident_ready, 1)

                @block.vector
                def _(dve):
                    link = Link(dve, dve_link)
                    link(dve.memset(rbb[:, :, :], 1.0))
                    dve.memset(rb[:, :], 1.0).then_inc(ones_ready, 1)
                    dve.wait_ge(bias_loaded, 32)
                    for h in range(HEADS):
                        link(dve.tensor_scalar(rbb[:, h, :], rbb[:, h, :], rb[:, h:h + 1], None, ALU.mult))
                    dve.wait_ge(vec_turned, 1)
                    link(dve.tensor_copy(vecT[:, :], bank[0][:, 0:NVEC]))
                    link(dve.tensor_scalar(vecT[:, VAT["k_norm_g"]:VAT["k_norm_g"] + 1],
                                           vecT[:, VAT["k_norm_g"]:VAT["k_norm_g"] + 1], HD ** -0.5, None, ALU.mult))
                    link(dve.tensor_scalar(vecT[:, VAT["subln_g"]:VAT["subln_g"] + 1],
                                           vecT[:, VAT["subln_g"]:VAT["subln_g"] + 1], 1.0 - 0.2, None, ALU.mult))
                    dve.wait_ge(lam_loaded, 64)
                    link(dve.tensor_tensor(lp[:, :, :], lv[:, 0:4:2, :], lv[:, 1:4:2, :], ALU.mult))
                    dve.tensor_reduce(ls[:, 0:2], lp[:, :, :], AX.X, ALU.add).then_inc(lam_summed, 1)
                    dve.wait_ge(lam_exp, 1)
                    dve.scalar_tensor_tensor(neg_lam[:, :], ls[:, 3:4], -0.2, ls[:, 2:3], ALU.add, ALU.subtract)\
                       .then_inc(dve_link, 1)

                @block.scalar
                def _(act):
                    act.wait_ge(lam_summed, 1)
                    act.activation(ls[:, 2:4], ls[:, 0:2], ACT.Exp).then_inc(lam_exp, 1)
                    for h in range(HEADS):
                        act.wait_ge(rows_product, h + 1)
                        act.activation(rep[:, h, :], bank[(h + 1) % 8][:, 0:SHEAR], ACT.Copy).then_inc(rows_ready, 1)

                @block.tensor
                def _(pe):
                    pe.wait_ge(ident_ready, 1)
                    pe.wait_ge(vec_loaded, 16 * nvec_dma)
                    pe.transpose(bank[0][:, 0:NVEC], vec[:, :], ident[0:NVEC, 0:NVEC]).then_inc(vec_turned, 1)
                    pe.wait_ge(dve_link, 1 + HEADS + 1)
                    for h in range(HEADS):
                        pe.matmul(bank[(h + 1) % 8][:, 0:SHEAR], rbb[:, h, :], cols[:, :], start=True, stop=True)\
                          .then_inc(rows_product, 1)

        norm_to_cols(nc, "mix", sem, sb, bank, ident, x, VAT["norm_mix_g"], vecT, hT)

        w_in = A["w_in"][0]
        QKW = 3 * D

        def act_copy(dst):
            return lambda eng, p, b, j, bk: eng.activation(dst(p, b, j), bk[:, :], ACT.Copy)

        def dve_copy(dst):
            return lambda eng, p, b, j, bk: eng.tensor_copy(dst(p, b, j), bk[:, :])

        def gemm_phase(pairs, pieces, operands, act_evac, act_js, dve_evac, dve_js):
            with nc.Block() as block:
                @block.sync
                def _(sp):
                    gemm.sp(sp, pairs, pieces)

                @block.tensor
                def _(pe):
                    gemm.pe(pe, pairs, operands)

                if act_js:
                    @block.scalar
                    def _(act):
                        gemm.drain(act, "act", pairs, act_js, act_evac)

                if dve_js:
                    @block.vector
                    def _(dve):
                        gemm.drain(dve, "dve", pairs, dve_js, dve_evac)
            gemm.done += pairs

        with ExitStack() as st:
            XG = st.enter_context(nc.sbuf_tensor("XG", [P, 2, KT, SEQ], F32))
            dst = lambda p, b, j: XG[:, p, 4 * b + j, :]
            gemm_phase(2, block_pieces(ring, w_in, col0=QKW), cols_of(ring, hT), act_copy(dst), (0, 2), dve_copy(dst), (1, 3))
            lru(nc, sem, bank, vecT, XG, A["w_rg_a"][0], A["w_rg_x"][0], rnnT)

        with ExitStack() as st:
            O = st.enter_context(nc.sbuf_tensor("diff_out", [P, TT, D], F32))
            with ExitStack() as st2:
                QKV = st2.enter_context(nc.sbuf_tensor("QKV", [P, 3, TT, D], F32))
                dst = lambda p, b, j: QKV[:, p, j, b * 512:(b + 1) * 512]
                gemm_phase(3, block_pieces(ring, w_in), rows_of(ring, hT), act_copy(dst), (0, 2), dve_copy(dst), (1, 3))
                diff_attention(nc, sem, bank, ident, vecT, QKV, biasE, neg_lam, O)
            sq = st.enter_context(nc.sbuf_tensor("subln_sq", [P, TT, D], F32))
            ss = st.enter_context(nc.sbuf_tensor("subln_stat", [P, TT * HEADS], F32))
            s1, s2, s3, s4 = (sem("subln_" + n) for n in ("squared", "dve_link", "rooted", "normed"))
            grouped = lambda t: t[:, :, :].rearrange("p t (h d) -> p (t h) d", d=P)
            with nc.Block() as block:
                @block.scalar
                def _(act):
                    act.activation(sq[:, :, :], O[:, :, :], ACT.Square).then_inc(s1, 1)
                    act.wait_ge(s2, 2)
                    act.activation(ss[:, :], ss[:, :], ACT.Sqrt).then_inc(s3, 1)

                @block.vector
                def _(dve):
                    link = Link(dve, s2)
                    dve.wait_ge(s1, 1)
                    link(dve.tensor_reduce(ss[:, :], grouped(sq), AX.X, ALU.add))
                    link(dve.tensor_scalar(ss[:, :], ss[:, :], 1.0 / P, EPS, ALU.mult, ALU.add))
                    dve.wait_ge(s3, 1)
                    link(dve.reciprocal(ss[:, :], ss[:, :]))
                    dve.tensor_tensor(grouped(O), grouped(O), ss[:, :].unsqueeze(2).broadcast_to([P, TT * HEADS, P]),
                                      ALU.mult).then_inc(s4, 1)
            transpose_rows(nc, "attn_out", sem, bank, ident, O, KT, attnT,
                           lambda j: vecT[:, VAT["subln_g"]:VAT["subln_g"] + 1])

        with ExitStack() as st:
            GT = st.enter_context(nc.sbuf_tensor("gatesT", [P, 2, KT, SEQ], F32))
            tmp = st.enter_context(nc.sbuf_tensor("merge_tmp", [P, 512], F32))
            merge_step = sem("merge_step")

            def sigmoid(eng, p, b, j, bk):
                return eng.activation(GT[:, p, 4 * b + j, :], bk[:, :], ACT.Sigmoid)
            gemm_phase(2, block_pieces(ring, w_in, col0=QKW + 2 * D), cols_of(ring, hT), sigmoid, (0, 1, 2, 3), None, ())
            gate = lambda which: (lambda eng, p, b, j, bk: eng.tensor_tensor(GT[:, which, 4 * b + j, :], bk[:, :],
                                                                           GT[:, which, 4 * b + j, :], ALU.mult))
            gemm_phase(1, block_pieces(ring, A["w_proj_attn"][0]), cols_of(ring, attnT), None, (), gate(0), (0, 1, 2, 3))
            gemm_phase(1, block_pieces(ring, A["w_proj_rnn"][0]), cols_of(ring, rnnT), None, (), gate(1), (0, 1, 2, 3))
            with nc.Block() as block:
                @block.vector
                def _(dve):
                    dve.tensor_tensor(GT[:, 0], GT[:, 0], GT[:, 1], ALU.add).then_inc(merge_step, 1)
            residual = lambda eng, p, b, j, bk: eng.tensor_tensor(x[:, j, b * 512:(b + 1) * 512], bk[:, :],
                                                                 x[:, j, b * 512:(b + 1) * 512], ALU.add)
            gemm_phase(1, block_pieces(ring, A["w_out"][0]), rows_of(ring, GT[:, 0]), None, (), residual, (0, 1, 2, 3))
        first.close()

        with ExitStack() as st:
            norm_to_cols(nc, "mlp", sem, sb, bank, ident, x, VAT["norm_mlp_g"], vecT, hT)
            upT = st.enter_context(nc.sbuf_tensor("upT", [P, FF // P, SEQ], F32))
            relu_done, squared = sem("relu_done"), sem("up_squared")
            pairs = FF // 1024
            with nc.Block() as block:
                @block.sync
                def _(sp):
                    gemm.sp(sp, pairs, block_pieces(ring, A["w_up"][0]))

                @block.tensor
                def _(pe):
                    gemm.pe(pe, pairs, cols_of(ring, hT))

                @block.vector
                def _(dve):
                    gemm.drain(dve, "dve", pairs, (0, 1, 2, 3),
                               lambda eng, p, b, j, bk: eng.tensor_scalar(upT[:, p * 8 + (4 * b + j), :], bk[:, :], 0.0,
                                                                          None, ALU.max))

                @block.scalar
                def _(act):
                    with act.Fori(0, pairs) as p:
                        for b in range(2):
                            for j in range(4):
                                held(act, gemm.carrier["act"], gemm.drained[j], 2 * (p + gemm.done) + b + 1)
                                act.activation(upT[:, p * 8 + (4 * b + j), :], upT[:, p * 8 + (4 * b + j), :],
                                               ACT.Square).then_inc(squared, 1)
            gemm.done += pairs
            w_down = A["w_down"][0]

            def down_pieces(p, b):
                src = w_down[bass.ds(p * D, D), b * 512:(b + 1) * 512].rearrange("(k q) n -> q k n", q=P)
                return [(ring[:, b, 0:4, :], src[:, 0:4, :]), (ring[:, b, 4:8, :], src[:, 4:8, :])]
            with nc.Block() as block:
                @block.sync
                def _(sp):
                    gemm.sp(sp, pairs, down_pieces)

                @block.tensor
                def _(pe):
                    for p in range(pairs):
                        gemm.pe_pair(pe, p + gemm.done,
                                     lambda r, b, j, k: (upT[:, 8 * p + k, j * P:(j + 1) * P], ring[:, b, k, :]),
                                     start=p == 0, stop=p == pairs - 1)

                @block.vector
                def _(dve):
                    for b in range(2):
                        for j in range(4):
                            dve.wait_ge(gemm.product, 4 * (2 * (gemm.done + pairs - 1) + b) + j + 1)
                            dve.tensor_tensor(x[:, j, b * 512:(b + 1) * 512], bank[4 * b + j][:, :],
                                              x[:, j, b * 512:(b + 1) * 512], ALU.add).then_inc(gemm.drained[j], 1)
                    for j in range(4):
                        dve.sem_inc(gemm.drained[j], 2 * (pairs - 1))
            gemm.done += pairs
        if stop == "first":
            finish(x[:, :, :])
            return
        second_layer(nc, A, outer, sem, sb, bank, ident, vecT, x, hT, gemm, out_rows, out_written, stop)


_OUT_SHAPE = (1, SEQ, D)
_VECTOR = {n for n, _ in VECS}


def kernel(**inputs):
    import numpy as np
    import concourse.bacc as bacc
    from concourse.bass_utils import run_bass_kernel_spmd

    nc = bacc.Bacc("TRN2", target_bir_lowering=False, num_devices=1)
    arrays, A = {}, {}
    inputs = dict(inputs)
    inputs["bias_columns"] = bias_columns()
    for name, value in inputs.items():
        a = np.ascontiguousarray(value)
        if name in _VECTOR:
            a = a.reshape(-1, P)
        arrays[f"in_{name}"] = a
        A[name] = nc.dram_tensor(f"in_{name}", a.shape, mybir.dt.from_np(a.dtype), kind="ExternalInput").ap()
    A["bias_scratch"] = nc.dram_tensor("bias_scratch", (HEADS * P * SHEAR,), F32, kind="Internal").ap()
    A["h2_scratch"] = nc.dram_tensor("h2_scratch", (SEQ, D), F32, kind="Internal").ap()
    A["slot_tokens"] = nc.dram_tensor("slot_tokens", ((ITEMS + 1) * P, 1), I32, kind="Internal").ap()
    A["expert_out"] = nc.dram_tensor("expert_out", ((ITEMS + 1) * P, D), F32, kind="Internal").ap()
    A["bias_parts"] = nc.dram_tensor("bias_parts", (EXPERTS, 3, 2 * D), BF16, kind="Internal").ap()
    out = nc.dram_tensor("out_rows", _OUT_SHAPE, F32, kind="ExternalOutput").ap()
    A["ln2_row"] = A["ln2_2"].rearrange("k p -> (k p)").unsqueeze(0)
    build(nc, A, out, STOP)
    r = run_bass_kernel_spmd(nc, [arrays], core_ids=[0])
    return r.results[0]["out_rows"]


STOP = None
```

```python
import math
from contextlib import ExitStack

import concourse.bass as bass
from concourse import mybir

F32 = mybir.dt.float32
BF16 = mybir.dt.bfloat16
F32R = mybir.dt.float32r
I32 = mybir.dt.int32
U32 = mybir.dt.uint32
ALU = mybir.AluOpType
ACT = mybir.ActivationFunctionType
AX = mybir.AxisListType

P = 128
SEQ = 512
TT = SEQ // P
D = 1024
KT = D // P
HEADS = 8
BUCKETS = 32
FF = 4096
EXPERTS = 32
TOPK = 4
EPS = 1e-6
NEG = -1e30
CMP_STRIDE = 16
CMP_BLOCK = 32
NCMP = (SEQ - CMP_BLOCK) // CMP_STRIDE + 1
HD = 64
SHEAR = 384
ITEMS = SEQ * TOPK // P + EXPERTS - 1

VECS = [("norm_mix_g", 8), ("norm_mlp_g", 8), ("conv_w", 32), ("conv_b", 8), ("b_rg_a", 8), ("b_rg_x", 8),
        ("lru_lambda", 8), ("ln1_2", 8), ("ln2_2", 8), ("ln_ple_2", 8), ("gn_nsa_2", 4), ("gn_fox_2", 4),
        ("subln_g", 1)]
VAT = {}
_r = 0
for _n, _k in VECS:
    VAT[_n] = _r
    _r += _k
VAT["q_norm_g"], VAT["k_norm_g"] = _r, _r + 1
NVEC = _r + 2


class Link:

    def __init__(self, eng, sem, base=0):
        self.eng, self.sem, self.base, self.n = eng, sem, base, 0

    def __call__(self, ins):
        ins.then_inc(self.sem, 1)
        self.n += 1
        self.eng.wait_ge(self.sem, self.base + self.n)
        return self

    def turn(self, base, i, per):
        self.base, self.n = base + i * per, 0


def held(eng, carrier, sem, value):
    eng.wait_ge(sem, value)
    if carrier is not None and not isinstance(value, int):
        eng.sem_inc(carrier, 1)


class PhaseSems:

    def __init__(self, nc):
        self.nc, self.all = nc, []

    def __call__(self, name):
        self.all.append(self.nc.alloc_semaphore(name=name))
        return self.all[-1]

    def over(self):
        self.nc.clear_and_free_semaphores(self.all)
        self.nc.all_engine_barrier()


class Gemm:

    def __init__(self, nc, sem, sb, ps):
        self.nc = nc
        self.loaded = [sem("weights_loaded0"), sem("weights_loaded1")]
        self.high_ready, self.split_ready = sem("weights_high"), sem("weights_split")
        self.half_used = sem("weights_half_used")
        self.product = sem("product_ready")
        self.drained = [sem(f"bank_drained{j}") for j in range(4)]
        self.carrier = {e: sem(f"carrier_{e}") for e in ("sp", "pe", "act", "dve", "pool")}
        self.ring = sb("weight_ring", [P, 2, 8, 512])
        self.bank = ps
        self.done = 0
        self.ahead = False

    def loads(self, sp, p, pair, pieces):
        for b in range(2):
            if not isinstance(pair, int) or pair > 0:
                held(sp, None, self.split_ready, 4 * (pair - 1) + 2 * b + 2)
            for dst, src in pieces(p, b):
                sp.dma_start(dst, src).then_inc(self.loaded[b], 16)

    def load_ahead(self, sp, pieces, pairs=0):
        self.loads(sp, 0, self.done + pairs, pieces)

    def sp(self, sp, pairs, pieces, following):
        if not self.ahead:
            self.loads(sp, 0, self.done, pieces)
        if pairs > 1:
            with sp.Fori(1, pairs) as p:
                self.loads(sp, p, p + self.done, pieces)
        if following:
            self.load_ahead(sp, following, pairs)

    def pe_block(self, pe, pair, b, operands, start=True, stop=True, width=512):
        for h in range(2):
            held(pe, None, self.split_ready, 4 * pair + 2 * b + h + 1)
            for j in range(4):
                if h == 0 and start and (not isinstance(pair, int) or pair > 0):
                    held(pe, None, self.drained[j], 2 * (pair - 1) + b + 1)
                for k in range(4 * h, 4 * h + 4):
                    for n, (wp, xp) in enumerate(((0, 0), (0, 1), (1, 0))):
                        lhsT, rhs = operands((self.high, self.low)[wp][:, h, k % 4, 0:width], xp, j, k)
                        mm = pe.matmul(self.bank[4 * b + j][:, 0:width], lhsT, rhs,
                                       start=start and k == 0 and n == 0, stop=stop and k == 7 and n == 2)
                if h == 1:
                    mm.then_inc(self.product, 1)
            if h == 0:
                mm.then_inc(self.half_used, 1)

    def split(self, eng, who, pair, b, width=512):
        n = 2 * pair + b
        for h in range(2):
            raw = self.ring[:, b, 4 * h:4 * h + 4, 0:width]
            if who == "act":
                held(eng, None, self.loaded[b], 32 * (pair + 1))
                if not isinstance(n, int) or n > 0:
                    held(eng, None, *((self.half_used, n) if h == 0 else (self.product, 4 * n)))
                eng.activation(self.high[:, h, :, 0:width], raw, ACT.Copy).then_inc(self.high_ready, 1)
            else:
                held(eng, None, self.high_ready, 2 * n + h + 1)
                eng.tensor_tensor(self.low[:, h, :, 0:width], raw, self.high[:, h, :, 0:width].bitcast(F32), ALU.subtract)\
                   .then_inc(self.split_ready, 1)

    def follow(self, eng, who, pairs, drain, widths=(512, 512), accumulate=False):
        split = lambda p, b: self.split(eng, who, p + self.done, b, widths[b])
        split(0, 0)
        if accumulate:
            for p in range(pairs - 1):
                split(p, 1)
                split(p + 1, 0)
        elif pairs > 1:
            with eng.Fori(0, pairs - 1) as p:
                split(p, 1)
                drain(eng, p, 0)
                split(p + 1, 0)
                drain(eng, p, 1)
        split(pairs - 1, 1)
        drain(eng, pairs - 1, 0)
        drain(eng, pairs - 1, 1)

    def drain(self, who, js, evac):
        def one(eng, p, b):
            for j in js:
                held(eng, self.carrier[who], self.product, 4 * (2 * (p + self.done) + b) + j + 1)
                evac(eng, p, b, j, self.bank[4 * b + j]).then_inc(self.drained[j], 1)
        return one

    def phase(self, pairs, pieces, operands, act_drain=None, dve_drain=None, following=None, widths=(512, 512),
              accumulate=False):
        nothing = lambda eng, p, b: None
        with self.nc.sbuf_tensor(f"split_high{self.done}", [P, 2, 4, 512], F32R) as self.high, \
                self.nc.sbuf_tensor(f"split_low{self.done}", [P, 2, 4, 512], F32R) as self.low:
            with self.nc.Block() as block:
                @block.sync
                def _(sp):
                    self.sp(sp, pairs, pieces, following)

                @block.tensor
                def _(pe):
                    if accumulate:
                        for p in range(pairs):
                            for b in range(2):
                                self.pe_block(pe, p + self.done, b, operands(p), start=p == 0, stop=p == pairs - 1)
                    else:
                        for b in range(2):
                            self.pe_block(pe, self.done, b, operands, width=widths[b])
                        if pairs > 1:
                            with pe.Fori(1, pairs) as p:
                                for b in range(2):
                                    self.pe_block(pe, p + self.done, b, operands, width=widths[b])

                @block.scalar
                def _(act):
                    self.follow(act, "act", pairs, act_drain or nothing, widths, accumulate)

                @block.vector
                def _(dve):
                    self.follow(dve, "dve", pairs, dve_drain or nothing, widths, accumulate)
                    if accumulate:
                        for j in range(4):
                            dve.sem_inc(self.drained[j], 2 * (pairs - 1))
        self.done += pairs
        self.ahead = following is not None


def cols_of(xT):
    return lambda w, part, j, k: (w[:, j * P:(j + 1) * P], xT[part][:, k, :])


def rows_of(xT):
    return lambda w, part, j, k: (xT[part][:, k, j * P:(j + 1) * P], w)


def block_pieces(ring, w, col0=0, row0=0):
    def pieces(p, b):
        src = w[row0:row0 + D, bass.ds(p * 1024 + (col0 + b * 512), 512)].rearrange("(k q) n -> q k n", q=P)
        return [(ring[:, b, 0:4, :], src[:, 0:4, :]), (ring[:, b, 4:8, :], src[:, 4:8, :])]
    return pieces


def norm_to_cols(nc, name, sem, sb, bank, ident, x, g_at, vecT, hT, at=0, width=D, width_at=0, keep=None):
    kt = width // P
    with ExitStack() as st:
        sq = st.enter_context(nc.sbuf_tensor(name + "_sq", [P, width], F32))
        rows = keep if keep is not None else st.enter_context(nc.sbuf_tensor(name + "_rows", [P, TT, width], F32))
        stat = st.enter_context(nc.sbuf_tensor(name + "_stat", [P, 4, TT], F32))
        act_link, dve_link, rooted, scaled, turned, high_ready, low_ready = (
            sem(f"{name}_{s}") for s in ("act_link", "dve_link", "rooted", "scaled", "turned", "high_ready", "low_ready"))
        with nc.Block() as block:
            @block.scalar
            def _(act):
                link = Link(act, act_link)
                for t in range(TT):
                    link(act.activation(sq[:, :], x[:, t, width_at:width_at + width], ACT.Square,
                                        accum_out=stat[:, 0, t:t + 1]))
                act.wait_ge(dve_link, 1)
                act.activation(stat[:, 2, :], stat[:, 1, :], ACT.Sqrt).then_inc(rooted, 1)
                for j in range(kt):
                    act.wait_ge(turned, j + 1)
                    act.activation(hT[0][:, at + j, :], bank[j % 8][:, :], ACT.Copy,
                                   scale=vecT[:, g_at + j:g_at + j + 1]).then_inc(high_ready, 1)

            @block.vector
            def _(dve):
                link = Link(dve, dve_link)
                dve.wait_ge(act_link, TT)
                link(dve.tensor_scalar(stat[:, 1, :], stat[:, 0, :], 1.0 / width, EPS, ALU.mult, ALU.add))
                dve.wait_ge(rooted, 1)
                link(dve.reciprocal(stat[:, 3, :], stat[:, 2, :]))
                for t in range(TT):
                    dve.tensor_scalar(rows[:, t, 0:width], x[:, t, width_at:width_at + width], stat[:, 3, t:t + 1],
                                      None, ALU.mult).then_inc(scaled, 1)
                for j in range(kt):
                    dve.wait_ge(high_ready, j + 1)
                    dve.scalar_tensor_tensor(hT[1][:, at + j, :], bank[j % 8][:, :], vecT[:, g_at + j:g_at + j + 1],
                                             hT[0][:, at + j, :].bitcast(F32), ALU.mult, ALU.subtract).then_inc(low_ready, 1)

            @block.tensor
            def _(pe):
                pe.wait_ge(scaled, TT)
                for j in range(kt):
                    for t in range(TT):
                        mm = pe.transpose(bank[j % 8][:, t * P:(t + 1) * P], rows[:, t, j * P:(j + 1) * P], ident[:, :])
                    mm.then_inc(turned, 1)


def log1p_steps(dve, link, out, e, s, s2):
    link(dve.tensor_scalar(s2, e, 2.0, None, ALU.add))
    link(dve.reciprocal(s, s2))
    link(dve.tensor_tensor(s, s, e, ALU.mult))
    link(dve.tensor_tensor(s2, s, s, ALU.mult))
    link(dve.tensor_scalar(out, s2, 1.0 / 17, None, ALU.mult))
    for k in range(7, 0, -1):
        link(dve.scalar_tensor_tensor(out, out, 1.0 / (2 * k + 1), s2, ALU.add, ALU.mult))
    link(dve.scalar_tensor_tensor(out, out, 1.0, s, ALU.add, ALU.mult))
    link(dve.tensor_scalar(out, out, 2.0, None, ALU.mult))


def transpose_rows(nc, name, sem, bank, ident, x, tiles, outT, scale):
    turned, high_ready, low_ready = sem(name + "_turned"), sem(name + "_high"), sem(name + "_low")
    with nc.Block() as block:
        @block.tensor
        def _(pe):
            for j in range(tiles):
                for t in range(TT):
                    mm = pe.transpose(bank[j][:, t * P:(t + 1) * P], x[:, t, j * P:(j + 1) * P], ident[:, :])
                mm.then_inc(turned, 1)

        @block.scalar
        def _(act):
            for j in range(tiles):
                act.wait_ge(turned, j + 1)
                act.activation(outT[0][:, j, :], bank[j][:, :], ACT.Copy, scale=scale).then_inc(high_ready, 1)

        @block.vector
        def _(dve):
            for j in range(tiles):
                dve.wait_ge(high_ready, j + 1)
                dve.scalar_tensor_tensor(outT[1][:, j, :], bank[j][:, :], scale, outT[0][:, j, :].bitcast(F32),
                                         ALU.mult, ALU.subtract).then_inc(low_ready, 1)


def split_cols(nc, name, sem, xT, outT):
    high_ready, low_ready = sem(name + "_high"), sem(name + "_low")
    with nc.Block() as block:
        @block.scalar
        def _(act):
            for j in range(KT):
                act.activation(outT[0][:, j, :], xT[:, j, :], ACT.Copy).then_inc(high_ready, 1)

        @block.vector
        def _(dve):
            for j in range(KT):
                dve.wait_ge(high_ready, j + 1)
                dve.tensor_tensor(outT[1][:, j, :], xT[:, j, :], outT[0][:, j, :].bitcast(F32), ALU.subtract)\
                   .then_inc(low_ready, 1)


def lru(nc, sem, bank, vecT, XG, w_a_dram, w_x_dram, rnnT):
    sem = PhaseSems(nc)
    with ExitStack() as st:
        def sb(name, shape):
            return st.enter_context(nc.sbuf_tensor(name, shape, F32))
        wa, wx = sb("lru_wa", [P, KT, P]), sb("lru_wx", [P, KT, P])
        xc, r, i = sb("lru_xc", [P, KT, SEQ]), sb("lru_r", [P, KT, SEQ]), sb("lru_i", [P, KT, SEQ])
        sp_t = sb("lru_softplus", [P, 5, KT])
        xr, gr, a = XG[:, 0], XG[:, 1], XG[:, 0]
        names = ("weights", "abs", "exp", "softplus", "convolved", "gate_product", "gate_ready", "input_gated",
                 "decay_ready", "tanh_ready", "one_minus", "rooted", "scaled", "scanned", "gelu", "out", "act_link", "dve_link")
        s = {n: sem("lru_" + n) for n in names}
        lam = vecT[:, VAT["lru_lambda"]:VAT["lru_lambda"] + KT]
        with nc.Block() as block:
            @block.sync
            def _(sp):
                sp.dma_start(wa[:, :, :], w_a_dram.rearrange("n e f -> e n f")).then_inc(s["weights"], 16)
                sp.dma_start(wx[:, :, :], w_x_dram.rearrange("n e f -> e n f")).then_inc(s["weights"], 16)

            @block.vector
            def _(dve):
                link = Link(dve, s["dve_link"])
                link(dve.tensor_scalar(sp_t[:, 0, :], lam, -1.0, None, ALU.mult))
                dve.tensor_tensor(sp_t[:, 0, :], sp_t[:, 0, :], lam, ALU.min).then_inc(s["abs"], 1)
                dve.wait_ge(s["exp"], 1)
                log1p_steps(dve, link, sp_t[:, 2, :], sp_t[:, 1, :], sp_t[:, 3, :], sp_t[:, 4, :])
                link(dve.tensor_scalar(sp_t[:, 3, :], lam, -1.0, 0.0, ALU.mult, ALU.max))
                link(dve.tensor_tensor(sp_t[:, 2, :], sp_t[:, 2, :], sp_t[:, 3, :], ALU.add))
                link(dve.tensor_scalar(sp_t[:, 2, :], sp_t[:, 2, :], 8.0, None, ALU.mult))
                dve.tensor_scalar(sp_t[:, 3, :], sp_t[:, 2, :], -1.0, None, ALU.mult).then_inc(s["softplus"], 1)
                for n in range(KT):
                    w = lambda tap: vecT[:, VAT["conv_w"] + tap * KT + n:VAT["conv_w"] + tap * KT + n + 1]
                    link(dve.tensor_scalar(xc[:, n, :], xr[:, n, :], w(3),
                                           vecT[:, VAT["conv_b"] + n:VAT["conv_b"] + n + 1], ALU.mult, ALU.add))
                    for tap in (2, 1, 0):
                        back = 3 - tap
                        last = dve.scalar_tensor_tensor(xc[:, n, back:], xr[:, n, 0:SEQ - back], w(tap),
                                                        xc[:, n, back:], ALU.mult, ALU.add)
                        if tap:
                            link(last)
                    last.then_inc(s["convolved"], 1)
                dve.wait_ge(s["convolved"], KT)
                dve.wait_ge(s["gate_ready"], 2 * KT)
                link(dve.tensor_tensor(i[:, :, :], i[:, :, :], xc[:, :, :], ALU.mult))
                dve.wait_ge(s["decay_ready"], KT)
                link(dve.tensor_tensor(xc[:, :, :], a, a, ALU.mult))
                dve.wait_ge(s["tanh_ready"], KT)
                dve.scalar_tensor_tensor(r[:, :, :].rearrange("p n t -> p (n t)"),
                                         xc[:, :, :].rearrange("p n t -> p (n t)"), 1.0,
                                         r[:, :, :].rearrange("p n t -> p (n t)"),
                                         ALU.add, ALU.mult).then_inc(s["one_minus"], 1)
                dve.wait_ge(s["rooted"], 1)
                link(dve.tensor_tensor(i[:, :, :], i[:, :, :], r[:, :, :], ALU.mult))
                for n in range(KT):
                    link(dve.tensor_tensor_scan(xc[:, n, :], a[:, n, :], i[:, n, :], 0.0, ALU.mult, ALU.add))
                dve.wait_ge(s["gelu"], 1)
                dve.tensor_tensor(rnnT[:, :, :], xc[:, :, :], gr, ALU.mult).then_inc(s["out"], 1)

            @block.tensor
            def _(pe):
                pe.wait_ge(s["weights"], 32)
                for n in range(KT):
                    pe.wait_ge(s["convolved"], n + 1)
                    if n >= 4:
                        pe.wait_ge(s["gate_ready"], 2 * (n - 3))
                    pe.matmul(bank[2 * (n % 4)][:, :], wa[:, n, :], xc[:, n, :], start=True, stop=True)\
                      .then_inc(s["gate_product"], 1)
                    pe.matmul(bank[2 * (n % 4) + 1][:, :], wx[:, n, :], xc[:, n, :], start=True, stop=True)\
                      .then_inc(s["gate_product"], 1)

            @block.scalar
            def _(act):
                act.wait_ge(s["abs"], 1)
                act.activation(sp_t[:, 1, :], sp_t[:, 0, :], ACT.Exp).then_inc(s["exp"], 1)
                for n in range(KT):
                    for m, (dst, b) in enumerate(((r, "b_rg_a"), (i, "b_rg_x"))):
                        act.wait_ge(s["gate_product"], 2 * n + m + 1)
                        act.activation(dst[:, n, :], bank[2 * (n % 4) + m][:, :], ACT.Sigmoid,
                                       bias=vecT[:, VAT[b] + n:VAT[b] + n + 1]).then_inc(s["gate_ready"], 1)
                act.wait_ge(s["convolved"], KT)
                act.wait_ge(s["softplus"], 1)
                act.wait_ge(s["gate_ready"], 2 * KT)
                for n in range(KT):
                    act.activation(a[:, n, :], r[:, n, :], ACT.Exp, scale=sp_t[:, 3, n:n + 1])\
                       .then_inc(s["decay_ready"], 1)
                act.wait_ge(s["decay_ready"], KT)
                for n in range(KT):
                    act.activation(r[:, n, :], r[:, n, :], ACT.Tanh, scale=sp_t[:, 2, n:n + 1])\
                       .then_inc(s["tanh_ready"], 1)
                act.wait_ge(s["one_minus"], 1)
                act.activation(r[:, :, :], r[:, :, :], ACT.Sqrt).then_inc(s["rooted"], 1)
                act.activation(gr, gr, ACT.Gelu_apprx_tanh).then_inc(s["gelu"], 1)
    sem.over()


def diff_attention(nc, sem, bank, ident, vecT, QKV, biasE, neg_lam, O):
    sem = PhaseSems(nc)
    with ExitStack() as st:
        def sb(name, shape):
            return st.enter_context(nc.sbuf_tensor(name, shape, F32))
        sq = O
        stat = sb("da_stat", [P, 2, TT, 2 * HEADS])
        rstd = sb("da_rstd", [P, 2, TT, 2 * HEADS])
        stage = sb("da_stage", [P, 2, TT, P])
        qkT = sb("da_qkT", [P, 2, SEQ])
        prob = sb("da_prob", [P, 4, SEQ])
        comb = sb("da_comb", [P, 2, SEQ])
        turned_sb = sb("da_turned", [P, 2, SEQ])
        nmax = sb("da_nmax", [P, 4])
        rsum = sb("da_rsum", [P, 4])
        rinv = sb("da_rinv", [P, 4])
        names = ("squared", "summed", "rooted", "staged", "qk_turned", "qk_ready", "scores_ready", "max_ready",
                 "probs_ready", "combined", "comb_turned", "combT_ready", "pv_ready", "out_stored", "dve_link", "act_link")
        s = {n: sem("da_" + n) for n in names}
        cr = {e: sem("da_carrier_" + e) for e in ("pe", "act", "dve")}
        S = [bank[0], bank[1], bank[2], bank[3]]
        T = [bank[4], bank[5]]
        OB = [bank[6], bank[7]]
        nk = [(q + 1) * P for q in range(TT)]
        with nc.Block() as block:
            @block.vector
            def _(dve):
                link = Link(dve, s["dve_link"])
                for m in range(2):
                    dve.wait_ge(s["squared"], m + 1)
                    dve.tensor_reduce(stat[:, m].rearrange("p t g -> p (t g)"),
                                      sq[:, :, :].rearrange("p t (g d) -> p (t g) d", d=HD), AX.X, ALU.add)\
                       .then_inc(s["summed"], 1)
                dve.wait_ge(s["summed"], 2)
                link(dve.tensor_scalar(stat[:, :, :, :], stat[:, :, :, :], 1.0 / HD, EPS, ALU.mult, ALU.add))
                dve.wait_ge(s["rooted"], 1)
                link(dve.reciprocal(rstd[:, :, :, :], rstd[:, :, :, :]))

                def unit_max(h, q):
                    for c in range(2):
                        u = 8 * h + 2 * q + c
                        dve.wait_ge(s["scores_ready"], u + 2)
                        dve.wait_ge(s["probs_ready"], u + 1)
                        dve.tensor_reduce(nmax[:, (2 * q + c) % 4:(2 * q + c) % 4 + 1], S[(2 * q + c) % 4][:, 0:nk[q]],
                                          AX.X, ALU.max, negate=True).then_inc(s["max_ready"], 1)

                def combine(h, q):
                    w = 4 * h + q
                    a, b = (2 * q) % 4, (2 * q + 1) % 4
                    dve.wait_ge(s["probs_ready"], 4 + 8 * h + 2 * q + 2)
                    link(dve.reciprocal(rinv[:, a:a + 2], rsum[:, a:a + 2]))
                    link(dve.tensor_tensor(rinv[:, b:b + 1], rinv[:, b:b + 1], neg_lam[:, 0:1], ALU.mult))
                    dve.wait_ge(s["comb_turned"], w + 1)
                    link(dve.tensor_scalar(comb[:, q % 2, 0:nk[q]], prob[:, a, 0:nk[q]], rinv[:, a:a + 1], None, ALU.mult))
                    dve.scalar_tensor_tensor(comb[:, q % 2, 0:nk[q]], prob[:, b, 0:nk[q]], rinv[:, b:b + 1],
                                             comb[:, q % 2, 0:nk[q]], ALU.mult, ALU.add).then_inc(s["combined"], 1)

                def store(h, q):
                    w = 4 * h + q
                    held(dve, cr["dve"], s["pv_ready"], 2 + w + 1)
                    dve.tensor_copy(O[:, q, bass.ds(h * P, P)], OB[q % 2][:, 0:P]).then_inc(s["out_stored"], 1)

                with dve.Fori(0, HEADS) as h:
                    link.turn(2, h, TT * 3)
                    for m in range(2):
                        held(dve, cr["dve"], s["qk_turned"], 2 * h + 1)
                        dve.tensor_tensor(stage[:, m].rearrange("p t (c d) -> p t c d", d=HD),
                                          QKV[:, m, :, bass.ds(h * P, P)].rearrange("p t (c d) -> p t c d", d=HD),
                                          rstd[:, m, :, bass.ds(h * 2, 2)].unsqueeze(3).broadcast_to([P, TT, 2, HD]),
                                          ALU.mult).then_inc(s["staged"], 1)
                    unit_max(h, 0)
                    unit_max(h, 1)
                    combine(h, 0)
                    unit_max(h, 2)
                    combine(h, 1)
                    store(h, 0)
                    unit_max(h, 3)
                    combine(h, 2)
                    store(h, 1)
                    combine(h, 3)
                    store(h, 2)
                    store(h, 3)

            @block.tensor
            def _(pe):
                def scores(h, q):
                    for c in range(2):
                        u = 8 * h + 2 * q + c
                        held(pe, None, s["probs_ready"], u + 1)
                        bk = S[(2 * q + c) % 4]
                        r0 = c * HD
                        pe.matmul(bk[:, 0:nk[q]], qkT[r0:r0 + HD, 0, q * P:(q + 1) * P], qkT[r0:r0 + HD, 1, 0:nk[q]],
                                  start=True, stop=False)
                        lo = max(q - 1, 0) * P
                        pe.matmul(bk[:, lo:nk[q]], ident[:, :],
                                  biasE[:, h, (2 * P - (nk[q] - lo)):2 * P],
                                  start=False, stop=True).then_inc(s["scores_ready"], 1)

                def turn(h, q):
                    w = 4 * h + q
                    held(pe, None, s["combined"], 2 + w + 1)
                    held(pe, None, s["combT_ready"], w + 1)
                    for k in range(q + 1):
                        mm = pe.transpose(T[q % 2][:, k * P:(k + 1) * P], comb[:, q % 2, k * P:(k + 1) * P], ident[:, :])
                    mm.then_inc(s["comb_turned"], 1)

                def values(h, q):
                    w = 4 * h + q
                    held(pe, cr["pe"], s["combT_ready"], 2 + w + 1)
                    held(pe, cr["pe"], s["out_stored"], w + 1)
                    for k in range(q + 1):
                        mm = pe.matmul(OB[q % 2][:, 0:P], turned_sb[:, q % 2, k * P:(k + 1) * P],
                                       QKV[:, 2, k, bass.ds(h * P, P)], start=k == 0, stop=k == q)
                    mm.then_inc(s["pv_ready"], 1)

                with pe.Fori(0, HEADS) as h:
                    for m in range(2):
                        held(pe, cr["pe"], s["staged"], 2 * h + m + 1)
                        held(pe, cr["pe"], s["combT_ready"], 4 * h + 2)
                        for t in range(TT):
                            mm = pe.transpose(T[m][:, t * P:(t + 1) * P], stage[:, m, t, :], ident[:, :])
                        mm.then_inc(s["qk_turned"], 1)
                    held(pe, cr["pe"], s["qk_ready"], 2 * h + 2)
                    scores(h, 0)
                    scores(h, 1)
                    turn(h, 0)
                    scores(h, 2)
                    values(h, 0)
                    turn(h, 1)
                    scores(h, 3)
                    values(h, 1)
                    turn(h, 2)
                    values(h, 2)
                    turn(h, 3)
                    values(h, 3)

            @block.scalar
            def _(act):
                act.sem_inc(s["probs_ready"], 4)
                act.sem_inc(s["qk_turned"], 1)
                act.sem_inc(s["scores_ready"], 1)
                act.sem_inc(s["combined"], 2)
                act.sem_inc(s["comb_turned"], 2)
                act.sem_inc(s["combT_ready"], 2)
                act.sem_inc(s["pv_ready"], 2)
                act.sem_inc(s["out_stored"], 2)
                for m in range(2):
                    if m:
                        act.wait_ge(s["summed"], 1)
                    act.activation(sq[:, :, :], QKV[:, m], ACT.Square).then_inc(s["squared"], 1)
                act.wait_ge(s["dve_link"], 1)
                act.activation(rstd[:, :, :, :], stat[:, :, :, :], ACT.Sqrt).then_inc(s["rooted"], 1)

                def exps(h, q):
                    for c in range(2):
                        u = 8 * h + 2 * q + c
                        held(act, None, s["max_ready"], u + 1)
                        held(act, None, s["combined"], 4 * h + q + 1)
                        sl = (2 * q + c) % 4
                        act.activation(prob[:, sl, 0:nk[q]], S[sl][:, 0:nk[q]], ACT.Exp, bias=nmax[:, sl:sl + 1],
                                       accum_out=rsum[:, sl:sl + 1]).then_inc(s["probs_ready"], 1)

                def keep(h, q):
                    w = 4 * h + q
                    held(act, None, s["comb_turned"], 2 + w + 1)
                    held(act, None, s["pv_ready"], w + 1)
                    act.activation(turned_sb[:, q % 2, 0:nk[q]], T[q % 2][:, 0:nk[q]], ACT.Copy)\
                       .then_inc(s["combT_ready"], 1)

                with act.Fori(0, HEADS) as h:
                    for m, g in enumerate(("q_norm_g", "k_norm_g")):
                        held(act, None, s["qk_turned"], 2 * h + m + 2)
                        held(act, None, s["scores_ready"], 8 * h + 1)
                        act.activation(qkT[:, m, :], T[m][:, :], ACT.Copy, scale=vecT[:, VAT[g]:VAT[g] + 1])\
                           .then_inc(s["qk_ready"], 1)
                    exps(h, 0)
                    exps(h, 1)
                    keep(h, 0)
                    exps(h, 2)
                    keep(h, 1)
                    exps(h, 3)
                    keep(h, 2)
                    keep(h, 3)
    sem.over()


def attention(nc, name, sem, bank, ident, q_of, k_of, nk, mask_of, v_of, O, out_at, gate_of, row_scale, add):
    sem = PhaseSems(nc)
    with ExitStack() as st:
        def sb(n, shape):
            return st.enter_context(nc.sbuf_tensor(f"{name}_{n}", shape, F32))
        q65 = sb("q", [HD + 1, 2, SEQ])
        ones = sb("ones", [HD + 1, SEQ])
        prob = sb("prob", [P, 4, SEQ])
        kept = sb("kept", [P, 2, SEQ])
        nmax, rsum, rinv = sb("nmax", [P, 4]), sb("rsum", [P, 4]), sb("rinv", [P, 4])
        S, T, OB = bank[0:4], bank[4:6], bank[6:8]
        s = {n: sem(f"{name}_{n}") for n in ("staged", "rowed", "scores", "maxed", "probs", "turned", "kept", "pv",
                                              "stored", "link", "ones")}
        cr = {e: sem(f"{name}_carrier_{e}") for e in ("pe", "act", "dve")}
        nkt = [-(-n // P) for n in nk]
        units = [(par, q) for par in range(2) for q in range(TT)]
        rows = min(P, nk[0])
        with nc.Block() as block:
            def turns(eng, body):
                with eng.Fori(0, 2) as g:
                    with eng.Fori(0, 2) as hh:
                        body(g, 2 * g + hh)

            @block.vector
            def _(dve):
                link = Link(dve, s["link"])
                dve.memset(q65[HD:HD + 1, :, :], 1.0).then_inc(s["ones"], 1)
                dve.memset(ones[:, :], 1.0).then_inc(s["ones"], 1)

                def body(g, hp):
                    link.turn(0, hp, 2 * len(units))

                    def top(m):
                        par, q = units[m]
                        held(dve, None, s["scores"], 5 + 8 * hp + m + 1)
                        dve.wait_ge(s["probs"], 8 * hp + m + 1)
                        dve.tensor_reduce(nmax[:, m % 4:m % 4 + 1], S[m % 4][:, 0:nk[q]], AX.X, ALU.max, negate=True)\
                           .then_inc(s["maxed"], 1)

                    def scale(m):
                        par, q = units[m]
                        held(dve, None, s["probs"], 4 + 8 * hp + m + 1)
                        link(dve.reciprocal(rinv[:, m % 4:m % 4 + 1], rsum[:, m % 4:m % 4 + 1]))
                        if gate_of:
                            link(dve.tensor_tensor(rinv[:, m % 4:m % 4 + 1], rinv[:, m % 4:m % 4 + 1],
                                                   gate_of(q, 2 * hp + par), ALU.mult))
                        else:
                            link(dve.tensor_copy(rinv[:, m % 4:m % 4 + 1], rinv[:, m % 4:m % 4 + 1]))

                    def store(m):
                        par, q = units[m]
                        dst = O[:, q, bass.ds(hp * P + (out_at + par * HD), HD)]
                        held(dve, cr["dve"], s["pv"], 2 + 8 * hp + m + 1)
                        r = rinv[:, m % 4:m % 4 + 1]
                        if add:
                            ins = dve.scalar_tensor_tensor(dst, OB[m % 2][:, 0:HD], r, dst, ALU.mult, ALU.add)
                        else:
                            ins = dve.tensor_scalar(dst, OB[m % 2][:, 0:HD], r, None, ALU.mult)
                        ins.then_inc(s["stored"], 1)

                    n = len(units)
                    for m in range(n + 3):
                        if m < n:
                            top(m)
                        if 0 <= m - 1 < n:
                            scale(m - 1)
                        if 0 <= m - 3 < n:
                            store(m - 3)
                turns(dve, body)

            @block.tensor
            def _(pe):
                def body(g, hp):
                    def scores(m):
                        par, q = units[m]
                        if q == 0:
                            held(pe, None, s["staged"], 2 * hp + par + 1)
                            if row_scale:
                                held(pe, None, s["rowed"], 2 * hp + par + 1)
                        held(pe, None, s["probs"], 8 * hp + m + 1)
                        pe.matmul(S[m % 4][:, 0:nk[q]], q65[:, par, q * P:(q + 1) * P], k_of(g, hp, par, nk[q]),
                                  start=True, stop=False)
                        (lo, hi), mask = mask_of(q)
                        pe.matmul(S[m % 4][:, lo:hi], ident[:, :], mask, start=False, stop=True).then_inc(s["scores"], 1)

                    def turn(m):
                        par, q = units[m]
                        held(pe, None, s["probs"], 4 + 8 * hp + m + 1)
                        held(pe, None, s["kept"], 8 * hp + m + 1)
                        for k in range(nkt[q]):
                            mm = pe.transpose(T[m % 2][0:rows, k * P:(k + 1) * P], prob[:, m % 4, k * P:k * P + rows],
                                              ident[:, :])
                        mm.then_inc(s["turned"], 1)

                    def values(m):
                        par, q = units[m]
                        held(pe, cr["pe"], s["kept"], 2 + 8 * hp + m + 1)
                        held(pe, cr["pe"], s["stored"], 8 * hp + m + 1)
                        for k in range(nkt[q]):
                            mm = pe.matmul(OB[m % 2][:, 0:HD], kept[0:rows, m % 2, k * P:(k + 1) * P],
                                           v_of(g, hp, par, k), start=k == 0, stop=k == nkt[q] - 1)
                        mm.then_inc(s["pv"], 1)

                    n = len(units)
                    for m in range(n + 3):
                        if m < n:
                            scores(m)
                        if 0 <= m - 2 < n:
                            turn(m - 2)
                        if 0 <= m - 3 < n:
                            values(m - 3)
                pe.wait_ge(s["ones"], 2)
                turns(pe, body)

            @block.scalar
            def _(act):
                act.sem_inc(s["scores"], 5)
                act.sem_inc(s["probs"], 4)
                act.sem_inc(s["turned"], 4)
                act.sem_inc(s["kept"], 2)
                act.sem_inc(s["pv"], 2)
                act.sem_inc(s["stored"], 2)
                act.wait_ge(s["ones"], 2)

                def body(g, hp):
                    for par in range(2):
                        held(act, cr["act"], s["scores"], 8 * hp + 4 * par + 1)
                        act.activation(q65[0:HD, par, :], q_of(hp, par), ACT.Copy, scale=HD ** -0.5)\
                           .then_inc(s["staged"], 1)
                        if row_scale:
                            act.activation(q65[HD:HD + 1, par, :], ones[HD:HD + 1, :], ACT.Copy,
                                           scale=row_scale(2 * hp + par)).then_inc(s["rowed"], 1)

                    def exp(m):
                        par, q = units[m]
                        held(act, None, s["maxed"], 8 * hp + m + 1)
                        held(act, None, s["turned"], 8 * hp + m + 1)
                        act.activation(prob[:, m % 4, 0:nk[q]], S[m % 4][:, 0:nk[q]], ACT.Exp, bias=nmax[:, m % 4:m % 4 + 1],
                                       accum_out=rsum[:, m % 4:m % 4 + 1]).then_inc(s["probs"], 1)

                    def keep(m):
                        par, q = units[m]
                        held(act, None, s["turned"], 4 + 8 * hp + m + 1)
                        held(act, None, s["pv"], 8 * hp + m + 1)
                        act.activation(kept[0:rows, m % 2, 0:nkt[q] * P], T[m % 2][0:rows, 0:nkt[q] * P], ACT.Copy)\
                           .then_inc(s["kept"], 1)

                    n = len(units)
                    for m in range(n + 2):
                        if m < n:
                            exp(m)
                        if 0 <= m - 2 < n:
                            keep(m - 2)
                turns(act, body)
    sem.over()


def concatenated(ring, w, spans):
    def pieces(p, b):
        got, at = [], 0
        for lo, hi in spans[2 * p + b]:
            got.append((ring[:, b, :, at:at + hi - lo], w[:, lo:hi].rearrange("(k q) n -> q k n", q=P)))
            at += hi - lo
        return got
    return pieces


def second_cols(ring, w_in):
    return concatenated(ring, w_in, [[(0, 256), (256, 512)], [(512, 896), (1024, 1152)], [(1304, 1560), (1560, 1816)],
                                     [(1816, 2072), (2072, 2328)]])


def second_layer(nc, A, outer, sem, sb, bank, ident, vecT, x, hT, gemm, out_rows, out_written, residual, stop):
    ring = gemm.ring
    w_in = A["w_in_2"][0]

    def finish(rows):
        with nc.Block() as block:
            @block.sync
            def _(sp):
                sp.dma_start(out_rows, rows).then_inc(out_written, 16)
                sp.wait_ge(out_written, 16)

    norm_to_cols(nc, "ln1", sem, sb, bank, ident, x, VAT["ln1_2"], vecT, hT)

    with ExitStack() as st:
        def tb(name, shape, dt=F32):
            return st.enter_context(nc.sbuf_tensor(name, shape, dt))
        T4 = tb("projT", [P, 4, 4, SEQ])
        R2 = tb("proj_rows", [P, 2, TT, 512])
        NG = 2 * P + 24
        rows_pieces = concatenated(ring, w_in, [[(2328, 2584), (2584, 2840)], [(896, 1024), (1152, 1304)]])
        for half in range(2):
            each = second_cols(ring, w_in)
            pieces = lambda p, b: each(half, b)
            later = (lambda p, b: each(1, b)) if half == 0 else rows_pieces
            gemm.phase(1, pieces, cols_of(hT),
                       gemm.drain("act", (0, 2), lambda e, p, b, j, bk: e.activation(T4[:, 2 * half + b, j, :], bk[:, :], ACT.Copy)),
                       gemm.drain("dve", (1, 3), lambda e, p, b, j, bk: e.tensor_copy(T4[:, 2 * half + b, j, :], bk[:, :])),
                       following=later)
        w = (512, NG)
        gemm.phase(1, rows_pieces, rows_of(hT),
                   gemm.drain("act", (0, 2), lambda e, p, b, j, bk: e.activation(R2[:, b, j, 0:w[b]], bk[:, 0:w[b]], ACT.Copy)),
                   gemm.drain("dve", (1, 3), lambda e, p, b, j, bk: e.tensor_copy(R2[:, b, j, 0:w[b]], bk[:, 0:w[b]])),
                   following=block_pieces(ring, A["w_out_2"][0]), widths=w)

        wf = tb("w_forget", [P, KT, HEADS])
        wfh, wfl = tb("w_forget_high", [P, KT, HEADS], F32R), tb("w_forget_low", [P, KT, HEADS], F32R)
        bf = tb("b_forget", [HEADS, 1])
        fz = tb("forget", [HEADS, 6, SEQ])
        kN = tb("nsa_keys", [HD + 1, 4, SEQ])
        kF = tb("fox_keys", [HD + 1, HEADS, SEQ])
        kC = tb("cmp_keys", [HD + 1, 2, NCMP])
        vC = tb("cmp_values", [NCMP, 2, HD])
        pos_i = tb("positions_int", [1, SEQ], I32)
        pos_f = tb("positions", [1, SEQ])
        mask = tb("causal_mask", [P, P])
        cmask = tb("cmp_mask", [P, TT, NCMP])
        slopes = tb("slopes", [HD + 1, HEADS])
        valid = tb("first_rows_valid", [P, 1])
        f_loaded, f_high, f_split, f_product, f_biased, f_abs, f_exp, f_link, cum_ready, cum_moved = (
            sem("forget_" + n) for n in ("loaded", "high", "split", "product", "biased", "abs", "exp", "link", "cum_ready",
                                         "cum_moved"))

        prep = ExitStack()
        pb = lambda name, shape: prep.enter_context(nc.sbuf_tensor(name, shape, F32))
        w1 = pb("cmp_w1", [P, 2, CMP_BLOCK, P])
        w2 = pb("cmp_w2", [P, 2, HD])
        pe_rows = pb("cmp_pe", [CMP_BLOCK, 2, HD])
        peT = pb("cmp_peT", [HD, 2, CMP_BLOCK])
        hconst = pb("cmp_const", [P, 2])
        hid = pb("cmp_hidden", [P, 4, NCMP])
        names = ("w_loaded", "pool_step", "iota_done", "pos_ready", "pos_moved", "keys_copied", "gates_ready", "dve_link",
                 "pe_turned", "peT_ready", "const_product", "const_ready", "hid_product", "hid_ready", "out_product", "out_ready")
        s = {n: sem("prep_" + n) for n in names}
        with nc.Block() as block:
            @block.sync
            def _(sp):
                sp.dma_start(wf[:, :, :], w_in[:, 2840:2848].rearrange("(k q) n -> q k n", q=P)).then_inc(f_loaded, 16)
                sp.dma_start(bf[:, :], A["b_fg_2"].rearrange("l h -> h l")).then_inc(f_loaded, 16)
                for i, n in enumerate(("k", "v")):
                    src = A[f"w_cmp1_{n}_2"][0].rearrange("(l d) h -> d l h", d=HD)
                    for half in range(2):
                        sp.dma_start(w1[half * HD:(half + 1) * HD, i], src).then_inc(s["w_loaded"], 16)
                    sp.dma_start(w2[:, i, :], A[f"w_cmp2_{n}_2"][0]).then_inc(s["w_loaded"], 16)
                    sp.dma_start(pe_rows[:, i, :], A[f"pe_cmp_{n}_2"][0]).then_inc(s["w_loaded"], 16)
                sp.wait_ge(s["pos_ready"], 1)
                for i in range(4):
                    sp.dma_start(kN[HD:HD + 1, i, :], pos_f[0:1, :]).then_inc(s["pos_moved"], 16)
                ends = pos_f[0:1, CMP_BLOCK - 1:CMP_BLOCK + CMP_STRIDE * (NCMP - 1):CMP_STRIDE]
                with nc.allow_non_contiguous_dma(reason="31 positions"):
                    for g in range(2):
                        sp.dma_start(kC[HD:HD + 1, g, :], ends).then_inc(s["pos_moved"], 16)
                sp.wait_ge(cum_ready, 1)
                sp.dma_start(kF[HD:HD + 1, :, :], fz[:, 5, :]).then_inc(cum_moved, 16)
                sp.wait_ge(s["pos_moved"], 16 * 6)
                sp.wait_ge(cum_moved, 16)

            @block.gpsimd
            def _(pool):
                link = Link(pool, s["pool_step"])
                pool.iota(pos_i[:, :], pattern=[[1, SEQ]], base=0, channel_multiplier=0).then_inc(s["iota_done"], 1)
                link(pool.memset(mask[:, :], 0.0))
                link(pool.memset(cmask[:, :, :], 0.0))
                link(pool.memset(valid[:, :], 1.0))
                for h in range(HEADS):
                    link(pool.memset(slopes[:, h:h + 1], 2.0 ** (-8.0 * (h + 1) / HEADS)))
                link(pool.affine_select(out=mask[:, :], in_=mask[:, :], compare_op=ALU.is_ge, fill=NEG, base=0,
                                        pattern=[[-1, P]], channel_multiplier=1))
                for t in range(TT):
                    link(pool.affine_select(out=cmask[:, t, :], in_=cmask[:, t, :], compare_op=ALU.is_ge, fill=NEG,
                                            base=t * P - (CMP_BLOCK - 1), pattern=[[-CMP_STRIDE, NCMP]],
                                            channel_multiplier=1))
                link(pool.affine_select(out=valid[:, :], in_=valid[:, :], compare_op=ALU.is_ge, fill=0.0,
                                        base=-(CMP_BLOCK - 1), pattern=[[0, 1]], channel_multiplier=1))

            @block.tensor
            def _(pe):
                pe.wait_ge(f_split, 1)
                for k in range(KT):
                    for n, (w_, x_) in enumerate(((wfh, hT[0]), (wfh, hT[1]), (wfl, hT[0]))):
                        mm = pe.matmul(bank[0][0:HEADS, :], w_[:, k, :], x_[:, k, :], start=k == 0 and n == 0,
                                       stop=k == KT - 1 and n == 2)
                mm.then_inc(f_product, 1)
                pe.wait_ge(s["w_loaded"], 16 * 8)
                for i in range(2):
                    pe.transpose(bank[1][0:HD, i * CMP_BLOCK:(i + 1) * CMP_BLOCK], pe_rows[:, i, :],
                                 ident[0:CMP_BLOCK, 0:CMP_BLOCK]).then_inc(s["pe_turned"], 1)
                pe.wait_ge(s["peT_ready"], 1)
                for i in range(2):
                    for l in range(CMP_BLOCK):
                        mm = pe.matmul(bank[2][:, i:i + 1], w1[0:HD, i, l, :], peT[:, i, l:l + 1],
                                       start=l == 0, stop=l == CMP_BLOCK - 1)
                    mm.then_inc(s["const_product"], 1)
                for i in range(2):
                    for g in range(2):
                        lo = g * HD
                        for l in range(CMP_BLOCK):
                            mm = pe.matmul(bank[3 + 2 * i + g][:, 0:NCMP], w1[lo:lo + HD, i, l, :],
                                           T4[lo:lo + HD, 1, i, l:l + CMP_STRIDE * (NCMP - 1) + 1:CMP_STRIDE],
                                           start=l == 0, stop=l == CMP_BLOCK - 1)
                        mm.then_inc(s["hid_product"], 1)
                pe.wait_ge(s["hid_ready"], 4)
                for g in range(2):
                    pe.matmul(bank[7][0:HD, g * 64:g * 64 + NCMP], w2[:, 0, :], hid[:, g, :], start=True, stop=True)\
                      .then_inc(s["out_product"], 1)
                for g in range(2):
                    pe.matmul(bank[1][0:NCMP, 256 + g * 64:256 + (g + 1) * 64], hid[:, 2 + g, :], w2[:, 1, :],
                              start=True, stop=True).then_inc(s["out_product"], 1)

            @block.scalar
            def _(act):
                act.wait_ge(f_loaded, 32)
                act.activation(wfh[:, :, :], wf[:, :, :], ACT.Copy).then_inc(f_high, 1)
                act.wait_ge(f_abs, 1)
                act.activation(fz[:, 2, :], fz[:, 1, :], ACT.Exp).then_inc(f_exp, 1)
                for h in range(HEADS):
                    hp, par = h // 2, h % 2
                    act.activation(kF[0:HD, h, :], T4[par * HD:(par + 1) * HD, 3, hp, :], ACT.Copy)\
                       .then_inc(s["keys_copied"], 1)
                for i in range(2):
                    for g in range(2):
                        act.activation(kN[0:HD, 2 * i + g, :], T4[g * HD:(g + 1) * HD, 1, 2 + i, :], ACT.Copy)\
                           .then_inc(s["keys_copied"], 1)
                act.activation(R2[:, 1, :, 2 * P:NG], R2[:, 1, :, 2 * P:NG], ACT.Sigmoid).then_inc(s["gates_ready"], 1)
                act.wait_ge(s["const_ready"], 1)
                for i in range(4):
                    act.wait_ge(s["hid_product"], i + 1)
                    act.activation(hid[:, i, :], bank[3 + i][:, 0:NCMP], ACT.Gelu_apprx_tanh,
                                   bias=hconst[:, i // 2:i // 2 + 1]).then_inc(s["hid_ready"], 1)
                act.wait_ge(s["out_product"], 4)
                for g in range(2):
                    act.activation(kC[0:HD, g, :], bank[7][0:HD, g * 64:g * 64 + NCMP], ACT.Copy)\
                       .then_inc(s["out_ready"], 1)
                for g in range(2):
                    act.activation(vC[:, g, :], bank[1][0:NCMP, 256 + g * 64:256 + (g + 1) * 64], ACT.Copy)\
                       .then_inc(s["out_ready"], 1)

            @block.vector
            def _(dve):
                link = Link(dve, s["dve_link"])
                dve.wait_ge(f_high, 1)
                dve.tensor_tensor(wfl[:, :, :], wf[:, :, :], wfh[:, :, :].bitcast(F32), ALU.subtract).then_inc(f_split, 1)
                dve.wait_ge(s["iota_done"], 1)
                dve.tensor_copy(pos_f[:, :], pos_i[:, :]).then_inc(s["pos_ready"], 1)
                dve.wait_ge(f_product, 1)
                link(dve.tensor_scalar(fz[:, 0, :], bank[0][0:HEADS, :], bf[:, 0:1], None, ALU.add))
                link(dve.tensor_scalar(fz[:, 1, :], fz[:, 0, :], -1.0, None, ALU.mult))
                dve.tensor_tensor(fz[:, 1, :], fz[:, 1, :], fz[:, 0, :], ALU.min).then_inc(f_abs, 1)
                dve.wait_ge(f_exp, 1)
                log1p_steps(dve, link, fz[:, 5, :], fz[:, 2, :], fz[:, 3, :], fz[:, 4, :])
                link(dve.tensor_scalar(fz[:, 1, :], fz[:, 0, :], -1.0, 0.0, ALU.mult, ALU.max))
                link(dve.tensor_tensor(fz[:, 1, :], fz[:, 1, :], fz[:, 5, :], ALU.add))
                link(dve.memset(fz[:, 2, :], 1.0))
                dve.tensor_tensor_scan(fz[:, 5, :], fz[:, 2, :], fz[:, 1, :], 0.0, ALU.mult, ALU.add)\
                   .then_inc(cum_ready, 1)
                dve.wait_ge(s["pe_turned"], 2)
                dve.tensor_copy(peT[:, :, :], bank[1][0:HD, 0:2 * CMP_BLOCK].rearrange("d (i l) -> d i l", i=2))\
                   .then_inc(s["peT_ready"], 1)
                dve.wait_ge(s["const_product"], 2)
                dve.tensor_copy(hconst[:, :], bank[2][:, 0:2]).then_inc(s["const_ready"], 1)
                dve.wait_ge(s["gates_ready"], 1)
                dve.wait_ge(s["pool_step"], 3 + HEADS + 1 + TT + 1)
                dve.tensor_scalar(R2[:, 1, 0, 2 * P:NG:3], R2[:, 1, 0, 2 * P:NG:3], valid[:, 0:1], None, ALU.mult)\
                   .then_inc(s["gates_ready"], 1)

        prep.close()
        O = tb("mix_out", [P, TT, D])

        gate = lambda br: (lambda q, h: R2[:, 1, q, bass.ds(h * 3 + (2 * P + br), 1)])
        q_from = lambda i: (lambda hp, par: T4[par * HD:(par + 1) * HD, i, hp, :])
        slope = lambda h: slopes[HD:HD + 1, bass.ds(h, 1)]
        full = [(q + 1) * P for q in range(TT)]
        causal = lambda q: ((q * P, (q + 1) * P), mask[:, :])
        attention(nc, "cmp", sem, bank, ident, q_from(0), lambda g, hp, par, n: kC[:, g, 0:n], [NCMP] * TT,
                  lambda q: ((0, NCMP), cmask[:, q, :]), lambda g, hp, par, k: vC[:, g, :], O, 0, gate(0), slope, False)
        attention(nc, "sel", sem, bank, ident, q_from(0), lambda g, hp, par, n: kN[:, g, 0:n], full, causal,
                  lambda g, hp, par, k: R2[:, 1, k, bass.ds(g * HD, HD)], O, 0, gate(1), slope, True)
        attention(nc, "win", sem, bank, ident, q_from(0), lambda g, hp, par, n: kN[:, 2 + g, 0:n], full, causal,
                  lambda g, hp, par, k: R2[:, 1, k, bass.ds(g * HD + P, HD)], O, 0, gate(2), slope, True)
        attention(nc, "fox", sem, bank, ident, q_from(2), lambda g, hp, par, n: kF[:, hp * 2 + par, 0:n], full, causal,
                  lambda g, hp, par, k: R2[:, 0, k, bass.ds(hp * P + par * HD, HD)], O, 4 * P, None, None, False)

        for name, at in (("gn_nsa", 0), ("gn_fox", 4)):
            norm_to_cols(nc, name, sem, sb, bank, ident, O, VAT[name + "_2"], vecT, hT, at=at, width=4 * P, width_at=at * P)

    gemm.phase(1, block_pieces(ring, A["w_out_2"][0]), rows_of(hT), None, residual)
    if stop == "mix":
        finish(x[:, :, :])
        return
    moe(nc, A, sem, bank, ident, vecT, x, hT, ring, gemm)
    if stop == "moe":
        finish(x[:, :, :])
        return
    last_stage(nc, A, sem, sb, bank, ident, vecT, x, hT, ring, gemm, out_rows, out_written)


def moe(nc, A, sem_, bank, ident, vecT, x, hT, ring, gemm):
    outer = ExitStack()

    def ob(name, shape, dt=F32):
        return outer.enter_context(nc.sbuf_tensor(name, shape, dt))
    wt = ob("route_weights", [P, TT, TOPK])
    wtT = ob("route_weightsT", [EXPERTS, SEQ])
    slot = ob("route_slots", [P, TT * TOPK], U32)
    out_row = ob("route_out_rows", [P, TT * TOPK], U32)
    work = ob("work_experts", [1, ITEMS], I32)
    total = ob("work_total", [1, 1], I32)

    with ExitStack() as st:
        def tb(name, shape, dt=F32):
            return st.enter_context(nc.sbuf_tensor(name, shape, dt))
        rows = tb("moe_rows", [P, TT, D])
        norm_to_cols(nc, "ln2", sem_, None, bank, ident, x, VAT["ln2_2"], vecT, hT, keep=rows)
        gain = tb("ln2_wide", [P, D])
        sem = PhaseSems(nc)
        wr, br = tb("w_router", [P, KT, EXPERTS]), tb("b_router", [1, EXPERTS])
        ones, tri = tb("ones_square", [P, P]), tb("before", [P, P])
        iota_i, iota = tb("iota_int", [P, EXPERTS], I32), tb("iota", [P, EXPERTS])
        item_i, item = tb("item_int", [1, ITEMS], I32), tb("item", [1, ITEMS])
        tok, zero = tb("token_ids", [P, TT], I32), tb("zero_slots", [P, ITEMS + 1], I32)
        lg, top = tb("logits", [P, TT, EXPERTS]), tb("top_values", [P, TT, 8])
        top_i, top_f = tb("top_index", [P, TT, 8], U32), tb("top_index_float", [P, TT, 8])
        stat = tb("route_stat", [P, 3, TT])
        eq = tb("pick_onehot", [P, TT, TOPK, EXPERTS])
        tmp = tb("pick_tmp", [P, TT, TOPK, EXPERTS])
        chosen, dense = tb("chosen", [P, TT, EXPERTS]), tb("dense_weights", [P, TT, EXPERTS])
        place = tb("places", [P, TT, EXPERTS])
        picks = tb("pick_rows", [P, TT, TOPK])
        line = tb("expert_line", [P, 4, EXPERTS])
        grid = tb("work_grid", [1, ITEMS, EXPERTS])
        found = tb("work_found", [1, ITEMS])
        bu = tb("b_up_rows", [EXPERTS, 2 * D])
        br1, br2 = tb("b_up_rest", [EXPERTS, 2 * D]), tb("b_up_rest2", [EXPERTS, 2 * D])
        parts = tb("b_up_parts", [EXPERTS, 3, 2 * D], BF16)
        names = ("loaded", "bias_loaded", "gain_loaded", "gained", "h2_written", "zero_ready", "zeroed", "pool_link", "iotas", "logits_ready", "dve_link",
                 "tops_negated", "exps_ready", "chosen_ready", "places_ready", "slots_ready", "scattered", "parts_ready",
                 "parts_written", "weights_turned")
        s = {n: sem("route_" + n) for n in names}
        with nc.Block() as block:
            @block.sync
            def _(sp):
                sp.dma_start(wr[:, :, :], A["w_router_2"][0].rearrange("(k q) e -> q k e", q=P)).then_inc(s["loaded"], 16)
                sp.dma_start(br[:, :], A["b_router_2"]).then_inc(s["loaded"], 16)
                sp.dma_start(bu[:, :], A["b_up_2"][0]).then_inc(s["bias_loaded"], 16)
                sp.dma_start(gain[:, :], A["ln2_row"].broadcast_to([P, D])).then_inc(s["gain_loaded"], 16)
                sp.wait_ge(s["gained"], TT)
                sp.dma_start(A["h2_scratch"].rearrange("(t p) d -> p t d", p=P), rows[:, :, :]).then_inc(s["h2_written"], 16)
                sp.wait_ge(s["zero_ready"], 1)
                sp.dma_start(A["slot_tokens"].rearrange("(p c) o -> p (c o)", p=P), zero[:, :]).then_inc(s["zeroed"], 16)
                sp.wait_ge(s["parts_ready"], 1)
                sp.dma_start(A["bias_parts"], parts[:, :, :]).then_inc(s["parts_written"], 16)
                sp.wait_ge(s["parts_written"], 16)
                sp.wait_ge(s["h2_written"], 16)

            @block.gpsimd
            def _(pool):
                pool.memset(zero[:, :], 0).then_inc(s["zero_ready"], 1)
                link = Link(pool, s["pool_link"])
                link(pool.memset(ones[:, :], 1.0))
                link(pool.memset(tri[:, :], 1.0))
                link(pool.affine_select(out=tri[:, :], in_=tri[:, :], compare_op=ALU.is_gt, fill=0.0, base=0,
                                        pattern=[[1, P]], channel_multiplier=-1))
                link(pool.iota(iota_i[:, :], pattern=[[1, EXPERTS]], base=0, channel_multiplier=0))
                link(pool.iota(item_i[:, :], pattern=[[1, ITEMS]], base=0, channel_multiplier=0))
                link(pool.iota(tok[:, :], pattern=[[P, TT]], base=0, channel_multiplier=1))
                pool.wait_ge(s["slots_ready"], 1)
                pool.wait_ge(s["zeroed"], 16)
                for t in range(TT):
                    for k in range(TOPK):
                        j = t * TOPK + k
                        pool.indirect_dma_start(A["slot_tokens"], bass.IndirectOffsetOnAxis(ap=slot[:, j:j + 1], axis=0),
                                                tok[:, t:t + 1], None).then_inc(s["scattered"], 16)
                pool.wait_ge(s["scattered"], 16 * TT * TOPK)

            @block.tensor
            def _(pe):
                pe.wait_ge(s["loaded"], 32)
                pe.wait_ge(s["pool_link"], 3)
                for t in range(TT):
                    for k in range(KT):
                        for part in range(2):
                            pe.matmul(bank[t][:, 0:EXPERTS], hT[part][:, k, t * P:(t + 1) * P].bitcast(F32), wr[:, k, :],
                                      start=k == 0 and part == 0, stop=False)
                    pe.matmul(bank[t][:, 0:EXPERTS], ones[0:1, :], br[:, :], start=False, stop=True)\
                      .then_inc(s["logits_ready"], 1)
                pe.wait_ge(s["chosen_ready"], 1)
                for t in range(TT):
                    for u in range(t):
                        pe.matmul(bank[4][:, t * EXPERTS:(t + 1) * EXPERTS], ones[:, :], chosen[:, u, :], start=u == 0, stop=False)
                    pe.matmul(bank[4][:, t * EXPERTS:(t + 1) * EXPERTS], tri[:, :], chosen[:, t, :], start=t == 0, stop=True)
                for u in range(TT):
                    mm = pe.matmul(bank[5][:, 0:EXPERTS], ones[:, :], chosen[:, u, :], start=u == 0, stop=u == TT - 1)
                mm.then_inc(s["places_ready"], 1)
                for t in range(TT):
                    mm = pe.transpose(bank[6][0:EXPERTS, t * P:(t + 1) * P], dense[:, t, :], ident[:, :])
                mm.then_inc(s["weights_turned"], 1)

            @block.scalar
            def _(act):
                act.wait_ge(s["tops_negated"], 1)
                for t in range(TT):
                    act.activation(wt[:, t, :], top[:, t, 0:TOPK], ACT.Exp, bias=stat[:, 0, t:t + 1],
                                   accum_out=stat[:, 1, t:t + 1]).then_inc(s["exps_ready"], 1)

            @block.vector
            def _(dve):
                link = Link(dve, s["dve_link"])
                dve.wait_ge(s["bias_loaded"], 16)
                dve.wait_ge(s["gain_loaded"], 16)
                for t in range(TT):
                    dve.tensor_tensor(rows[:, t, :], rows[:, t, :], gain[:, :], ALU.mult).then_inc(s["gained"], 1)
                link(dve.tensor_copy(parts[:, 0, :], bu[:, :]))
                link(dve.tensor_tensor(br1[:, :], bu[:, :], parts[:, 0, :], ALU.subtract))
                link(dve.tensor_copy(parts[:, 1, :], br1[:, :]))
                link(dve.tensor_tensor(br2[:, :], br1[:, :], parts[:, 1, :], ALU.subtract))
                dve.tensor_copy(parts[:, 2, :], br2[:, :]).then_inc(s["parts_ready"], 1)
                dve.wait_ge(s["pool_link"], 6)
                link(dve.tensor_copy(iota[:, :], iota_i[:, :]))
                link(dve.tensor_copy(item[:, :], item_i[:, :]))
                for t in range(TT):
                    dve.wait_ge(s["logits_ready"], t + 1)
                    link(dve.tensor_copy(lg[:, t, :], bank[t][:, 0:EXPERTS]))
                    link(dve.max(top[:, t, :], lg[:, t, :]))
                    link(dve.max_index(top_i[:, t, :], top[:, t, :], lg[:, t, :]))
                dve.tensor_scalar(stat[:, 0, :], top[:, :, 0], -1.0, None, ALU.mult).then_inc(s["tops_negated"], 1)
                link(dve.tensor_copy(top_f[:, :, :], top_i[:, :, :]))
                for t in range(TT):
                    link(dve.tensor_tensor(eq[:, t], iota[:, :].unsqueeze(1).broadcast_to([P, TOPK, EXPERTS]),
                                           top_f[:, t, 0:TOPK].unsqueeze(2).broadcast_to([P, TOPK, EXPERTS]), ALU.is_equal))
                link(dve.tensor_reduce(chosen[:, :, :], eq[:, :, :, :].rearrange("p t k e -> p t e k"), AX.X, ALU.add))
                dve.wait_ge(s["exps_ready"], TT)
                link(dve.reciprocal(stat[:, 2, :], stat[:, 1, :]))
                link(dve.tensor_tensor(wt[:, :, :], wt[:, :, :], stat[:, 2, :].unsqueeze(2).broadcast_to([P, TT, TOPK]), ALU.mult))
                for t in range(TT):
                    link(dve.tensor_tensor(tmp[:, t], eq[:, t], wt[:, t, :].unsqueeze(2).broadcast_to([P, TOPK, EXPERTS]), ALU.mult))
                dve.tensor_reduce(dense[:, :, :], tmp[:, :, :, :].rearrange("p t k e -> p t e k"), AX.X, ALU.add)\
                   .then_inc(s["chosen_ready"], 1)
                dve.wait_ge(s["chosen_ready"], 1)
                dve.wait_ge(s["places_ready"], 1)
                link(dve.tensor_copy(line[:, 0, :], bank[5][:, 0:EXPERTS]))
                link(dve.tensor_scalar(line[:, 1, :], line[:, 0, :], 0.0, None, ALU.is_gt))
                for j in range(1, SEQ // P):
                    link(dve.scalar_tensor_tensor(line[:, 1, :], line[:, 0, :], float(j * P), line[:, 1, :], ALU.is_gt, ALU.add))
                link(dve.memset(line[:, 3, :], 1.0))
                link(dve.tensor_tensor_scan(line[:, 2, :], line[:, 3, :], line[:, 1, :], 0.0, ALU.mult, ALU.add))
                link(dve.tensor_tensor(line[:, 3, :], line[:, 2, :], line[:, 1, :], ALU.subtract))
                link(dve.tensor_copy(place[:, :, :], bank[4][:, 0:TT * EXPERTS].rearrange("p (t e) -> p t e", t=TT)))
                link(dve.scalar_tensor_tensor(place[:, :, :], line[:, 3, :].unsqueeze(1).broadcast_to([P, TT, EXPERTS]), float(P),
                                              place[:, :, :], ALU.mult, ALU.add))
                for t in range(TT):
                    link(dve.tensor_tensor(tmp[:, t], eq[:, t], place[:, t, :].unsqueeze(1).broadcast_to([P, TOPK, EXPERTS]), ALU.mult))
                link(dve.tensor_reduce(picks[:, :, :], tmp[:, :, :, :], AX.X, ALU.add))
                dve.tensor_copy(slot[:, :], picks[:, :, :].rearrange("p t k -> p (t k)")).then_inc(s["slots_ready"], 1)
                link(dve.tensor_scalar(out_row[:, :], picks[:, :, :].rearrange("p t k -> p (t k)"), float(P), None, ALU.add))
                link(dve.tensor_tensor(grid[:, :, :], line[0:1, 2, :].unsqueeze(1).broadcast_to([1, ITEMS, EXPERTS]),
                                       item[:, :].unsqueeze(2).broadcast_to([1, ITEMS, EXPERTS]), ALU.is_le))
                link(dve.tensor_reduce(found[:, :], grid[:, :, :], AX.X, ALU.add))
                link(dve.tensor_scalar(work[:, :], found[:, :], float(EXPERTS - 1), None, ALU.min))
                link(dve.tensor_copy(total[:, :], line[0:1, 2, EXPERTS - 1:EXPERTS]))
                dve.wait_ge(s["weights_turned"], 1)
                link(dve.tensor_copy(wtT[:, :], bank[6][0:EXPERTS, :]))
        sem.over()

    with ExitStack() as st:
        def tb(name, shape, dt=F32):
            return st.enter_context(nc.sbuf_tensor(name, shape, dt))
        UNITS, RAW, SPLIT = 12, 6, 4
        ring4 = ring[:, :, :, :].rearrange("p a k n -> p (a k n)").rearrange("p (r n) -> p r n", r=4)
        raw2 = tb("raw_units", [P, 2, 2048])
        raw = [ring4[:, r, :] for r in range(4)] + [raw2[:, r, :] for r in range(2)]
        uh, ul = tb("unit_high", [P, SPLIT, 2048], F32R), tb("unit_low", [P, SPLIT, 2048], F32R)
        index = tb("item_tokens", [P, 1], I32)
        xg = tb("gathered", [P, D])
        xh, xl, ah, al = (hT[n % 2][:, :, (n // 2) * P:(n // 2 + 1) * P] for n in range(4))
        biasb, ones3 = tb("bias_row_parts", [3, 2 * D], BF16), tb("ones_three", [3, P], BF16)
        gs, sg, ls = tb("gate_part", [P, D]), tb("gate_sigmoid", [P, D]), tb("linear_part", [P, D])
        at, y = tb("activated", [P, D]), tb("expert_rows", [P, D])
        zero_rows = tb("zero_rows", [P, D])
        sem = PhaseSems(nc)
        raw_loaded = [sem(f"raw_loaded{r}") for r in range(RAW)]
        names = ("ones", "index_loaded", "gathered", "xg_turned", "xg_high", "xg_ready", "bias_loaded", "up_ready",
                 "high_ready", "split_ready", "unit_used", "gate_ready", "sigmoid_ready", "act_ready", "act_turned",
                 "act_high", "actT_ready", "y_kept", "y_written", "dve_link", "counted")
        s = {n: sem("moe_" + n) for n in names}
        carrier = sem("moe_carrier_pool")
        w_up = A["w_up_2"][0].rearrange("e k n -> (e k) n")
        w_down = A["w_down_2"][0].rearrange("e k n -> (e k) n")
        bias_rows = A["bias_parts"].rearrange("e a n -> (e a) n")
        four = lambda bk: bk[:, :].rearrange("p (k t) -> p k t", k=4)
        with nc.Block() as block:
            def items(eng, body, skipped=None):
                n = eng.value_load(total[0:1, 0:1], min_val=1, max_val=ITEMS)
                with eng.Fori(0, ITEMS) as i:
                    with eng.If(i < n):
                        body(i)
                    if skipped:
                        with eng.Else():
                            skipped(i)
                    eng.nop()
                return n

            @block.sync
            def _(sp):
                def body(i):
                    e = sp.value_load(work[0:1, bass.ds(i, 1)], min_val=0, max_val=EXPERTS - 1)
                    for u in range(UNITS):
                        held(sp, None, s["split_ready"], UNITS * i + u + 1)
                        dst = raw[u % RAW].rearrange("p (k n) -> p k n", k=2)
                        if u < 8:
                            c, j = u // 4, u % 4
                            src = w_up[bass.ds(e * D + j * 2 * P, 2 * P), :].rearrange("(k q) (s n) -> q k s n", q=P, s=2)
                            for k in range(2):
                                sp.dma_start(dst[:, k, :].rearrange("p (s n) -> p s n", s=2),
                                             src[:, k, :, c * 512:(c + 1) * 512]).then_inc(raw_loaded[u % RAW], 16)
                        else:
                            src = w_down[bass.ds(e * D + (u - 8) * 2 * P, 2 * P), :].rearrange("(k q) n -> q k n", q=P)
                            for k in range(2):
                                sp.dma_start(dst[:, k, :], src[:, k, :]).then_inc(raw_loaded[u % RAW], 16)
                        if u == 0:
                            held(sp, None, s["up_ready"], 2 * i + 1)
                            sp.dma_start(biasb[:, :], bias_rows[bass.ds(e * 3, 3), :]).then_inc(s["bias_loaded"], 16)
                sp.wait_ge(s["counted"], 2)
                items(sp, body)

            @block.gpsimd
            def _(pool):
                for name, n in (("split_ready", RAW), ("unit_used", SPLIT), ("up_ready", 1), ("act_ready", 2),
                                ("y_kept", 1), ("y_written", 16)):
                    pool.sem_inc(s[name], n)
                pool.sem_inc(s["counted"], 1)

                def gather(i):
                    pool.dma_start(index[:, :], A["slot_tokens"][bass.ds(i * P, P), :]).then_inc(s["index_loaded"], 16)
                    held(pool, carrier, s["index_loaded"], 16 * i + 16)
                    pool.indirect_dma_start(xg[:, :], None, A["h2_scratch"],
                                            bass.IndirectOffsetOnAxis(ap=index[:, 0:1], axis=0)).then_inc(s["gathered"], 16)

                def body(i):
                    held(pool, carrier, s["xg_turned"], i + 1)
                    gather(i + 1)
                gather(0)
                items(pool, body)

            @block.tensor
            def _(pe):
                def three(bk, xs, k, ws, first, last):
                    (h, l), (wh, wl) = xs, ws
                    pe.matmul(bk, h[:, k, :], wh, start=first, stop=False)
                    pe.matmul(bk, h[:, k, :], wl, start=False, stop=False)
                    return pe.matmul(bk, l[:, k, :], wh, start=False, stop=last)

                def turn_rows(i):
                    held(pe, None, s["gathered"], 16 * i + 16)
                    for k in range(KT):
                        mm = pe.transpose(bank[k // 4][:, (k % 4) * P:(k % 4 + 1) * P], xg[:, k * P:(k + 1) * P], ident[:, :])
                    mm.then_inc(s["xg_turned"], 1)

                def turn_act(i, c):
                    held(pe, None, s["act_ready"], 2 + 2 * i + c + 1)
                    for k in range(4):
                        mm = pe.transpose(bank[4 + c][:, k * P:(k + 1) * P], at[:, (4 * c + k) * P:(4 * c + k + 1) * P], ident[:, :])
                    mm.then_inc(s["act_turned"], 1)

                def unit(i, u):
                    held(pe, None, s["split_ready"], RAW + UNITS * i + u + 1)
                    for k in range(2):
                        for h in range(2):
                            at_ = slice(k * 1024 + h * 512, k * 1024 + (h + 1) * 512)
                            ws = (uh[:, u % SPLIT, at_], ul[:, u % SPLIT, at_])
                            if u < 8:
                                c, kk = u // 4, 2 * (u % 4) + k
                                mm = three(bank[2 * c + h][:, :], (xh, xl), kk, ws, kk == 0, False)
                            else:
                                kk = 2 * (u - 8) + k
                                mm = three(bank[6 + h][:, :], (ah, al), kk, ws, kk == 0, kk == KT - 1)
                    mm.then_inc(s["unit_used"], 1)

                def bias(c):
                    for h in range(2):
                        mm = pe.matmul(bank[2 * c + h][:, :], ones3[:, :], biasb[:, h * D + c * 512:h * D + (c + 1) * 512],
                                       start=False, stop=True)
                    mm.then_inc(s["up_ready"], 1)

                def body(i):
                    held(pe, None, s["xg_ready"], 2 * i + 2)
                    for u in range(4):
                        unit(i, u)
                    held(pe, None, s["bias_loaded"], 16 * i + 16)
                    bias(0)
                    held(pe, None, s["act_ready"], 2 * i + 2)
                    for u in range(4, 7):
                        unit(i, u)
                    turn_act(i, 0)
                    unit(i, 7)
                    bias(1)
                    held(pe, None, s["actT_ready"], 2 * i + 1)
                    held(pe, None, s["y_kept"], 2 * i + 1)
                    unit(i, 8)
                    unit(i, 9)
                    turn_act(i, 1)
                    turn_rows(i + 1)
                    held(pe, None, s["actT_ready"], 2 * i + 2)
                    unit(i, 10)
                    unit(i, 11)
                pe.wait_ge(s["ones"], 1)
                pe.wait_ge(s["counted"], 2)
                turn_rows(0)
                items(pe, body)

            @block.vector
            def _(dve):
                dve.memset(ones3[:, :], 1.0).then_inc(s["ones"], 1)
                dve.memset(zero_rows[:, :], 0.0).then_inc(s["counted"], 1)
                link = Link(dve, s["dve_link"])

                def low(i, u):
                    held(dve, None, s["high_ready"], UNITS * i + u + 1)
                    dve.tensor_tensor(ul[:, u % SPLIT, :], raw[u % RAW], uh[:, u % SPLIT, :].bitcast(F32), ALU.subtract)\
                       .then_inc(s["split_ready"], 1)

                def rows_low(i):
                    for c in range(2):
                        held(dve, None, s["xg_high"], 2 * i + c + 1)
                        dve.tensor_tensor(xl[:, 4 * c:4 * c + 4, :], four(bank[c]), xh[:, 4 * c:4 * c + 4, :].bitcast(F32),
                                          ALU.subtract).then_inc(s["xg_ready"], 1)

                def act_low(i, c):
                    held(dve, None, s["act_high"], 2 * i + c + 1)
                    dve.tensor_tensor(al[:, 4 * c:4 * c + 4, :], four(bank[4 + c]), ah[:, 4 * c:4 * c + 4, :].bitcast(F32),
                                      ALU.subtract).then_inc(s["actT_ready"], 1)

                def swiglu(i, c):
                    cols = slice(c * 512, (c + 1) * 512)
                    held(dve, None, s["up_ready"], 1 + 2 * i + c + 1)
                    dve.tensor_scalar(gs[:, cols], bank[2 * c][:, :], 7.0, None, ALU.min).then_inc(s["gate_ready"], 1)
                    link(dve.tensor_scalar(ls[:, cols], bank[2 * c + 1][:, :], 7.0, -7.0, ALU.min, ALU.max))
                    link(dve.scalar_tensor_tensor(ls[:, cols], ls[:, cols], 1.0, gs[:, cols], ALU.add, ALU.mult))
                    held(dve, None, s["sigmoid_ready"], 2 * i + c + 1)
                    dve.tensor_tensor(at[:, cols], ls[:, cols], sg[:, cols], ALU.mult).then_inc(s["act_ready"], 1)

                def body(i):
                    link.turn(0, i, 4)
                    for u in range(8):
                        low(i, u)
                    swiglu(i, 0)
                    for u in range(8, 11):
                        low(i, u)
                    act_low(i, 0)
                    swiglu(i, 1)
                    low(i, 11)
                    act_low(i, 1)
                    rows_low(i + 1)
                dve.wait_ge(s["counted"], 2)
                rows_low(0)
                items(dve, body)

            @block.scalar
            def _(act):
                def high(i, u):
                    r = u % RAW
                    held(act, None, raw_loaded[r], 64 * i + 32 * (u // RAW) + 32)
                    held(act, None, s["unit_used"], UNITS * i + u + 1)
                    act.activation(uh[:, u % SPLIT, :], raw[r], ACT.Copy).then_inc(s["high_ready"], 1)

                def rows_high(i):
                    held(act, None, s["xg_turned"], i + 1)
                    for c in range(2):
                        act.activation(xh[:, 4 * c:4 * c + 4, :], four(bank[c]), ACT.Copy).then_inc(s["xg_high"], 1)

                def act_high(i, c):
                    held(act, None, s["act_turned"], 2 * i + c + 1)
                    act.activation(ah[:, 4 * c:4 * c + 4, :], four(bank[4 + c]), ACT.Copy).then_inc(s["act_high"], 1)

                def sigmoid(i, c):
                    cols = slice(c * 512, (c + 1) * 512)
                    held(act, None, s["gate_ready"], 2 * i + c + 1)
                    act.activation(sg[:, cols], gs[:, cols], ACT.Sigmoid, scale=1.702).then_inc(s["sigmoid_ready"], 1)

                def keep_rows(i):
                    held(act, None, s["unit_used"], SPLIT + UNITS * i)
                    held(act, None, s["y_written"], 16 * i + 16)
                    for n in range(2):
                        act.activation(y[:, n * 512:(n + 1) * 512], bank[6 + n][:, :], ACT.Copy).then_inc(s["y_kept"], 1)
                    held(act, None, s["y_kept"], 1 + 2 * i + 2)
                    act.dma_start(A["expert_out"][bass.ds(i * P, P), :], y[:, :]).then_inc(s["y_written"], 16)

                def body(i):
                    for u in range(4):
                        high(i, u)
                    keep_rows(i)
                    for u in range(4, 8):
                        high(i, u)
                    sigmoid(i, 0)
                    for u in range(8, 11):
                        high(i, u)
                    act_high(i, 0)
                    high(i, 11)
                    sigmoid(i, 1)
                    act_high(i, 1)
                    rows_high(i + 1)

                def skipped(i):
                    act.dma_start(A["expert_out"][bass.ds(i * P + P, P), :], zero_rows[:, :]).then_inc(s["y_written"], 16)
                act.wait_ge(s["counted"], 2)
                for n in range(2):
                    act.activation(bank[6 + n][:, :], zero_rows[:, 0:512], ACT.Copy).then_inc(s["ones"], 1)
                act.wait_ge(s["ones"], 3)
                rows_high(0)
                n = items(act, body, skipped)
                held(act, None, s["unit_used"], n * UNITS + SPLIT)
                act.wait_ge(s["y_written"], ITEMS * 16 + 16)
                for h in range(2):
                    act.activation(y[:, h * 512:(h + 1) * 512], bank[6 + h][:, :], ACT.Copy).then_inc(s["y_kept"], 1)
                held(act, None, s["y_kept"], n * 2 + 3)
                act.dma_start(A["expert_out"][bass.ds(n * P, P), :], y[:, :]).then_inc(s["y_written"], 16)
                act.wait_ge(s["y_written"], ITEMS * 16 + 32)
        sem.over()

    with ExitStack() as st:
        def tb(name, shape, dt=F32):
            return st.enter_context(nc.sbuf_tensor(name, shape, dt))
        back = tb("picked_rows", [P, 4, D])
        bd = tb("b_down", [EXPERTS, D])
        sem = PhaseSems(nc)
        b_loaded, b_product, link_sem, added = (sem("combine_" + n) for n in ("b_loaded", "b_product", "link", "added"))
        fetched = [sem(f"combine_fetched{i}") for i in range(4)]
        with nc.Block() as block:
            @block.sync
            def _(sp):
                sp.dma_start(bd[:, :], A["b_down_2"][0]).then_inc(b_loaded, 16)

            @block.gpsimd
            def _(pool):
                for t in range(TT):
                    for k in range(TOPK):
                        j = t * TOPK + k
                        if j >= 4:
                            pool.wait_ge(added, j - 3)
                        pool.indirect_dma_start(back[:, j % 4, :], None, A["expert_out"],
                                                bass.IndirectOffsetOnAxis(ap=out_row[:, j:j + 1], axis=0))\
                            .then_inc(fetched[j % 4], 16)

            @block.tensor
            def _(pe):
                pe.wait_ge(b_loaded, 16)
                for t in range(TT):
                    for n in range(2):
                        pe.matmul(bank[2 * t + n][:, :], wtT[:, t * P:(t + 1) * P], bd[:, n * 512:(n + 1) * 512],
                                  start=True, stop=True).then_inc(b_product, 1)

            @block.vector
            def _(dve):
                link = Link(dve, link_sem)
                for t in range(TT):
                    for n in range(2):
                        dve.wait_ge(b_product, 2 * t + n + 1)
                        link(dve.tensor_tensor(x[:, t, n * 512:(n + 1) * 512], bank[2 * t + n][:, :],
                                               x[:, t, n * 512:(n + 1) * 512], ALU.add))
                for t in range(TT):
                    for k in range(TOPK):
                        j = t * TOPK + k
                        dve.wait_ge(fetched[j % 4], 16 * (j // 4 + 1))
                        dve.scalar_tensor_tensor(x[:, t, :], back[:, j % 4, :], wt[:, t, k:k + 1], x[:, t, :],
                                                 ALU.mult, ALU.add).then_inc(added, 1)
                        dve.wait_ge(added, j + 1)
        sem.over()
    outer.close()


def last_stage(nc, A, sem, sb, bank, ident, vecT, x, hT, ring, gemm, out_rows, out_written):
    norm_to_cols(nc, "ple", sem, sb, bank, ident, x, VAT["ln_ple_2"], vecT, hT)
    with ExitStack() as st:
        def tb(name, shape, dt=F32):
            return st.enter_context(nc.sbuf_tensor(name, shape, dt))
        PD = 256
        sg = tb("ple_gate", [P, TT, D])
        gemm.phase(1, block_pieces(ring, A["w_ple_gate_2"][0]), rows_of(hT),
                   gemm.drain("act", range(4), lambda eng, p, b, j, bk: eng.activation(sg[:, j, b * 512:(b + 1) * 512], bk[:, :],
                                                                                       ACT.Sigmoid)))
        pr, pT, wp = tb("ple_input", [P, TT, PD]), tb("ple_T", [P, PD // P, SEQ]), tb("w_ple", [P, PD // P, D])
        gf = tb("ln_f", [P, D])
        tmp, stat = tb("ple_tmp", [P, 2, D]), tb("final_stat", [P, 3, TT])
        s = {n: sem("last_" + n) for n in ("loaded", "turned", "kept", "product", "gated", "link", "squared", "rooted", "scaled")}
        with nc.Block() as block:
            @block.sync
            def _(sp):
                sp.dma_start(pr[:, :, :], A["p_2"][0, 0].rearrange("(t q) d -> q t d", q=P)).then_inc(s["loaded"], 16)
                sp.dma_start(wp[:, :, :], A["w_ple_2"][0].rearrange("(k q) n -> q k n", q=P)).then_inc(s["loaded"], 16)
                sp.dma_start(gf[:, :], A["ln_f_2"].unsqueeze(0).broadcast_to([P, D])).then_inc(s["loaded"], 16)
                for t in range(TT):
                    sp.wait_ge(s["scaled"], t + 1)
                    sp.dma_start(out_rows[:, t, :], x[:, t, :]).then_inc(out_written, 16)
                sp.wait_ge(out_written, 16 * TT)

            @block.tensor
            def _(pe):
                pe.wait_ge(s["loaded"], 48)
                for k in range(PD // P):
                    for t in range(TT):
                        mm = pe.transpose(bank[k][:, t * P:(t + 1) * P], pr[:, t, k * P:(k + 1) * P], ident[:, :])
                    mm.then_inc(s["turned"], 1)
                pe.wait_ge(s["kept"], 2)
                for t in range(TT):
                    for n in range(2):
                        for k in range(PD // P):
                            mm = pe.matmul(bank[2 * t + n][:, :], pT[:, k, t * P:(t + 1) * P], wp[:, k, n * 512:(n + 1) * 512],
                                           start=k == 0, stop=k == PD // P - 1)
                        mm.then_inc(s["product"], 1)

            @block.scalar
            def _(act):
                for k in range(2):
                    act.wait_ge(s["turned"], k + 1)
                    act.activation(pT[:, k, :], bank[k][:, :], ACT.Copy).then_inc(s["kept"], 1)
                for t in range(TT):
                    act.wait_ge(s["link"], 4 * t + 4)
                    if t:
                        act.wait_ge(s["squared"], t)
                    act.activation(sg[:, 0, :], x[:, t, :], ACT.Square, accum_out=stat[:, 0, t:t + 1]).then_inc(s["squared"], 1)
                act.wait_ge(s["link"], 4 * TT + 1)
                act.activation(stat[:, 2, :], stat[:, 1, :], ACT.Sqrt).then_inc(s["rooted"], 1)

            @block.vector
            def _(dve):
                link = Link(dve, s["link"])
                for t in range(TT):
                    for n in range(2):
                        dve.wait_ge(s["product"], 2 * t + n + 1)
                        cols = slice(n * 512, (n + 1) * 512)
                        link(dve.tensor_tensor(tmp[:, 0, cols], bank[2 * t + n][:, :], sg[:, t, cols], ALU.mult))
                        link(dve.tensor_tensor(x[:, t, cols], x[:, t, cols], tmp[:, 0, cols], ALU.add))
                dve.wait_ge(s["squared"], TT)
                link(dve.tensor_scalar(stat[:, 1, :], stat[:, 0, :], 1.0 / D, EPS, ALU.mult, ALU.add))
                dve.wait_ge(s["rooted"], 1)
                link(dve.reciprocal(stat[:, 0, :], stat[:, 2, :]))
                for t in range(TT):
                    dve.scalar_tensor_tensor(x[:, t, :], x[:, t, :], stat[:, 0, t:t + 1], gf[:, :], ALU.mult, ALU.mult)\
                       .then_inc(s["scaled"], 1)


def bias_columns():
    import numpy as np
    m = np.zeros((BUCKETS + 1, SHEAR), np.float32)
    half = BUCKETS // 2
    for c in range(SHEAR):
        n = 2 * P - 1 - c
        if n < 0:
            m[BUCKETS, c] = NEG
            continue
        b = n if n < half else min(half + int(math.log(max(n, 1) / half) / math.log(128 / half) * (BUCKETS - half)), BUCKETS - 1)
        m[b, c] += 1.0
        m[BUCKETS - 1, c] -= 1.0
    return m


def build(nc, A, out, stop=None):
    outer = ExitStack()
    with outer:
        def sem(name):
            return outer.enter_context(nc.semaphore(name))

        def sb(name, shape, dt=F32):
            return outer.enter_context(nc.sbuf_tensor(name, shape, dt))

        bank = [outer.enter_context(nc.psum_tensor(f"bank{i}", [P, 512], F32)) for i in range(8)]
        out_rows = out[0].rearrange("(t p) d -> p t d", p=P)

        ident = sb("ident", [P, P])
        vecT = sb("vecT", [P, NVEC])
        x = sb("x_rows", [P, TT, D])
        hT = (sb("hT_high", [P, KT, SEQ], F32R), sb("hT_low", [P, KT, SEQ], F32R))
        gemm = Gemm(nc, sem, sb, bank)
        ring = gemm.ring
        out_written = sem("out_written")

        def finish(rows):
            with nc.Block() as block:
                @block.sync
                def _(sp):
                    sp.dma_start(out_rows, rows).then_inc(out_written, 16)
                    sp.wait_ge(out_written, 16)

        first = ExitStack()
        rnnT = first.enter_context(nc.sbuf_tensor("rnnT", [P, KT, SEQ], F32))
        biasE = first.enter_context(nc.sbuf_tensor("biasE", [P, HEADS, 2 * P], F32))
        neg_lam = first.enter_context(nc.sbuf_tensor("neg_lam", [P, 1], F32))

        w_in = A["w_in"][0]
        QKW = 3 * D
        recurrent = block_pieces(ring, w_in, col0=QKW)

        with ExitStack() as st:
            vec = st.enter_context(nc.sbuf_tensor("vec", [NVEC, P], F32))
            lv = st.enter_context(nc.sbuf_tensor("lambda_vectors", [P, 4, HD], F32))
            lp = st.enter_context(nc.sbuf_tensor("lambda_products", [P, 2, HD], F32))
            ls = st.enter_context(nc.sbuf_tensor("lambda_sums", [P, 4], F32))
            rb = st.enter_context(nc.sbuf_tensor("rel_bias", [BUCKETS + 1, HEADS], F32))
            rbb = st.enter_context(nc.sbuf_tensor("rel_bias_wide", [BUCKETS + 1, HEADS, P], F32))
            cols = st.enter_context(nc.sbuf_tensor("bias_columns", [BUCKETS + 1, SHEAR], F32))
            rep = st.enter_context(nc.sbuf_tensor("bias_rows", [P, HEADS, SHEAR], F32))
            zeroed, ident_ready, vec_loaded, x_loaded, lam_loaded, bias_loaded, ones_ready = (
                sem(n) for n in ("zeroed", "ident_ready", "vec_loaded", "x_loaded", "lam_loaded", "bias_loaded", "ones_ready"))
            vec_turned, wide_ready, rows_product, rows_ready, sheared, lam_summed, lam_exp, dve_link, bias_ready = (
                sem("setup_" + n) for n in ("vec_turned", "wide_ready", "rows_product", "rows_ready", "sheared",
                                            "lam_summed", "lam_exp", "dve_link", "bias_ready"))
            flat = A["bias_scratch"]
            nvec_dma = len(VECS) + 4
            with nc.Block() as block:
                @block.sync
                def _(sp):
                    for name, k in VECS:
                        r = VAT[name]
                        sp.dma_start(vec[r:r + k, :], A[name]).then_inc(vec_loaded, 16)
                    for name in ("q_norm_g", "k_norm_g"):
                        for half in range(2):
                            sp.dma_start(vec[VAT[name]:VAT[name] + 1, half * HD:(half + 1) * HD], A[name])\
                              .then_inc(vec_loaded, 16)
                    sp.dma_start(x[:, :, :], A["x"][0].rearrange("(t p) d -> p t d", p=P)).then_inc(x_loaded, 16)
                    for i, n in enumerate(("lambda_q1", "lambda_k1", "lambda_q2", "lambda_k2")):
                        sp.dma_start(lv[:, i, :], A[n].broadcast_to([P, HD])).then_inc(lam_loaded, 16)
                    gemm.load_ahead(sp, recurrent)
                    sp.wait_ge(ones_ready, 1)
                    sp.dma_start(rb[0:BUCKETS, :], A["rel_bias"]).then_inc(bias_loaded, 16)
                    sp.dma_start(cols[:, :], A["bias_columns"]).then_inc(bias_loaded, 16)
                    sp.wait_ge(rows_ready, HEADS)
                    sp.dma_start(flat.rearrange("(h p m) -> p h m", h=HEADS, p=P), rep[:, :, :]).then_inc(sheared, 16)
                    sp.wait_ge(sheared, 16)
                    for h in range(HEADS):
                        at = h * P * SHEAR + P - 1
                        sp.dma_start(biasE[:, h, :], flat[at:at + P * (SHEAR - 1)]
                                     .rearrange("(p m) -> p m", p=P)[:, 0:2 * P]).then_inc(bias_ready, 16)
                    sp.wait_ge(bias_ready, 16 * HEADS)
                    sp.wait_ge(x_loaded, 16)

                @block.gpsimd
                def _(pool):
                    pool.memset(ident[:, :], 0.0).then_inc(zeroed, 1)
                    pool.wait_ge(zeroed, 1)
                    pool.affine_select(out=ident[:, :], in_=ident[:, :], compare_op=ALU.not_equal, fill=1.0, base=0,
                                       pattern=[[-1, P]], channel_multiplier=1).then_inc(ident_ready, 1)

                @block.vector
                def _(dve):
                    link = Link(dve, dve_link)
                    link(dve.memset(rbb[:, :, :], 1.0))
                    dve.memset(rb[:, :], 1.0).then_inc(ones_ready, 1)
                    dve.wait_ge(bias_loaded, 32)
                    for h in range(HEADS):
                        link(dve.tensor_scalar(rbb[:, h, :], rbb[:, h, :], rb[:, h:h + 1], None, ALU.mult))
                    dve.wait_ge(vec_turned, 1)
                    link(dve.tensor_copy(vecT[:, :], bank[0][:, 0:NVEC]))
                    link(dve.tensor_scalar(vecT[:, VAT["k_norm_g"]:VAT["k_norm_g"] + 1],
                                           vecT[:, VAT["k_norm_g"]:VAT["k_norm_g"] + 1], HD ** -0.5, None, ALU.mult))
                    link(dve.tensor_scalar(vecT[:, VAT["subln_g"]:VAT["subln_g"] + 1],
                                           vecT[:, VAT["subln_g"]:VAT["subln_g"] + 1], 1.0 - 0.2, None, ALU.mult))
                    dve.wait_ge(lam_loaded, 64)
                    link(dve.tensor_tensor(lp[:, :, :], lv[:, 0:4:2, :], lv[:, 1:4:2, :], ALU.mult))
                    dve.tensor_reduce(ls[:, 0:2], lp[:, :, :], AX.X, ALU.add).then_inc(lam_summed, 1)
                    dve.wait_ge(lam_exp, 1)
                    dve.scalar_tensor_tensor(neg_lam[:, :], ls[:, 3:4], -0.2, ls[:, 2:3], ALU.add, ALU.subtract)\
                       .then_inc(dve_link, 1)

                @block.scalar
                def _(act):
                    act.wait_ge(lam_summed, 1)
                    act.activation(ls[:, 2:4], ls[:, 0:2], ACT.Exp).then_inc(lam_exp, 1)
                    for h in range(HEADS):
                        act.wait_ge(rows_product, h + 1)
                        act.activation(rep[:, h, :], bank[(h + 1) % 8][:, 0:SHEAR], ACT.Copy).then_inc(rows_ready, 1)

                @block.tensor
                def _(pe):
                    pe.wait_ge(ident_ready, 1)
                    pe.wait_ge(vec_loaded, 16 * nvec_dma)
                    pe.transpose(bank[0][:, 0:NVEC], vec[:, :], ident[0:NVEC, 0:NVEC]).then_inc(vec_turned, 1)
                    pe.wait_ge(dve_link, 1 + HEADS + 1)
                    for h in range(HEADS):
                        pe.matmul(bank[(h + 1) % 8][:, 0:SHEAR], rbb[:, h, :], cols[:, :], start=True, stop=True)\
                          .then_inc(rows_product, 1)

        norm_to_cols(nc, "mix", sem, sb, bank, ident, x, VAT["norm_mix_g"], vecT, hT)

        gemm.ahead = True

        def copies(dst):
            return (gemm.drain("act", (0, 2), lambda eng, p, b, j, bk: eng.activation(dst(p, b, j), bk[:, :], ACT.Copy)),
                    gemm.drain("dve", (1, 3), lambda eng, p, b, j, bk: eng.tensor_copy(dst(p, b, j), bk[:, :])))
        residual = gemm.drain("dve", range(4), lambda eng, p, b, j, bk: eng.tensor_tensor(
            x[:, j, b * 512:(b + 1) * 512], bk[:, :], x[:, j, b * 512:(b + 1) * 512], ALU.add))

        with ExitStack() as st:
            XG = st.enter_context(nc.sbuf_tensor("XG", [P, 2, KT, SEQ], F32))
            gemm.phase(2, recurrent, cols_of(hT), *copies(lambda p, b, j: XG[:, p, 4 * b + j, :]),
                       following=block_pieces(ring, w_in))
            lru(nc, sem, bank, vecT, XG, A["w_rg_a"][0], A["w_rg_x"][0], rnnT)

        O = first.enter_context(nc.sbuf_tensor("diff_out", [P, TT, D], F32))
        with ExitStack() as st:
            QKV = st.enter_context(nc.sbuf_tensor("QKV", [P, 3, TT, D], F32))
            gates_in = block_pieces(ring, w_in, col0=QKW + 2 * D)
            gemm.phase(3, block_pieces(ring, w_in), rows_of(hT), *copies(lambda p, b, j: QKV[:, p, j, b * 512:(b + 1) * 512]),
                       following=gates_in)
            diff_attention(nc, sem, bank, ident, vecT, QKV, biasE, neg_lam, O)
        mixT = tuple(first.enter_context(nc.sbuf_tensor(n, [P, KT, SEQ], F32R)) for n in ("mixT_high", "mixT_low"))
        with ExitStack() as st:
            sq = st.enter_context(nc.sbuf_tensor("subln_sq", [P, TT, D], F32))
            ss = st.enter_context(nc.sbuf_tensor("subln_stat", [P, TT * HEADS], F32))
            s1, s2, s3, s4 = (sem("subln_" + n) for n in ("squared", "dve_link", "rooted", "normed"))
            grouped = lambda t: t[:, :, :].rearrange("p t (h d) -> p (t h) d", d=P)
            with nc.Block() as block:
                @block.scalar
                def _(act):
                    act.activation(sq[:, :, :], O[:, :, :], ACT.Square).then_inc(s1, 1)
                    act.wait_ge(s2, 2)
                    act.activation(ss[:, :], ss[:, :], ACT.Sqrt).then_inc(s3, 1)

                @block.vector
                def _(dve):
                    link = Link(dve, s2)
                    dve.wait_ge(s1, 1)
                    link(dve.tensor_reduce(ss[:, :], grouped(sq), AX.X, ALU.add))
                    link(dve.tensor_scalar(ss[:, :], ss[:, :], 1.0 / P, EPS, ALU.mult, ALU.add))
                    dve.wait_ge(s3, 1)
                    link(dve.reciprocal(ss[:, :], ss[:, :]))
                    dve.tensor_tensor(grouped(O), grouped(O), ss[:, :].unsqueeze(2).broadcast_to([P, TT * HEADS, P]),
                                      ALU.mult).then_inc(s4, 1)
            transpose_rows(nc, "attn_out", sem, bank, ident, O, KT, mixT, vecT[:, VAT["subln_g"]:VAT["subln_g"] + 1])

        GA = O[:, :, :].rearrange("p t d -> p (t d)").rearrange("p (k s) -> p k s", k=KT)
        with ExitStack() as st:
            GR = st.enter_context(nc.sbuf_tensor("rnn_gateT", [P, KT, SEQ], F32))
            merged = sem("merged")
            both = (GA, GR)
            for p, G in enumerate(both):
                sigmoid = gemm.drain("act", range(4), lambda eng, p, b, j, bk: eng.activation(G[:, 4 * b + j, :], bk[:, :],
                                                                                            ACT.Sigmoid))
                gemm.phase(1, block_pieces(ring, w_in, col0=QKW + 2 * D + p * D), cols_of(hT), sigmoid, None,
                           following=block_pieces(ring, w_in, col0=QKW + 3 * D) if p == 0 else
                           block_pieces(ring, A["w_proj_attn"][0]))
            gated = gemm.drain("dve", range(4), lambda eng, p, b, j, bk: eng.tensor_tensor(
                GA[:, 4 * b + j, :], bk[:, :], GA[:, 4 * b + j, :], ALU.mult))
            gemm.phase(1, block_pieces(ring, A["w_proj_attn"][0]), cols_of(mixT), None, gated,
                       following=block_pieces(ring, A["w_proj_rnn"][0]))
            split_cols(nc, "rnn", sem, rnnT, mixT)

            def gate_and_add(eng, p, b):
                for j in range(4):
                    n = 4 * b + j
                    eng.wait_ge(gemm.product, 4 * (2 * gemm.done + b) + j + 1)
                    eng.tensor_tensor(GR[:, n, :], bank[n][:, :], GR[:, n, :], ALU.mult).then_inc(gemm.drained[j], 1)
                    eng.wait_ge(gemm.drained[j], 2 * gemm.done + b + 1)
                    eng.tensor_tensor(GA[:, n, :], GA[:, n, :], GR[:, n, :], ALU.add).then_inc(merged, 1)
            gemm.phase(1, block_pieces(ring, A["w_proj_rnn"][0]), cols_of(mixT), None, gate_and_add,
                       following=block_pieces(ring, A["w_out"][0]))
            split_cols(nc, "merge", sem, GA, mixT)
            gemm.phase(1, block_pieces(ring, A["w_out"][0]), rows_of(mixT), None, residual,
                       following=block_pieces(ring, A["w_up"][0]))
        first.close()

        norm_to_cols(nc, "mlp", sem, sb, bank, ident, x, VAT["norm_mlp_g"], vecT, hT)
        with ExitStack() as st:
            HALF = FF // 2
            pairs = HALF // 1024
            upT = tuple(st.enter_context(nc.sbuf_tensor(n, [P, HALF // P, SEQ], F32R)) for n in ("upT_high", "upT_low"))
            act_in = st.enter_context(nc.sbuf_tensor("up_squares", [P, 4, SEQ], F32))
            squared, high_done, low_done = (sem("up_" + n) for n in ("squared", "high_done", "low_done"))

            def down_pieces(half):
                def pieces(p, b):
                    src = A["w_down"][0][bass.ds(p * D + half * HALF, D), b * 512:(b + 1) * 512]\
                        .rearrange("(k q) n -> q k n", q=P)
                    return [(ring[:, b, 0:4, :], src[:, 0:4, :]), (ring[:, b, 4:8, :], src[:, 4:8, :])]
                return pieces
            for half in range(2):
                up_pieces = lambda h: block_pieces(ring, A["w_up"][0], col0=h * HALF)
                n_of = lambda p, b: 4 * (2 * (p + half * pairs) + b)

                def act_drain(act, p, b):
                    for j in range(4):
                        held(act, None, gemm.product, 4 * (2 * (p + gemm.done) + b) + j + 1)
                        if not isinstance(p, int) or n_of(p, b):
                            held(act, None, low_done, n_of(p, b) - 3 + j)
                        act.activation(act_in[:, j, :], bank[4 * b + j][:, :], ACT.Relu).then_inc(gemm.drained[j], 1)
                    for j in range(4):
                        held(act, gemm.carrier["act"], squared, n_of(p, b) + j + 1)
                        act.activation(upT[0][:, p * 8 + (4 * b + j), :], act_in[:, j, :], ACT.Copy).then_inc(high_done, 1)

                def dve_drain(dve, p, b):
                    for j in range(4):
                        held(dve, None, gemm.drained[j], 2 * (p + gemm.done) + b + 1)
                        dve.tensor_tensor(act_in[:, j, :], act_in[:, j, :], act_in[:, j, :], ALU.mult).then_inc(squared, 1)
                    for j in range(4):
                        held(dve, gemm.carrier["dve"], high_done, n_of(p, b) + j + 1)
                        dve.tensor_tensor(upT[1][:, p * 8 + (4 * b + j), :], act_in[:, j, :],
                                          upT[0][:, p * 8 + (4 * b + j), :].bitcast(F32), ALU.subtract).then_inc(low_done, 1)
                gemm.phase(pairs, up_pieces(half), cols_of(hT), act_drain, dve_drain, following=down_pieces(half))
                down = lambda p: (lambda w, part, j, k: (upT[part][:, 8 * p + k, j * P:(j + 1) * P], w))
                gemm.phase(pairs, down_pieces(half), down, None, residual, accumulate=True,
                           following=up_pieces(1) if half == 0 else second_cols(ring, A["w_in_2"][0]))
        if stop == "first":
            finish(x[:, :, :])
            return
        second_layer(nc, A, outer, sem, sb, bank, ident, vecT, x, hT, gemm, out_rows, out_written, residual, stop)


_OUT_SHAPE = (1, SEQ, D)
_VECTOR = {n for n, _ in VECS}


def kernel(**inputs):
    import numpy as np
    import concourse.bacc as bacc
    from concourse.bass_utils import run_bass_kernel_spmd

    nc = bacc.Bacc("TRN2", target_bir_lowering=False, num_devices=1)
    arrays, A = {}, {}
    inputs = dict(inputs)
    inputs["bias_columns"] = bias_columns()
    for name, value in inputs.items():
        a = np.ascontiguousarray(value)
        if name in _VECTOR:
            a = a.reshape(-1, P)
        arrays[f"in_{name}"] = a
        A[name] = nc.dram_tensor(f"in_{name}", a.shape, mybir.dt.from_np(a.dtype), kind="ExternalInput").ap()
    A["bias_scratch"] = nc.dram_tensor("bias_scratch", (HEADS * P * SHEAR,), F32, kind="Internal").ap()
    A["h2_scratch"] = nc.dram_tensor("h2_scratch", (SEQ, D), F32, kind="Internal").ap()
    A["slot_tokens"] = nc.dram_tensor("slot_tokens", ((ITEMS + 1) * P, 1), I32, kind="Internal").ap()
    A["expert_out"] = nc.dram_tensor("expert_out", ((ITEMS + 1) * P, D), F32, kind="Internal").ap()
    A["bias_parts"] = nc.dram_tensor("bias_parts", (EXPERTS, 3, 2 * D), BF16, kind="Internal").ap()
    out = nc.dram_tensor("out_rows", _OUT_SHAPE, F32, kind="ExternalOutput").ap()
    A["ln2_row"] = A["ln2_2"].rearrange("k p -> (k p)").unsqueeze(0)
    build(nc, A, out, STOP)
    r = run_bass_kernel_spmd(nc, [arrays], core_ids=[0])
    return r.results[0]["out_rows"]


STOP = None
```

```python
import math
from contextlib import ExitStack

import concourse.bass as bass
from concourse import mybir

F32 = mybir.dt.float32
BF16 = mybir.dt.bfloat16
F32R = mybir.dt.float32r
I32 = mybir.dt.int32
U32 = mybir.dt.uint32
ALU = mybir.AluOpType
ACT = mybir.ActivationFunctionType
AX = mybir.AxisListType

P = 128
SEQ = 512
TT = SEQ // P
D = 1024
KT = D // P
HEADS = 8
BUCKETS = 32
FF = 4096
EXPERTS = 32
TOPK = 4
EPS = 1e-6
NEG = -1e30
CMP_STRIDE = 16
CMP_BLOCK = 32
NCMP = (SEQ - CMP_BLOCK) // CMP_STRIDE + 1
HD = 64
SHEAR = 384
ITEMS = SEQ * TOPK // P + EXPERTS - 1

VECS = [("norm_mix_g", 8), ("norm_mlp_g", 8), ("conv_w", 32), ("conv_b", 8), ("b_rg_a", 8), ("b_rg_x", 8),
        ("lru_lambda", 8), ("ln1_2", 8), ("ln2_2", 8), ("ln_ple_2", 8), ("gn_nsa_2", 4), ("gn_fox_2", 4),
        ("subln_g", 1)]
VAT = {}
_r = 0
for _n, _k in VECS:
    VAT[_n] = _r
    _r += _k
VAT["q_norm_g"], VAT["k_norm_g"] = _r, _r + 1
NVEC = _r + 2


class Link:

    def __init__(self, eng, sem, base=0):
        self.eng, self.sem, self.base, self.n = eng, sem, base, 0

    def __call__(self, ins):
        ins.then_inc(self.sem, 1)
        self.n += 1
        self.eng.wait_ge(self.sem, self.base + self.n)
        return self

    def turn(self, base, i, per):
        self.base, self.n = base + i * per, 0


def held(eng, carrier, sem, value):
    eng.wait_ge(sem, value)
    if carrier is not None and not isinstance(value, int):
        eng.sem_inc(carrier, 1)


class PhaseSems:

    def __init__(self, nc):
        self.nc, self.all = nc, []

    def __call__(self, name):
        self.all.append(self.nc.alloc_semaphore(name=name))
        return self.all[-1]

    def over(self):
        self.nc.clear_and_free_semaphores(self.all)
        self.nc.all_engine_barrier()


class Gemm:

    def __init__(self, nc, sem, sb, ps):
        self.nc = nc
        self.loaded = [sem("weights_loaded0"), sem("weights_loaded1")]
        self.high_ready, self.split_ready = sem("weights_high"), sem("weights_split")
        self.half_used = sem("weights_half_used")
        self.product = sem("product_ready")
        self.drained = [sem(f"bank_drained{j}") for j in range(4)]
        self.carrier = {e: sem(f"carrier_{e}") for e in ("sp", "pe", "act", "dve", "pool")}
        self.ring = sb("weight_ring", [P, 2, 8, 512])
        self.bank = ps
        self.done = 0
        self.ahead = False

    def loads(self, sp, p, pair, pieces):
        for b in range(2):
            if not isinstance(pair, int) or pair > 0:
                held(sp, None, self.split_ready, 4 * (pair - 1) + 2 * b + 2)
            for dst, src in pieces(p, b):
                sp.dma_start(dst, src).then_inc(self.loaded[b], 16)

    def load_ahead(self, sp, pieces, pairs=0):
        self.loads(sp, 0, self.done + pairs, pieces)

    def sp(self, sp, pairs, pieces, following, unrolled):
        if not self.ahead:
            self.loads(sp, 0, self.done, pieces)
        if unrolled:
            for p in range(1, pairs):
                self.loads(sp, p, p + self.done, pieces)
        elif pairs > 1:
            with sp.Fori(1, pairs) as p:
                self.loads(sp, p, p + self.done, pieces)
        if following:
            self.load_ahead(sp, following, pairs)

    def pe_block(self, pe, pair, b, operands, start=True, stop=True, width=512):
        for h in range(2):
            held(pe, None, self.split_ready, 4 * pair + 2 * b + h + 1)
            for j in range(4):
                if h == 0 and start and (not isinstance(pair, int) or pair > 0):
                    held(pe, None, self.drained[j], 2 * (pair - 1) + b + 1)
                for k in range(4 * h, 4 * h + 4):
                    for n, (wp, xp) in enumerate(((0, 0), (0, 1), (1, 0))):
                        lhsT, rhs = operands((self.high, self.low)[wp][:, h, k % 4, 0:width], xp, j, k)
                        mm = pe.matmul(self.bank[4 * b + j][:, 0:width], lhsT, rhs,
                                       start=start and k == 0 and n == 0, stop=stop and k == 7 and n == 2)
                if h == 1:
                    mm.then_inc(self.product, 1)
            if h == 0:
                mm.then_inc(self.half_used, 1)

    def split(self, eng, who, pair, b, width=512):
        n = 2 * pair + b
        for h in range(2):
            raw = self.ring[:, b, 4 * h:4 * h + 4, 0:width]
            if who == "act":
                held(eng, None, self.loaded[b], 32 * (pair + 1))
                if not isinstance(n, int) or n > 0:
                    held(eng, None, *((self.half_used, n) if h == 0 else (self.product, 4 * n)))
                eng.activation(self.high[:, h, :, 0:width], raw, ACT.Copy).then_inc(self.high_ready, 1)
            else:
                held(eng, None, self.high_ready, 2 * n + h + 1)
                eng.tensor_tensor(self.low[:, h, :, 0:width], raw, self.high[:, h, :, 0:width].bitcast(F32), ALU.subtract)\
                   .then_inc(self.split_ready, 1)

    def follow(self, eng, who, pairs, drain, width, unrolled):
        split = lambda p, b: self.split(eng, who, p + self.done, b, width(p, b))

        def turn(p):
            split(p, 1)
            drain(eng, p, 0)
            split(p + 1, 0)
            drain(eng, p, 1)
        split(0, 0)
        if unrolled:
            for p in range(pairs - 1):
                turn(p)
        elif pairs > 1:
            with eng.Fori(0, pairs - 1) as p:
                turn(p)
        split(pairs - 1, 1)
        drain(eng, pairs - 1, 0)
        drain(eng, pairs - 1, 1)

    def drain(self, who, js, evac):
        def one(eng, p, b):
            for j in js:
                held(eng, self.carrier[who], self.product, 4 * (2 * (p + self.done) + b) + j + 1)
                evac(eng, p, b, j, self.bank[4 * b + j]).then_inc(self.drained[j], 1)
        return one

    def phase(self, pairs, pieces, operands, act_drain=None, dve_drain=None, following=None, unrolled=False,
              width=lambda p, b: 512, spans=lambda p: (True, True), before=None):
        nothing = lambda eng, p, b: None
        with self.nc.sbuf_tensor(f"split_high{self.done}", [P, 2, 4, 512], F32R) as self.high, \
                self.nc.sbuf_tensor(f"split_low{self.done}", [P, 2, 4, 512], F32R) as self.low:
            with self.nc.Block() as block:
                @block.sync
                def _(sp):
                    self.sp(sp, pairs, pieces, following, unrolled)

                @block.tensor
                def _(pe):
                    if unrolled:
                        for p in range(pairs):
                            if before:
                                before(pe, p)
                            for b in range(2):
                                self.pe_block(pe, p + self.done, b, operands(p), *spans(p), width=width(p, b))
                    else:
                        for b in range(2):
                            self.pe_block(pe, self.done, b, operands)
                        if pairs > 1:
                            with pe.Fori(1, pairs) as p:
                                for b in range(2):
                                    self.pe_block(pe, p + self.done, b, operands)

                @block.scalar
                def _(act):
                    self.follow(act, "act", pairs, act_drain or nothing, width, unrolled)

                @block.vector
                def _(dve):
                    self.follow(dve, "dve", pairs, dve_drain or nothing, width, unrolled)
        self.done += pairs
        self.ahead = following is not None


def cols_of(xT):
    return lambda w, part, j, k: (w[:, j * P:(j + 1) * P], xT[part][:, k, :])


def rows_of(xT):
    return lambda w, part, j, k: (xT[part][:, k, j * P:(j + 1) * P], w)


def block_pieces(ring, w, col0=0, row0=0):
    def pieces(p, b):
        src = w[row0:row0 + D, bass.ds(p * 1024 + (col0 + b * 512), 512)].rearrange("(k q) n -> q k n", q=P)
        return [(ring[:, b, 0:4, :], src[:, 0:4, :]), (ring[:, b, 4:8, :], src[:, 4:8, :])]
    return pieces


def norm_to_cols(nc, name, sem, sb, bank, ident, x, g_at, vecT, hT, at=0, width=D, width_at=0, keep=None,
                 meanwhile=None):
    kt = width // P
    with ExitStack() as st:
        sq = st.enter_context(nc.sbuf_tensor(name + "_sq", [P, width], F32))
        rows = keep if keep is not None else st.enter_context(nc.sbuf_tensor(name + "_rows", [P, TT, width], F32))
        stat = st.enter_context(nc.sbuf_tensor(name + "_stat", [P, 4, TT], F32))
        act_link, dve_link, rooted, scaled, turned, high_ready, low_ready = (
            sem(f"{name}_{s}") for s in ("act_link", "dve_link", "rooted", "scaled", "turned", "high_ready", "low_ready"))
        with nc.Block() as block:
            if meanwhile:
                @block.sync
                def _(sp):
                    meanwhile(sp)

            @block.scalar
            def _(act):
                link = Link(act, act_link)
                for t in range(TT):
                    link(act.activation(sq[:, :], x[:, t, width_at:width_at + width], ACT.Square,
                                        accum_out=stat[:, 0, t:t + 1]))
                act.wait_ge(dve_link, 1)
                act.activation(stat[:, 2, :], stat[:, 1, :], ACT.Sqrt).then_inc(rooted, 1)
                for j in range(kt):
                    act.wait_ge(turned, j + 1)
                    act.activation(hT[0][:, at + j, :], bank[j % 8][:, :], ACT.Copy,
                                   scale=vecT[:, g_at + j:g_at + j + 1]).then_inc(high_ready, 1)

            @block.vector
            def _(dve):
                link = Link(dve, dve_link)
                dve.wait_ge(act_link, TT)
                link(dve.tensor_scalar(stat[:, 1, :], stat[:, 0, :], 1.0 / width, EPS, ALU.mult, ALU.add))
                dve.wait_ge(rooted, 1)
                link(dve.reciprocal(stat[:, 3, :], stat[:, 2, :]))
                for t in range(TT):
                    dve.tensor_scalar(rows[:, t, 0:width], x[:, t, width_at:width_at + width], stat[:, 3, t:t + 1],
                                      None, ALU.mult).then_inc(scaled, 1)
                for j in range(kt):
                    dve.wait_ge(high_ready, j + 1)
                    dve.scalar_tensor_tensor(hT[1][:, at + j, :], bank[j % 8][:, :], vecT[:, g_at + j:g_at + j + 1],
                                             hT[0][:, at + j, :].bitcast(F32), ALU.mult, ALU.subtract).then_inc(low_ready, 1)

            @block.tensor
            def _(pe):
                pe.wait_ge(scaled, TT)
                for j in range(kt):
                    for t in range(TT):
                        mm = pe.transpose(bank[j % 8][:, t * P:(t + 1) * P], rows[:, t, j * P:(j + 1) * P], ident[:, :])
                    mm.then_inc(turned, 1)


def log1p_steps(dve, link, out, e, s, s2):
    link(dve.tensor_scalar(s2, e, 2.0, None, ALU.add))
    link(dve.reciprocal(s, s2))
    link(dve.tensor_tensor(s, s, e, ALU.mult))
    link(dve.tensor_tensor(s2, s, s, ALU.mult))
    link(dve.tensor_scalar(out, s2, 1.0 / 17, None, ALU.mult))
    for k in range(7, 0, -1):
        link(dve.scalar_tensor_tensor(out, out, 1.0 / (2 * k + 1), s2, ALU.add, ALU.mult))
    link(dve.scalar_tensor_tensor(out, out, 1.0, s, ALU.add, ALU.mult))
    link(dve.tensor_scalar(out, out, 2.0, None, ALU.mult))


def transpose_rows(nc, name, sem, bank, ident, x, tiles, outT, scale):
    turned, high_ready, low_ready = sem(name + "_turned"), sem(name + "_high"), sem(name + "_low")
    with nc.Block() as block:
        @block.tensor
        def _(pe):
            for j in range(tiles):
                for t in range(TT):
                    mm = pe.transpose(bank[j][:, t * P:(t + 1) * P], x[:, t, j * P:(j + 1) * P], ident[:, :])
                mm.then_inc(turned, 1)

        @block.scalar
        def _(act):
            for j in range(tiles):
                act.wait_ge(turned, j + 1)
                act.activation(outT[0][:, j, :], bank[j][:, :], ACT.Copy, scale=scale).then_inc(high_ready, 1)

        @block.vector
        def _(dve):
            for j in range(tiles):
                dve.wait_ge(high_ready, j + 1)
                dve.scalar_tensor_tensor(outT[1][:, j, :], bank[j][:, :], scale, outT[0][:, j, :].bitcast(F32),
                                         ALU.mult, ALU.subtract).then_inc(low_ready, 1)


def split_cols(nc, name, sem, xT, outT):
    high_ready, low_ready = sem(name + "_high"), sem(name + "_low")
    with nc.Block() as block:
        @block.scalar
        def _(act):
            for j in range(KT):
                act.activation(outT[0][:, j, :], xT[:, j, :], ACT.Copy).then_inc(high_ready, 1)

        @block.vector
        def _(dve):
            for j in range(KT):
                dve.wait_ge(high_ready, j + 1)
                dve.tensor_tensor(outT[1][:, j, :], xT[:, j, :], outT[0][:, j, :].bitcast(F32), ALU.subtract)\
                   .then_inc(low_ready, 1)


def lru(nc, sem, bank, vecT, XG, w_a_dram, w_x_dram, rnnT):
    sem = PhaseSems(nc)
    with ExitStack() as st:
        def sb(name, shape):
            return st.enter_context(nc.sbuf_tensor(name, shape, F32))
        wa, wx = sb("lru_wa", [P, KT, P]), sb("lru_wx", [P, KT, P])
        xc, r, i = sb("lru_xc", [P, KT, SEQ]), sb("lru_r", [P, KT, SEQ]), sb("lru_i", [P, KT, SEQ])
        sp_t = sb("lru_softplus", [P, 5, KT])
        xr, gr, a = XG[:, 0], XG[:, 1], XG[:, 0]
        names = ("weights", "abs", "exp", "softplus", "convolved", "gate_product", "gate_ready", "input_gated",
                 "decay_ready", "tanh_ready", "one_minus", "rooted", "scaled", "scanned", "gelu", "out", "act_link", "dve_link")
        s = {n: sem("lru_" + n) for n in names}
        lam = vecT[:, VAT["lru_lambda"]:VAT["lru_lambda"] + KT]
        with nc.Block() as block:
            @block.sync
            def _(sp):
                sp.dma_start(wa[:, :, :], w_a_dram.rearrange("n e f -> e n f")).then_inc(s["weights"], 16)
                sp.dma_start(wx[:, :, :], w_x_dram.rearrange("n e f -> e n f")).then_inc(s["weights"], 16)

            @block.vector
            def _(dve):
                link = Link(dve, s["dve_link"])
                link(dve.tensor_scalar(sp_t[:, 0, :], lam, -1.0, None, ALU.mult))
                dve.tensor_tensor(sp_t[:, 0, :], sp_t[:, 0, :], lam, ALU.min).then_inc(s["abs"], 1)
                dve.wait_ge(s["exp"], 1)
                log1p_steps(dve, link, sp_t[:, 2, :], sp_t[:, 1, :], sp_t[:, 3, :], sp_t[:, 4, :])
                link(dve.tensor_scalar(sp_t[:, 3, :], lam, -1.0, 0.0, ALU.mult, ALU.max))
                link(dve.tensor_tensor(sp_t[:, 2, :], sp_t[:, 2, :], sp_t[:, 3, :], ALU.add))
                link(dve.tensor_scalar(sp_t[:, 2, :], sp_t[:, 2, :], 8.0, None, ALU.mult))
                dve.tensor_scalar(sp_t[:, 3, :], sp_t[:, 2, :], -1.0, None, ALU.mult).then_inc(s["softplus"], 1)

                def gate_input(n):
                    dve.wait_ge(s["convolved"], n + 1)
                    dve.wait_ge(s["gate_ready"], 2 * n + 2)
                    link(dve.tensor_tensor(i[:, n, :], i[:, n, :], xc[:, n, :], ALU.mult))
                for n in range(KT):
                    w = lambda tap: vecT[:, VAT["conv_w"] + tap * KT + n:VAT["conv_w"] + tap * KT + n + 1]
                    link(dve.tensor_scalar(xc[:, n, :], xr[:, n, :], w(3),
                                           vecT[:, VAT["conv_b"] + n:VAT["conv_b"] + n + 1], ALU.mult, ALU.add))
                    for tap in (2, 1, 0):
                        back = 3 - tap
                        last = dve.scalar_tensor_tensor(xc[:, n, back:], xr[:, n, 0:SEQ - back], w(tap),
                                                        xc[:, n, back:], ALU.mult, ALU.add)
                        if tap:
                            link(last)
                    last.then_inc(s["convolved"], 1)
                    if n >= 2:
                        gate_input(n - 2)
                gate_input(KT - 2)
                gate_input(KT - 1)
                dve.wait_ge(s["decay_ready"], KT)
                link(dve.tensor_tensor(xc[:, :, :], a, a, ALU.mult))
                dve.wait_ge(s["tanh_ready"], KT)
                dve.scalar_tensor_tensor(r[:, :, :].rearrange("p n t -> p (n t)"),
                                         xc[:, :, :].rearrange("p n t -> p (n t)"), 1.0,
                                         r[:, :, :].rearrange("p n t -> p (n t)"),
                                         ALU.add, ALU.mult).then_inc(s["one_minus"], 1)
                dve.wait_ge(s["rooted"], 1)
                link(dve.tensor_tensor(i[:, :, :], i[:, :, :], r[:, :, :], ALU.mult))
                for n in range(KT):
                    link(dve.tensor_tensor_scan(xc[:, n, :], a[:, n, :], i[:, n, :], 0.0, ALU.mult, ALU.add))
                dve.wait_ge(s["gelu"], 1)
                dve.tensor_tensor(rnnT[:, :, :], xc[:, :, :], gr, ALU.mult).then_inc(s["out"], 1)

            @block.tensor
            def _(pe):
                pe.wait_ge(s["weights"], 32)
                for n in range(KT):
                    pe.wait_ge(s["convolved"], n + 1)
                    if n >= 4:
                        pe.wait_ge(s["gate_ready"], 2 * (n - 3))
                    pe.matmul(bank[2 * (n % 4)][:, :], wa[:, n, :], xc[:, n, :], start=True, stop=True)\
                      .then_inc(s["gate_product"], 1)
                    pe.matmul(bank[2 * (n % 4) + 1][:, :], wx[:, n, :], xc[:, n, :], start=True, stop=True)\
                      .then_inc(s["gate_product"], 1)

            @block.scalar
            def _(act):
                act.wait_ge(s["abs"], 1)
                act.activation(sp_t[:, 1, :], sp_t[:, 0, :], ACT.Exp).then_inc(s["exp"], 1)
                act.activation(gr, gr, ACT.Gelu_apprx_tanh).then_inc(s["gelu"], 1)
                for n in range(KT):
                    for m, (dst, b) in enumerate(((r, "b_rg_a"), (i, "b_rg_x"))):
                        act.wait_ge(s["gate_product"], 2 * n + m + 1)
                        act.activation(dst[:, n, :], bank[2 * (n % 4) + m][:, :], ACT.Sigmoid,
                                       bias=vecT[:, VAT[b] + n:VAT[b] + n + 1]).then_inc(s["gate_ready"], 1)
                act.wait_ge(s["convolved"], KT)
                act.wait_ge(s["softplus"], 1)
                act.wait_ge(s["gate_ready"], 2 * KT)
                for n in range(KT):
                    act.activation(a[:, n, :], r[:, n, :], ACT.Exp, scale=sp_t[:, 3, n:n + 1])\
                       .then_inc(s["decay_ready"], 1)
                act.wait_ge(s["decay_ready"], KT)
                for n in range(KT):
                    act.activation(r[:, n, :], r[:, n, :], ACT.Tanh, scale=sp_t[:, 2, n:n + 1])\
                       .then_inc(s["tanh_ready"], 1)
                act.wait_ge(s["one_minus"], 1)
                act.activation(r[:, :, :], r[:, :, :], ACT.Sqrt).then_inc(s["rooted"], 1)
    sem.over()


def diff_attention(nc, sem, bank, ident, vecT, QKV, biasE, neg_lam, O):
    sem = PhaseSems(nc)
    with ExitStack() as st:
        def sb(name, shape):
            return st.enter_context(nc.sbuf_tensor(name, shape, F32))
        sq = O
        stat = sb("da_stat", [P, 2, TT, 2 * HEADS])
        rstd = sb("da_rstd", [P, 2, TT, 2 * HEADS])
        stage = sb("da_stage", [P, 2, TT, P])
        qkT = sb("da_qkT", [P, 2, SEQ])
        prob = sb("da_prob", [P, 4, SEQ])
        comb = sb("da_comb", [P, 2, SEQ])
        turned_sb = sb("da_turned", [P, 2, SEQ])
        nmax = sb("da_nmax", [P, 4])
        rsum = sb("da_rsum", [P, 4])
        rinv = sb("da_rinv", [P, 4])
        names = ("squared", "summed", "rooted", "staged", "qk_turned", "qk_ready", "scores_ready", "max_ready",
                 "probs_ready", "combined", "comb_turned", "combT_ready", "pv_ready", "out_stored", "dve_link", "act_link")
        s = {n: sem("da_" + n) for n in names}
        cr = {e: sem("da_carrier_" + e) for e in ("pe", "act", "dve")}
        S = [bank[0], bank[1], bank[2], bank[3]]
        T = [bank[4], bank[5]]
        OB = [bank[6], bank[7]]
        nk = [(q + 1) * P for q in range(TT)]
        with nc.Block() as block:
            @block.vector
            def _(dve):
                link = Link(dve, s["dve_link"])
                for m in range(2):
                    dve.wait_ge(s["squared"], m + 1)
                    dve.tensor_reduce(stat[:, m].rearrange("p t g -> p (t g)"),
                                      sq[:, :, :].rearrange("p t (g d) -> p (t g) d", d=HD), AX.X, ALU.add)\
                       .then_inc(s["summed"], 1)
                dve.wait_ge(s["summed"], 2)
                link(dve.tensor_scalar(stat[:, :, :, :], stat[:, :, :, :], 1.0 / HD, EPS, ALU.mult, ALU.add))
                dve.wait_ge(s["rooted"], 1)
                link(dve.reciprocal(rstd[:, :, :, :], rstd[:, :, :, :]))

                def unit_max(h, q):
                    for c in range(2):
                        u = 8 * h + 2 * q + c
                        dve.wait_ge(s["scores_ready"], u + 2)
                        dve.wait_ge(s["probs_ready"], u + 1)
                        dve.tensor_reduce(nmax[:, (2 * q + c) % 4:(2 * q + c) % 4 + 1], S[(2 * q + c) % 4][:, 0:nk[q]],
                                          AX.X, ALU.max, negate=True).then_inc(s["max_ready"], 1)

                def combine(h, q):
                    w = 4 * h + q
                    a, b = (2 * q) % 4, (2 * q + 1) % 4
                    dve.wait_ge(s["probs_ready"], 4 + 8 * h + 2 * q + 2)
                    link(dve.reciprocal(rinv[:, a:a + 2], rsum[:, a:a + 2]))
                    link(dve.tensor_tensor(rinv[:, b:b + 1], rinv[:, b:b + 1], neg_lam[:, 0:1], ALU.mult))
                    dve.wait_ge(s["comb_turned"], w + 1)
                    link(dve.tensor_scalar(comb[:, q % 2, 0:nk[q]], prob[:, a, 0:nk[q]], rinv[:, a:a + 1], None, ALU.mult))
                    dve.scalar_tensor_tensor(comb[:, q % 2, 0:nk[q]], prob[:, b, 0:nk[q]], rinv[:, b:b + 1],
                                             comb[:, q % 2, 0:nk[q]], ALU.mult, ALU.add).then_inc(s["combined"], 1)

                def store(h, q):
                    w = 4 * h + q
                    held(dve, cr["dve"], s["pv_ready"], 2 + w + 1)
                    dve.tensor_copy(O[:, q, bass.ds(h * P, P)], OB[q % 2][:, 0:P]).then_inc(s["out_stored"], 1)

                def stage_rows(h):
                    for m in range(2):
                        held(dve, cr["dve"], s["qk_turned"], 2 * h + 1)
                        dve.tensor_tensor(stage[:, m].rearrange("p t (c d) -> p t c d", d=HD),
                                          QKV[:, m, :, bass.ds(h * P, P)].rearrange("p t (c d) -> p t c d", d=HD),
                                          rstd[:, m, :, bass.ds(h * 2, 2)].unsqueeze(3).broadcast_to([P, TT, 2, HD]),
                                          ALU.mult).then_inc(s["staged"], 1)

                def head(h, last):
                    link.turn(5, h, TT * 3)
                    if not last:
                        stage_rows(h + 1)
                    unit_max(h, 2)
                    combine(h, 1)
                    unit_max(h, 3)
                    store(h, 0)
                    combine(h, 2)
                    if not last:
                        unit_max(h + 1, 0)
                    store(h, 1)
                    combine(h, 3)
                    if not last:
                        unit_max(h + 1, 1)
                    store(h, 2)
                    if not last:
                        combine(h + 1, 0)
                    store(h, 3)
                stage_rows(0)
                unit_max(0, 0)
                unit_max(0, 1)
                combine(0, 0)
                with dve.Fori(0, HEADS - 1) as h:
                    head(h, False)
                head(HEADS - 1, True)

            @block.tensor
            def _(pe):
                def scores(h, q):
                    for c in range(2):
                        u = 8 * h + 2 * q + c
                        held(pe, None, s["probs_ready"], u + 1)
                        bk = S[(2 * q + c) % 4]
                        r0 = c * HD
                        pe.matmul(bk[:, 0:nk[q]], qkT[r0:r0 + HD, 0, q * P:(q + 1) * P], qkT[r0:r0 + HD, 1, 0:nk[q]],
                                  start=True, stop=False)
                        lo = max(q - 1, 0) * P
                        pe.matmul(bk[:, lo:nk[q]], ident[:, :],
                                  biasE[:, h, (2 * P - (nk[q] - lo)):2 * P],
                                  start=False, stop=True).then_inc(s["scores_ready"], 1)

                def turn(h, q, last=False):
                    w = 4 * h + q
                    held(pe, None, s["combined"], 2 + w + 1)
                    if q < 2 or last:
                        held(pe, None, s["combT_ready"], w + 1)
                    else:
                        held(pe, None, s["qk_ready"], 2 * (h + 1) + q - 1)
                    for k in range(q + 1):
                        mm = pe.transpose(T[q % 2][:, k * P:(k + 1) * P], comb[:, q % 2, k * P:(k + 1) * P], ident[:, :])
                    mm.then_inc(s["comb_turned"], 1)

                def values(h, q):
                    w = 4 * h + q
                    held(pe, cr["pe"], s["combT_ready"], 2 + w + 1)
                    held(pe, cr["pe"], s["out_stored"], w + 1)
                    for k in range(q + 1):
                        mm = pe.matmul(OB[q % 2][:, 0:P], turned_sb[:, q % 2, k * P:(k + 1) * P],
                                       QKV[:, 2, k, bass.ds(h * P, P)], start=k == 0, stop=k == q)
                    mm.then_inc(s["pv_ready"], 1)

                def turn_qk(h):
                    for m in range(2):
                        held(pe, None, s["staged"], 2 * h + m + 1)
                        if not isinstance(h, int) or h > 0:
                            held(pe, None, s["combT_ready"], 4 * h - 1 + m)
                        for t in range(TT):
                            mm = pe.transpose(T[m][:, t * P:(t + 1) * P], stage[:, m, t, :], ident[:, :])
                        mm.then_inc(s["qk_turned"], 1)

                def head(h, last):
                    turn(h, 0)
                    scores(h, 2)
                    values(h, 0)
                    turn(h, 1)
                    scores(h, 3)
                    if not last:
                        turn_qk(h + 1)
                    values(h, 1)
                    turn(h, 2, last)
                    if not last:
                        held(pe, cr["pe"], s["qk_ready"], 2 * (h + 1) + 2)
                        scores(h + 1, 0)
                    values(h, 2)
                    turn(h, 3, last)
                    if not last:
                        scores(h + 1, 1)
                    values(h, 3)
                turn_qk(0)
                pe.wait_ge(s["qk_ready"], 2)
                scores(0, 0)
                scores(0, 1)
                with pe.Fori(0, HEADS - 1) as h:
                    head(h, False)
                head(HEADS - 1, True)

            @block.scalar
            def _(act):
                act.sem_inc(s["probs_ready"], 4)
                act.sem_inc(s["qk_turned"], 1)
                act.sem_inc(s["scores_ready"], 1)
                act.sem_inc(s["combined"], 2)
                act.sem_inc(s["comb_turned"], 2)
                act.sem_inc(s["combT_ready"], 2)
                act.sem_inc(s["pv_ready"], 2)
                act.sem_inc(s["out_stored"], 2)
                for m in range(2):
                    if m:
                        act.wait_ge(s["summed"], 1)
                    act.activation(sq[:, :, :], QKV[:, m], ACT.Square).then_inc(s["squared"], 1)
                act.wait_ge(s["dve_link"], 1)
                act.activation(rstd[:, :, :, :], stat[:, :, :, :], ACT.Sqrt).then_inc(s["rooted"], 1)

                def exps(h, q):
                    for c in range(2):
                        u = 8 * h + 2 * q + c
                        held(act, None, s["max_ready"], u + 1)
                        held(act, None, s["combined"], 4 * h + q + 1)
                        sl = (2 * q + c) % 4
                        act.activation(prob[:, sl, 0:nk[q]], S[sl][:, 0:nk[q]], ACT.Exp, bias=nmax[:, sl:sl + 1],
                                       accum_out=rsum[:, sl:sl + 1]).then_inc(s["probs_ready"], 1)

                def keep(h, q):
                    w = 4 * h + q
                    held(act, None, s["comb_turned"], 2 + w + 1)
                    held(act, None, s["pv_ready"], w + 1)
                    act.activation(turned_sb[:, q % 2, 0:nk[q]], T[q % 2][:, 0:nk[q]], ACT.Copy)\
                       .then_inc(s["combT_ready"], 1)

                def keep_qk(h):
                    for m, g in enumerate(("q_norm_g", "k_norm_g")):
                        held(act, None, s["qk_turned"], 2 * h + m + 2)
                        held(act, None, s["scores_ready"], 8 * h + 1)
                        act.activation(qkT[:, m, :], T[m][:, :], ACT.Copy, scale=vecT[:, VAT[g]:VAT[g] + 1])\
                           .then_inc(s["qk_ready"], 1)

                def head(h, last):
                    keep(h, 0)
                    exps(h, 2)
                    keep(h, 1)
                    if not last:
                        keep_qk(h + 1)
                    exps(h, 3)
                    keep(h, 2)
                    if not last:
                        exps(h + 1, 0)
                    keep(h, 3)
                    if not last:
                        exps(h + 1, 1)
                keep_qk(0)
                exps(0, 0)
                exps(0, 1)
                with act.Fori(0, HEADS - 1) as h:
                    head(h, False)
                head(HEADS - 1, True)
    sem.over()


def attention(nc, name, sem, bank, ident, q_of, branches, per_turn, O, out_at, row_scale, meanwhile=None):
    sem = PhaseSems(nc)
    with ExitStack() as st:
        def sb(n, shape):
            return st.enter_context(nc.sbuf_tensor(f"{name}_{n}", shape, F32))
        q65 = sb("q", [HD + 1, per_turn, SEQ])
        if row_scale:
            ones = sb("ones", [HD + 1, SEQ])
        prob = sb("prob", [P, 4, SEQ])
        kept = sb("kept", [P, 2, SEQ])
        nmax, rsum, rinv = sb("nmax", [P, 8]), sb("rsum", [P, 8]), sb("rinv", [P, 8])
        S, T, OB = bank[0:4], bank[4:6], bank[6:8]
        s = {n: sem(f"{name}_{n}") for n in ("staged", "rowed", "scores", "maxed", "probs", "turned", "kept", "pv",
                                              "stored", "link", "ones")}
        cr = {e: sem(f"{name}_carrier_{e}") for e in ("pe", "act", "dve")}
        units = [(a, br, q) for a in range(per_turn) for q in range(TT) for br in range(len(branches))]
        n = len(units)
        a_head = n // per_turn
        links = sum(2 if branches[br][4] else 1 for a, br, q in units)

        def shape_of(m):
            a, br, q = units[m]
            nk = branches[br][0]
            return a, br, q, nk[q], -(-nk[q] // P), min(P, nk[0])
        with nc.Block() as block:
            if meanwhile:
                @block.sync
                def _(sp):
                    meanwhile(sp)

            def turns(eng, body):
                with eng.Fori(0, 2) as g:
                    if per_turn == 4:
                        body(g, g, 4 * g)
                    else:
                        with eng.Fori(0, 2) as hh:
                            body(2 * g + hh, g, 4 * g + 2 * hh)

            def steps(turn_of):
                for m in range(n + max(lag for lag, _ in turn_of)):
                    for lag, do in turn_of:
                        if 0 <= m - lag < n:
                            do(m - lag)

            @block.vector
            def _(dve):
                link = Link(dve, s["link"])
                dve.memset(q65[HD:HD + 1, :, :], 1.0).then_inc(s["ones"], 1)
                if row_scale:
                    dve.memset(ones[:, :], 1.0).then_inc(s["ones"], 1)

                def body(t, g, h0):
                    link.turn(0, t, links)

                    def top(m):
                        nk = shape_of(m)[3]
                        held(dve, None, s["scores"], n + n * t + m + 1)
                        dve.wait_ge(s["probs"], n * t + m + 1)
                        dve.tensor_reduce(nmax[:, m % 8:m % 8 + 1], S[m % 4][:, 0:nk], AX.X, ALU.max, negate=True)\
                           .then_inc(s["maxed"], 1)

                    def scale(m):
                        a, br, q = units[m]
                        gate_of = branches[br][4]
                        held(dve, None, s["probs"], 4 + n * t + m + 1)
                        link(dve.reciprocal(rinv[:, m % 8:m % 8 + 1], rsum[:, m % 8:m % 8 + 1]))
                        if gate_of:
                            link(dve.tensor_tensor(rinv[:, m % 8:m % 8 + 1], rinv[:, m % 8:m % 8 + 1], gate_of(q, h0 + a),
                                                   ALU.mult))

                    def store(m):
                        a, br, q = units[m]
                        dst = O[:, q, bass.ds(h0 * HD + (out_at + a * HD), HD)]
                        if br:
                            held(dve, cr["dve"], s["stored"], 2 + n * t + m)
                        held(dve, cr["dve"], s["pv"], 2 + n * t + m + 1)
                        r = rinv[:, m % 8:m % 8 + 1]
                        if br:
                            ins = dve.scalar_tensor_tensor(dst, OB[m % 2][:, 0:HD], r, dst, ALU.mult, ALU.add)
                        else:
                            ins = dve.tensor_scalar(dst, OB[m % 2][:, 0:HD], r, None, ALU.mult)
                        ins.then_inc(s["stored"], 1)
                    steps([(0, top), (1, scale), (5, store)])
                turns(dve, body)

            @block.tensor
            def _(pe):
                def body(t, g, h0):
                    def scores(m):
                        a, br, q, nk, _, _ = shape_of(m)
                        if br == 0 and q == 0:
                            held(pe, None, s["staged"], per_turn * t + a + 1)
                            if row_scale:
                                held(pe, None, s["rowed"], per_turn * t + a + 1)
                        held(pe, None, s["probs"], n * t + m + 1)
                        pe.matmul(S[m % 4][:, 0:nk], q65[:, a, q * P:(q + 1) * P], branches[br][1](g, h0 + a, nk),
                                  start=True, stop=False)
                        (lo, hi), mask = branches[br][2](q)
                        pe.matmul(S[m % 4][:, lo:hi], ident[:, :], mask, start=False, stop=True).then_inc(s["scores"], 1)

                    def turn(m):
                        _, _, _, _, tiles, rows = shape_of(m)
                        held(pe, None, s["probs"], 4 + n * t + m + 1)
                        held(pe, None, s["kept"], n * t + m + 1)
                        for k in range(tiles):
                            mm = pe.transpose(T[m % 2][0:rows, k * P:(k + 1) * P], prob[:, m % 4, k * P:k * P + rows],
                                              ident[:, :])
                        mm.then_inc(s["turned"], 1)

                    def values(m):
                        a, br, _, _, tiles, rows = shape_of(m)
                        held(pe, cr["pe"], s["kept"], 2 + n * t + m + 1)
                        held(pe, cr["pe"], s["stored"], n * t + m + 1)
                        for k in range(tiles):
                            mm = pe.matmul(OB[m % 2][:, 0:HD], kept[0:rows, m % 2, k * P:(k + 1) * P],
                                           branches[br][3](g, h0 + a, k), start=k == 0, stop=k == tiles - 1)
                        mm.then_inc(s["pv"], 1)
                    steps([(0, scores), (3, turn), (4, values)])
                pe.wait_ge(s["ones"], 2 if row_scale else 1)
                turns(pe, body)

            @block.scalar
            def _(act):
                act.sem_inc(s["scores"], n)
                act.sem_inc(s["probs"], 4)
                act.sem_inc(s["turned"], 4)
                act.sem_inc(s["kept"], 2)
                act.sem_inc(s["pv"], 2)
                act.sem_inc(s["stored"], 2)
                act.wait_ge(s["ones"], 2 if row_scale else 1)

                def body(t, g, h0):
                    for a in range(per_turn):
                        held(act, cr["act"], s["scores"], n * t + a_head * (a + 1))
                        act.activation(q65[0:HD, a, :], q_of(t, a), ACT.Copy, scale=HD ** -0.5).then_inc(s["staged"], 1)
                        if row_scale:
                            act.activation(q65[HD:HD + 1, a, :], ones[HD:HD + 1, :], ACT.Copy,
                                           scale=row_scale(h0 + a)).then_inc(s["rowed"], 1)

                    def exp(m):
                        nk = shape_of(m)[3]
                        held(act, None, s["maxed"], n * t + m + 1)
                        held(act, None, s["turned"], n * t + m + 1)
                        act.activation(prob[:, m % 4, 0:nk], S[m % 4][:, 0:nk], ACT.Exp, bias=nmax[:, m % 8:m % 8 + 1],
                                       accum_out=rsum[:, m % 8:m % 8 + 1]).then_inc(s["probs"], 1)

                    def keep(m):
                        _, _, _, _, tiles, rows = shape_of(m)
                        held(act, None, s["turned"], 4 + n * t + m + 1)
                        held(act, None, s["pv"], n * t + m + 1)
                        act.activation(kept[0:rows, m % 2, 0:tiles * P], T[m % 2][0:rows, 0:tiles * P], ACT.Copy)\
                           .then_inc(s["kept"], 1)
                    steps([(3, keep), (0, exp)])
                turns(act, body)
    sem.over()


def concatenated(ring, w, spans):
    def pieces(p, b):
        got, at = [], 0
        for lo, hi in spans[2 * p + b]:
            got.append((ring[:, b, :, at:at + hi - lo], w[:, lo:hi].rearrange("(k q) n -> q k n", q=P)))
            at += hi - lo
        return got
    return pieces


def second_cols(ring, w_in):
    return concatenated(ring, w_in, [[(0, 256), (256, 512)], [(512, 896), (1024, 1152)], [(1304, 1560), (1560, 1816)],
                                     [(1816, 2072), (2072, 2328)]])


def second_layer(nc, A, outer, sem, sb, bank, ident, vecT, x, hT, gemm, out_rows, out_written, residual, stop):
    ring = gemm.ring
    w_in = A["w_in_2"][0]

    def finish(rows):
        with nc.Block() as block:
            @block.sync
            def _(sp):
                sp.dma_start(out_rows, rows).then_inc(out_written, 16)
                sp.wait_ge(out_written, 16)

    norm_to_cols(nc, "ln1", sem, sb, bank, ident, x, VAT["ln1_2"], vecT, hT)

    with ExitStack() as st:
        def tb(name, shape, dt=F32):
            return st.enter_context(nc.sbuf_tensor(name, shape, dt))
        T4 = tb("projT", [P, 4, 4, SEQ])
        R2 = tb("proj_rows", [P, 2, TT, 512])
        NG = 2 * P + 24
        cols_pieces = second_cols(ring, w_in)
        rows_pieces = concatenated(ring, w_in, [[(2328, 2584), (2584, 2840)], [(896, 1024), (1152, 1304)]])
        width = lambda p, b: NG if (p, b) == (2, 1) else 512
        place = lambda p, b, j: T4[:, 2 * p + b, j, :] if p < 2 else R2[:, b, j, 0:width(p, b)]
        gemm.phase(3, lambda p, b: cols_pieces(p, b) if p < 2 else rows_pieces(0, b),
                   lambda p: cols_of(hT) if p < 2 else rows_of(hT),
                   gemm.drain("act", (0, 2), lambda e, p, b, j, bk: e.activation(place(p, b, j), bk[:, 0:width(p, b)], ACT.Copy)),
                   gemm.drain("dve", (1, 3), lambda e, p, b, j, bk: e.tensor_copy(place(p, b, j), bk[:, 0:width(p, b)])),
                   unrolled=True, width=width)

        kN = tb("nsa_keys", [HD + 1, 4, SEQ])
        kF = tb("fox_keys", [HD + 1, HEADS, SEQ])
        kC = tb("cmp_keys", [HD + 1, 2, NCMP])
        vC = tb("cmp_values", [NCMP, 2, HD])
        mask = tb("causal_mask", [P, P])
        cmask = tb("cmp_mask", [P, TT, NCMP])
        slopes = tb("slopes", [HD + 1, HEADS])
        valid = tb("first_rows_valid", [P, 1])
        f_loaded, f_high, f_split, f_product, f_abs, f_exp, cum_ready, cum_moved = (
            sem("forget_" + n) for n in ("loaded", "high", "split", "product", "abs", "exp", "cum_ready", "cum_moved"))

        prep = ExitStack()
        pb = lambda name, shape, dt=F32: prep.enter_context(nc.sbuf_tensor(name, shape, dt))
        wf, bf = pb("w_forget", [P, KT, HEADS]), pb("b_forget", [HEADS, 1])
        wfh, wfl = pb("w_forget_high", [P, KT, HEADS], F32R), pb("w_forget_low", [P, KT, HEADS], F32R)
        fz = pb("forget", [HEADS, 6, SEQ])
        pos_i, pos_f = pb("positions_int", [1, SEQ], I32), pb("positions", [1, SEQ])
        w1 = pb("cmp_w1", [P, 2, CMP_BLOCK, P])
        w2 = pb("cmp_w2", [P, 2, HD])
        pe_rows = pb("cmp_pe", [CMP_BLOCK, 2, 2, HD])
        peT = pb("cmp_peT", [P, 2, CMP_BLOCK])
        XD = ring[:, 0].rearrange("p k n -> p (k n)").rearrange("p (i a s) -> p i a s", i=2, a=2)
        hid = pb("cmp_hidden", [P, 4, NCMP])
        names = ("w_loaded", "pe_loaded", "pool_step", "iota_done", "pos_ready", "pos_moved", "keys_copied", "gates_ready", "dve_link",
                 "pe_turned", "peT_ready", "cleared", "placed", "hid_product", "hid_ready", "out_product", "out_ready")
        s = {n: sem("prep_" + n) for n in names}
        with nc.Block() as block:
            @block.sync
            def _(sp):
                sp.dma_start(wf[:, :, :], w_in[:, 2840:2848].rearrange("(k q) n -> q k n", q=P)).then_inc(f_loaded, 16)
                sp.dma_start(bf[:, :], A["b_fg_2"].rearrange("l h -> h l")).then_inc(f_loaded, 16)
                for i, n in enumerate(("k", "v")):
                    src = A[f"w_cmp1_{n}_2"][0].rearrange("(l d) h -> d l h", d=HD)
                    for half in range(2):
                        sp.dma_start(w1[half * HD:(half + 1) * HD, i], src).then_inc(s["w_loaded"], 16)
                    sp.dma_start(w2[:, i, :], A[f"w_cmp2_{n}_2"][0]).then_inc(s["w_loaded"], 16)
                    for half in range(2):
                        sp.dma_start(pe_rows[:, i, half, :], A[f"pe_cmp_{n}_2"][0]).then_inc(s["pe_loaded"], 16)
                sp.wait_ge(s["pos_ready"], 1)
                for i in range(4):
                    sp.dma_start(kN[HD:HD + 1, i, :], pos_f[0:1, :]).then_inc(s["pos_moved"], 16)
                ends = pos_f[0:1, CMP_BLOCK - 1:CMP_BLOCK + CMP_STRIDE * (NCMP - 1):CMP_STRIDE]
                with nc.allow_non_contiguous_dma(reason="31 positions"):
                    for g in range(2):
                        sp.dma_start(kC[HD:HD + 1, g, :], ends).then_inc(s["pos_moved"], 16)
                sp.wait_ge(cum_ready, 1)
                sp.dma_start(kF[HD:HD + 1, :, :], fz[:, 5, :]).then_inc(cum_moved, 16)
                sp.wait_ge(s["pos_moved"], 16 * 6)
                sp.wait_ge(cum_moved, 16)

            @block.gpsimd
            def _(pool):
                link = Link(pool, s["pool_step"])
                for g in range(2):
                    pool.memset(XD[g * HD:(g + 1) * HD, :, :, (1 - g) * SEQ:(2 - g) * SEQ], 0.0).then_inc(s["cleared"], 1)
                    pool.wait_ge(s["cleared"], g + 1)
                pool.iota(pos_i[:, :], pattern=[[1, SEQ]], base=0, channel_multiplier=0).then_inc(s["iota_done"], 1)
                link(pool.memset(mask[:, :], 0.0))
                link(pool.memset(cmask[:, :, :], 0.0))
                link(pool.memset(valid[:, :], 1.0))
                for h in range(HEADS):
                    link(pool.memset(slopes[:, h:h + 1], 2.0 ** (-8.0 * (h + 1) / HEADS)))
                link(pool.affine_select(out=mask[:, :], in_=mask[:, :], compare_op=ALU.is_ge, fill=NEG, base=0,
                                        pattern=[[-1, P]], channel_multiplier=1))
                for t in range(TT):
                    link(pool.affine_select(out=cmask[:, t, :], in_=cmask[:, t, :], compare_op=ALU.is_ge, fill=NEG,
                                            base=t * P - (CMP_BLOCK - 1), pattern=[[-CMP_STRIDE, NCMP]],
                                            channel_multiplier=1))
                link(pool.affine_select(out=valid[:, :], in_=valid[:, :], compare_op=ALU.is_ge, fill=0.0,
                                        base=-(CMP_BLOCK - 1), pattern=[[0, 1]], channel_multiplier=1))

            @block.tensor
            def _(pe):
                pe.wait_ge(f_split, 1)
                for k in range(KT):
                    for n, (w_, x_) in enumerate(((wfh, hT[0]), (wfh, hT[1]), (wfl, hT[0]))):
                        mm = pe.matmul(bank[0][0:HEADS, :], w_[:, k, :], x_[:, k, :], start=k == 0 and n == 0,
                                       stop=k == KT - 1 and n == 2)
                mm.then_inc(f_product, 1)
                pe.wait_ge(s["pe_loaded"], 16 * 4)
                for i in range(2):
                    pe.transpose(bank[1][:, i * CMP_BLOCK:(i + 1) * CMP_BLOCK], pe_rows[:, i, :, :].rearrange("l a d -> l (a d)"),
                                 ident[0:CMP_BLOCK, 0:CMP_BLOCK]).then_inc(s["pe_turned"], 1)
                pe.wait_ge(s["w_loaded"], 16 * 6)
                pe.wait_ge(s["cleared"], 2)
                pe.wait_ge(s["placed"], 8)
                for i in range(2):
                    for l in range(CMP_BLOCK):
                        both = XD[:, i, l // CMP_STRIDE, :].rearrange("p (g s) -> p g s", g=2)
                        mm = pe.matmul(bank[3 + i][:, 0:2 * NCMP], w1[:, i, l, :],
                                       both[:, :, l:l + CMP_STRIDE * (NCMP - 1) + 1:CMP_STRIDE],
                                       start=l == 0, stop=l == CMP_BLOCK - 1)
                    mm.then_inc(s["hid_product"], 1)
                pe.wait_ge(s["hid_ready"], 2)
                for g in range(2):
                    pe.matmul(bank[7][0:HD, g * 64:g * 64 + NCMP], w2[:, 0, :], hid[:, g, :], start=True, stop=True)\
                      .then_inc(s["out_product"], 1)
                for g in range(2):
                    pe.matmul(bank[1][0:NCMP, 256 + g * 64:256 + (g + 1) * 64], hid[:, 2 + g, :], w2[:, 1, :],
                              start=True, stop=True).then_inc(s["out_product"], 1)

            @block.scalar
            def _(act):
                act.wait_ge(f_loaded, 32)
                act.activation(wfh[:, :, :], wf[:, :, :], ACT.Copy).then_inc(f_high, 1)
                act.wait_ge(f_abs, 1)
                act.activation(fz[:, 2, :], fz[:, 1, :], ACT.Exp).then_inc(f_exp, 1)
                for h in range(HEADS):
                    hp, par = h // 2, h % 2
                    act.activation(kF[0:HD, h, :], T4[par * HD:(par + 1) * HD, 3, hp, :], ACT.Copy)\
                       .then_inc(s["keys_copied"], 1)
                for i in range(2):
                    for g in range(2):
                        act.activation(kN[0:HD, 2 * i + g, :], T4[g * HD:(g + 1) * HD, 1, 2 + i, :], ACT.Copy)\
                           .then_inc(s["keys_copied"], 1)
                act.activation(R2[:, 1, :, 2 * P:NG], R2[:, 1, :, 2 * P:NG], ACT.Sigmoid).then_inc(s["gates_ready"], 1)
                for i in range(2):
                    act.wait_ge(s["hid_product"], i + 1)
                    act.activation(hid[:, 2 * i:2 * i + 2, :].rearrange("p g n -> p (g n)"), bank[3 + i][:, 0:2 * NCMP],
                                   ACT.Gelu_apprx_tanh).then_inc(s["hid_ready"], 1)
                act.wait_ge(s["out_product"], 4)
                for g in range(2):
                    act.activation(kC[0:HD, g, :], bank[7][0:HD, g * 64:g * 64 + NCMP], ACT.Copy)\
                       .then_inc(s["out_ready"], 1)
                for g in range(2):
                    act.activation(vC[:, g, :], bank[1][0:NCMP, 256 + g * 64:256 + (g + 1) * 64], ACT.Copy)\
                       .then_inc(s["out_ready"], 1)

            @block.vector
            def _(dve):
                link = Link(dve, s["dve_link"])
                dve.wait_ge(f_high, 1)
                dve.tensor_tensor(wfl[:, :, :], wf[:, :, :], wfh[:, :, :].bitcast(F32), ALU.subtract).then_inc(f_split, 1)
                dve.wait_ge(s["iota_done"], 1)
                dve.tensor_copy(pos_f[:, :], pos_i[:, :]).then_inc(s["pos_ready"], 1)
                dve.wait_ge(s["pe_turned"], 2)
                dve.tensor_copy(peT[:, :, :], bank[1][:, 0:2 * CMP_BLOCK].rearrange("d (i l) -> d i l", i=2))\
                   .then_inc(s["peT_ready"], 1)
                dve.wait_ge(s["peT_ready"], 1)
                for i in range(2):
                    for a in range(2):
                        for g in range(2):
                            at = slice(g * HD, (g + 1) * HD)
                            by16 = lambda ap: ap.rearrange("p (n r) -> p n r", r=CMP_STRIDE)
                            part = peT[at, i, a * CMP_STRIDE:(a + 1) * CMP_STRIDE]
                            dve.tensor_tensor(by16(XD[at, i, a, g * SEQ:(g + 1) * SEQ]), by16(T4[at, 1, i, :]),
                                              part.unsqueeze(1).broadcast_to([HD, SEQ // CMP_STRIDE, CMP_STRIDE]), ALU.add)\
                               .then_inc(s["placed"], 1)
                dve.wait_ge(f_product, 1)
                link(dve.tensor_scalar(fz[:, 0, :], bank[0][0:HEADS, :], bf[:, 0:1], None, ALU.add))
                link(dve.tensor_scalar(fz[:, 1, :], fz[:, 0, :], -1.0, None, ALU.mult))
                dve.tensor_tensor(fz[:, 1, :], fz[:, 1, :], fz[:, 0, :], ALU.min).then_inc(f_abs, 1)
                dve.wait_ge(f_exp, 1)
                log1p_steps(dve, link, fz[:, 5, :], fz[:, 2, :], fz[:, 3, :], fz[:, 4, :])
                link(dve.tensor_scalar(fz[:, 1, :], fz[:, 0, :], -1.0, 0.0, ALU.mult, ALU.max))
                link(dve.tensor_tensor(fz[:, 1, :], fz[:, 1, :], fz[:, 5, :], ALU.add))
                link(dve.memset(fz[:, 2, :], 1.0))
                dve.tensor_tensor_scan(fz[:, 5, :], fz[:, 2, :], fz[:, 1, :], 0.0, ALU.mult, ALU.add)\
                   .then_inc(cum_ready, 1)
                dve.wait_ge(s["gates_ready"], 1)
                dve.wait_ge(s["pool_step"], 3 + HEADS + 1 + TT + 1)
                dve.tensor_scalar(R2[:, 1, 0, 2 * P:NG:3], R2[:, 1, 0, 2 * P:NG:3], valid[:, 0:1], None, ALU.mult)\
                   .then_inc(s["gates_ready"], 1)

        prep.close()
        O = tb("mix_out", [P, TT, D])

        gate = lambda br: (lambda q, h: R2[:, 1, q, bass.ds(h * 3 + (2 * P + br), 1)])
        q_from = lambda i, n: (lambda t, a: T4[a % 2 * HD:(a % 2 + 1) * HD, i, t * n + a // 2, :])
        slope = lambda h: slopes[HD:HD + 1, bass.ds(h, 1)]
        full = [(q + 1) * P for q in range(TT)]
        causal = lambda q: ((q * P, (q + 1) * P), mask[:, :])
        compressed = ([NCMP] * TT, lambda g, h, n: kC[:, g, 0:n], lambda q: ((0, NCMP), cmask[:, q, :]),
                      lambda g, h, k: vC[:, g, :], gate(0))
        selected = (full, lambda g, h, n: kN[:, g, 0:n], causal, lambda g, h, k: R2[:, 1, k, bass.ds(g * HD, HD)], gate(1))
        window = (full, lambda g, h, n: kN[:, 2 + g, 0:n], causal, lambda g, h, k: R2[:, 1, k, bass.ds(g * HD + P, HD)], gate(2))
        fox = (full, lambda g, h, n: kF[:, h, 0:n], causal, lambda g, h, k: R2[:, 0, k, bass.ds(h * HD, HD)], None)
        attention(nc, "nsa", sem, bank, ident, q_from(0, 1), [selected, compressed, window], 2, O, 0, slope)
        attention(nc, "fox", sem, bank, ident, q_from(2, 2), [fox], 4, O, 4 * P, None,
                  meanwhile=lambda sp: gemm.load_ahead(sp, block_pieces(ring, A["w_out_2"][0])))
        gemm.ahead = True

        for name, at in (("gn_nsa", 0), ("gn_fox", 4)):
            norm_to_cols(nc, name, sem, sb, bank, ident, O, VAT[name + "_2"], vecT, hT, at=at, width=4 * P, width_at=at * P)

    gemm.phase(1, block_pieces(ring, A["w_out_2"][0]), rows_of(hT), None, residual)
    if stop == "mix":
        finish(x[:, :, :])
        return
    moe(nc, A, sem, bank, ident, vecT, x, hT, ring, gemm)
    if stop == "moe":
        finish(x[:, :, :])
        return
    last_stage(nc, A, sem, sb, bank, ident, vecT, x, hT, ring, gemm, out_rows, out_written)


def moe(nc, A, sem_, bank, ident, vecT, x, hT, ring, gemm):
    outer = ExitStack()

    def ob(name, shape, dt=F32):
        return outer.enter_context(nc.sbuf_tensor(name, shape, dt))
    wt = ob("route_weights", [P, TT, TOPK])
    wtT = ob("route_weightsT", [EXPERTS, SEQ])
    slot = ob("route_slots", [P, TT * TOPK], U32)
    out_row = ob("route_out_rows", [P, TT * TOPK], U32)
    work = ob("work_experts", [1, ITEMS], I32)
    total = ob("work_total", [1, 1], I32)

    with ExitStack() as st:
        def tb(name, shape, dt=F32):
            return st.enter_context(nc.sbuf_tensor(name, shape, dt))
        rows = tb("moe_rows", [P, TT, D])
        norm_to_cols(nc, "ln2", sem_, None, bank, ident, x, VAT["ln2_2"], vecT, hT, keep=rows)
        gain = tb("ln2_wide", [P, D])
        sem = PhaseSems(nc)
        wr, br = tb("w_router", [P, KT, EXPERTS]), tb("b_router", [1, EXPERTS])
        ones, tri = tb("ones_square", [P, P]), tb("before", [P, P])
        iota_i, iota = tb("iota_int", [P, EXPERTS], I32), tb("iota", [P, EXPERTS])
        item_i, item = tb("item_int", [1, ITEMS], I32), tb("item", [1, ITEMS])
        tok, zero = tb("token_ids", [P, TT], I32), tb("zero_slots", [P, ITEMS + 1], I32)
        lg, top = tb("logits", [P, TT, EXPERTS]), tb("top_values", [P, TT, 8])
        top_i, top_f = tb("top_index", [P, TT, 8], U32), tb("top_index_float", [P, TT, 8])
        stat = tb("route_stat", [P, 3, TT])
        eq = tb("pick_onehot", [P, TT, TOPK, EXPERTS])
        tmp = tb("pick_tmp", [P, TT, TOPK, EXPERTS])
        chosen, dense = tb("chosen", [P, TT, EXPERTS]), tb("dense_weights", [P, TT, EXPERTS])
        place = tb("places", [P, TT, EXPERTS])
        picks = tb("pick_rows", [P, TT, TOPK])
        line = tb("expert_line", [P, 4, EXPERTS])
        grid = tb("work_grid", [1, ITEMS, EXPERTS])
        found = tb("work_found", [1, ITEMS])
        bu = tb("b_up_rows", [EXPERTS, 2 * D])
        br1, br2 = tb("b_up_rest", [EXPERTS, 2 * D]), tb("b_up_rest2", [EXPERTS, 2 * D])
        parts = tb("b_up_parts", [EXPERTS, 3, 2 * D], BF16)
        names = ("loaded", "bias_loaded", "gain_loaded", "gained", "h2_written", "zero_ready", "zeroed", "pool_link", "iotas", "logits_ready", "dve_link",
                 "tops_negated", "exps_ready", "chosen_ready", "places_ready", "slots_ready", "scattered", "parts_ready",
                 "parts_written", "weights_turned")
        s = {n: sem("route_" + n) for n in names}
        with nc.Block() as block:
            @block.sync
            def _(sp):
                sp.dma_start(wr[:, :, :], A["w_router_2"][0].rearrange("(k q) e -> q k e", q=P)).then_inc(s["loaded"], 16)
                sp.dma_start(br[:, :], A["b_router_2"]).then_inc(s["loaded"], 16)
                sp.dma_start(bu[:, :], A["b_up_2"][0]).then_inc(s["bias_loaded"], 16)
                sp.dma_start(gain[:, :], A["ln2_row"].broadcast_to([P, D])).then_inc(s["gain_loaded"], 16)
                sp.wait_ge(s["gained"], TT)
                sp.dma_start(A["h2_scratch"].rearrange("(t p) d -> p t d", p=P), rows[:, :, :]).then_inc(s["h2_written"], 16)
                sp.wait_ge(s["zero_ready"], 1)
                sp.dma_start(A["slot_tokens"].rearrange("(p c) o -> p (c o)", p=P), zero[:, :]).then_inc(s["zeroed"], 16)
                sp.wait_ge(s["parts_ready"], 1)
                sp.dma_start(A["bias_parts"], parts[:, :, :]).then_inc(s["parts_written"], 16)
                sp.wait_ge(s["parts_written"], 16)
                sp.wait_ge(s["h2_written"], 16)

            @block.gpsimd
            def _(pool):
                pool.memset(zero[:, :], 0).then_inc(s["zero_ready"], 1)
                link = Link(pool, s["pool_link"])
                link(pool.memset(ones[:, :], 1.0))
                link(pool.memset(tri[:, :], 1.0))
                link(pool.affine_select(out=tri[:, :], in_=tri[:, :], compare_op=ALU.is_gt, fill=0.0, base=0,
                                        pattern=[[1, P]], channel_multiplier=-1))
                link(pool.iota(iota_i[:, :], pattern=[[1, EXPERTS]], base=0, channel_multiplier=0))
                link(pool.iota(item_i[:, :], pattern=[[1, ITEMS]], base=0, channel_multiplier=0))
                link(pool.iota(tok[:, :], pattern=[[P, TT]], base=0, channel_multiplier=1))
                pool.wait_ge(s["slots_ready"], 1)
                pool.wait_ge(s["zeroed"], 16)
                for t in range(TT):
                    for k in range(TOPK):
                        j = t * TOPK + k
                        pool.indirect_dma_start(A["slot_tokens"], bass.IndirectOffsetOnAxis(ap=slot[:, j:j + 1], axis=0),
                                                tok[:, t:t + 1], None).then_inc(s["scattered"], 16)
                pool.wait_ge(s["scattered"], 16 * TT * TOPK)

            @block.tensor
            def _(pe):
                pe.wait_ge(s["loaded"], 32)
                pe.wait_ge(s["pool_link"], 3)
                for t in range(TT):
                    for k in range(KT):
                        for part in range(2):
                            pe.matmul(bank[t][:, 0:EXPERTS], hT[part][:, k, t * P:(t + 1) * P].bitcast(F32), wr[:, k, :],
                                      start=k == 0 and part == 0, stop=False)
                    pe.matmul(bank[t][:, 0:EXPERTS], ones[0:1, :], br[:, :], start=False, stop=True)\
                      .then_inc(s["logits_ready"], 1)
                pe.wait_ge(s["chosen_ready"], 1)
                for t in range(TT):
                    for u in range(t):
                        pe.matmul(bank[4][:, t * EXPERTS:(t + 1) * EXPERTS], ones[:, :], chosen[:, u, :], start=u == 0, stop=False)
                    pe.matmul(bank[4][:, t * EXPERTS:(t + 1) * EXPERTS], tri[:, :], chosen[:, t, :], start=t == 0, stop=True)
                for u in range(TT):
                    mm = pe.matmul(bank[5][:, 0:EXPERTS], ones[:, :], chosen[:, u, :], start=u == 0, stop=u == TT - 1)
                mm.then_inc(s["places_ready"], 1)
                for t in range(TT):
                    mm = pe.transpose(bank[6][0:EXPERTS, t * P:(t + 1) * P], dense[:, t, :], ident[:, :])
                mm.then_inc(s["weights_turned"], 1)

            @block.scalar
            def _(act):
                act.wait_ge(s["tops_negated"], 1)
                for t in range(TT):
                    act.activation(wt[:, t, :], top[:, t, 0:TOPK], ACT.Exp, bias=stat[:, 0, t:t + 1],
                                   accum_out=stat[:, 1, t:t + 1]).then_inc(s["exps_ready"], 1)

            @block.vector
            def _(dve):
                link = Link(dve, s["dve_link"])
                dve.wait_ge(s["bias_loaded"], 16)
                dve.wait_ge(s["gain_loaded"], 16)
                for t in range(TT):
                    dve.tensor_tensor(rows[:, t, :], rows[:, t, :], gain[:, :], ALU.mult).then_inc(s["gained"], 1)
                link(dve.tensor_copy(parts[:, 0, :], bu[:, :]))
                link(dve.tensor_tensor(br1[:, :], bu[:, :], parts[:, 0, :], ALU.subtract))
                link(dve.tensor_copy(parts[:, 1, :], br1[:, :]))
                link(dve.tensor_tensor(br2[:, :], br1[:, :], parts[:, 1, :], ALU.subtract))
                dve.tensor_copy(parts[:, 2, :], br2[:, :]).then_inc(s["parts_ready"], 1)
                dve.wait_ge(s["pool_link"], 6)
                link(dve.tensor_copy(iota[:, :], iota_i[:, :]))
                link(dve.tensor_copy(item[:, :], item_i[:, :]))
                for t in range(TT):
                    dve.wait_ge(s["logits_ready"], t + 1)
                    link(dve.tensor_copy(lg[:, t, :], bank[t][:, 0:EXPERTS]))
                    link(dve.max(top[:, t, :], lg[:, t, :]))
                    link(dve.max_index(top_i[:, t, :], top[:, t, :], lg[:, t, :]))
                dve.tensor_scalar(stat[:, 0, :], top[:, :, 0], -1.0, None, ALU.mult).then_inc(s["tops_negated"], 1)
                link(dve.tensor_copy(top_f[:, :, :], top_i[:, :, :]))
                for t in range(TT):
                    link(dve.tensor_tensor(eq[:, t], iota[:, :].unsqueeze(1).broadcast_to([P, TOPK, EXPERTS]),
                                           top_f[:, t, 0:TOPK].unsqueeze(2).broadcast_to([P, TOPK, EXPERTS]), ALU.is_equal))
                link(dve.tensor_reduce(chosen[:, :, :], eq[:, :, :, :].rearrange("p t k e -> p t e k"), AX.X, ALU.add))
                dve.wait_ge(s["exps_ready"], TT)
                link(dve.reciprocal(stat[:, 2, :], stat[:, 1, :]))
                link(dve.tensor_tensor(wt[:, :, :], wt[:, :, :], stat[:, 2, :].unsqueeze(2).broadcast_to([P, TT, TOPK]), ALU.mult))
                for t in range(TT):
                    link(dve.tensor_tensor(tmp[:, t], eq[:, t], wt[:, t, :].unsqueeze(2).broadcast_to([P, TOPK, EXPERTS]), ALU.mult))
                dve.tensor_reduce(dense[:, :, :], tmp[:, :, :, :].rearrange("p t k e -> p t e k"), AX.X, ALU.add)\
                   .then_inc(s["chosen_ready"], 1)
                dve.wait_ge(s["chosen_ready"], 1)
                dve.wait_ge(s["places_ready"], 1)
                link(dve.tensor_copy(line[:, 0, :], bank[5][:, 0:EXPERTS]))
                link(dve.tensor_scalar(line[:, 1, :], line[:, 0, :], 0.0, None, ALU.is_gt))
                for j in range(1, SEQ // P):
                    link(dve.scalar_tensor_tensor(line[:, 1, :], line[:, 0, :], float(j * P), line[:, 1, :], ALU.is_gt, ALU.add))
                link(dve.memset(line[:, 3, :], 1.0))
                link(dve.tensor_tensor_scan(line[:, 2, :], line[:, 3, :], line[:, 1, :], 0.0, ALU.mult, ALU.add))
                link(dve.tensor_tensor(line[:, 3, :], line[:, 2, :], line[:, 1, :], ALU.subtract))
                link(dve.tensor_copy(place[:, :, :], bank[4][:, 0:TT * EXPERTS].rearrange("p (t e) -> p t e", t=TT)))
                link(dve.scalar_tensor_tensor(place[:, :, :], line[:, 3, :].unsqueeze(1).broadcast_to([P, TT, EXPERTS]), float(P),
                                              place[:, :, :], ALU.mult, ALU.add))
                for t in range(TT):
                    link(dve.tensor_tensor(tmp[:, t], eq[:, t], place[:, t, :].unsqueeze(1).broadcast_to([P, TOPK, EXPERTS]), ALU.mult))
                link(dve.tensor_reduce(picks[:, :, :], tmp[:, :, :, :], AX.X, ALU.add))
                dve.tensor_copy(slot[:, :], picks[:, :, :].rearrange("p t k -> p (t k)")).then_inc(s["slots_ready"], 1)
                link(dve.tensor_scalar(out_row[:, :], picks[:, :, :].rearrange("p t k -> p (t k)"), float(P), None, ALU.add))
                link(dve.tensor_tensor(grid[:, :, :], line[0:1, 2, :].unsqueeze(1).broadcast_to([1, ITEMS, EXPERTS]),
                                       item[:, :].unsqueeze(2).broadcast_to([1, ITEMS, EXPERTS]), ALU.is_le))
                link(dve.tensor_reduce(found[:, :], grid[:, :, :], AX.X, ALU.add))
                link(dve.tensor_scalar(work[:, :], found[:, :], float(EXPERTS - 1), None, ALU.min))
                link(dve.tensor_copy(total[:, :], line[0:1, 2, EXPERTS - 1:EXPERTS]))
                dve.wait_ge(s["weights_turned"], 1)
                link(dve.tensor_copy(wtT[:, :], bank[6][0:EXPERTS, :]))
        sem.over()

    with ExitStack() as st:
        def tb(name, shape, dt=F32):
            return st.enter_context(nc.sbuf_tensor(name, shape, dt))
        UNITS, RAW, SPLIT = 12, 6, 4
        ring4 = ring[:, :, :, :].rearrange("p a k n -> p (a k n)").rearrange("p (r n) -> p r n", r=4)
        raw2 = tb("raw_units", [P, 2, 2048])
        raw = [ring4[:, r, :] for r in range(4)] + [raw2[:, r, :] for r in range(2)]
        uh, ul = tb("unit_high", [P, SPLIT, 2048], F32R), tb("unit_low", [P, SPLIT, 2048], F32R)
        index = tb("item_tokens", [P, 1], I32)
        xg = tb("gathered", [P, D])
        xh, xl, ah, al = (hT[n % 2][:, :, (n // 2) * P:(n // 2 + 1) * P] for n in range(4))
        biasb, ones3 = tb("bias_row_parts", [3, 2 * D], BF16), tb("ones_three", [3, P], BF16)
        gs, sg, ls = tb("gate_part", [P, D]), tb("gate_sigmoid", [P, D]), tb("linear_part", [P, D])
        at, y = tb("activated", [P, D]), tb("expert_rows", [P, D])
        zero_rows = tb("zero_rows", [P, D])
        sem = PhaseSems(nc)
        raw_loaded = [sem(f"raw_loaded{r}") for r in range(RAW)]
        names = ("ones", "index_loaded", "gathered", "xg_turned", "xg_high", "xg_ready", "bias_loaded", "up_ready",
                 "high_ready", "split_ready", "unit_used", "gate_ready", "sigmoid_ready", "act_ready", "act_turned",
                 "act_high", "actT_ready", "y_kept", "y_written", "dve_link", "counted")
        s = {n: sem("moe_" + n) for n in names}
        carrier = sem("moe_carrier_pool")
        w_up = A["w_up_2"][0].rearrange("e k n -> (e k) n")
        w_down = A["w_down_2"][0].rearrange("e k n -> (e k) n")
        bias_rows = A["bias_parts"].rearrange("e a n -> (e a) n")
        four = lambda bk: bk[:, :].rearrange("p (k t) -> p k t", k=4)
        with nc.Block() as block:
            def items(eng, body, skipped=None):
                n = eng.value_load(total[0:1, 0:1], min_val=1, max_val=ITEMS)
                with eng.Fori(0, ITEMS) as i:
                    with eng.If(i < n):
                        body(i)
                    if skipped:
                        with eng.Else():
                            skipped(i)
                    eng.nop()
                return n

            @block.sync
            def _(sp):
                def body(i):
                    e = sp.value_load(work[0:1, bass.ds(i, 1)], min_val=0, max_val=EXPERTS - 1)
                    for u in range(UNITS):
                        held(sp, None, s["split_ready"], UNITS * i + u + 1)
                        dst = raw[u % RAW].rearrange("p (k n) -> p k n", k=2)
                        if u < 8:
                            c, j = u // 4, u % 4
                            src = w_up[bass.ds(e * D + j * 2 * P, 2 * P), :].rearrange("(k q) (s n) -> q k s n", q=P, s=2)
                            for k in range(2):
                                sp.dma_start(dst[:, k, :].rearrange("p (s n) -> p s n", s=2),
                                             src[:, k, :, c * 512:(c + 1) * 512]).then_inc(raw_loaded[u % RAW], 16)
                        else:
                            src = w_down[bass.ds(e * D + (u - 8) * 2 * P, 2 * P), :].rearrange("(k q) n -> q k n", q=P)
                            for k in range(2):
                                sp.dma_start(dst[:, k, :], src[:, k, :]).then_inc(raw_loaded[u % RAW], 16)
                        if u == 0:
                            held(sp, None, s["up_ready"], 2 * i + 1)
                            sp.dma_start(biasb[:, :], bias_rows[bass.ds(e * 3, 3), :]).then_inc(s["bias_loaded"], 16)
                sp.wait_ge(s["counted"], 2)
                items(sp, body)

            @block.gpsimd
            def _(pool):
                for name, n in (("split_ready", RAW), ("unit_used", SPLIT), ("up_ready", 1), ("act_ready", 2),
                                ("y_kept", 1), ("y_written", 16)):
                    pool.sem_inc(s[name], n)
                pool.sem_inc(s["counted"], 1)

                def gather(i):
                    pool.dma_start(index[:, :], A["slot_tokens"][bass.ds(i * P, P), :]).then_inc(s["index_loaded"], 16)
                    held(pool, carrier, s["index_loaded"], 16 * i + 16)
                    pool.indirect_dma_start(xg[:, :], None, A["h2_scratch"],
                                            bass.IndirectOffsetOnAxis(ap=index[:, 0:1], axis=0)).then_inc(s["gathered"], 16)

                def body(i):
                    held(pool, carrier, s["xg_turned"], i + 1)
                    gather(i + 1)
                gather(0)
                items(pool, body)

            @block.tensor
            def _(pe):
                def three(bk, xs, k, ws, first, last):
                    (h, l), (wh, wl) = xs, ws
                    pe.matmul(bk, h[:, k, :], wh, start=first, stop=False)
                    pe.matmul(bk, h[:, k, :], wl, start=False, stop=False)
                    return pe.matmul(bk, l[:, k, :], wh, start=False, stop=last)

                def turn_rows(i):
                    held(pe, None, s["gathered"], 16 * i + 16)
                    for k in range(KT):
                        mm = pe.transpose(bank[k // 4][:, (k % 4) * P:(k % 4 + 1) * P], xg[:, k * P:(k + 1) * P], ident[:, :])
                    mm.then_inc(s["xg_turned"], 1)

                def turn_act(i, c):
                    held(pe, None, s["act_ready"], 2 + 2 * i + c + 1)
                    for k in range(4):
                        mm = pe.transpose(bank[4 + c][:, k * P:(k + 1) * P], at[:, (4 * c + k) * P:(4 * c + k + 1) * P], ident[:, :])
                    mm.then_inc(s["act_turned"], 1)

                def unit(i, u):
                    held(pe, None, s["split_ready"], RAW + UNITS * i + u + 1)
                    for k in range(2):
                        for h in range(2):
                            at_ = slice(k * 1024 + h * 512, k * 1024 + (h + 1) * 512)
                            ws = (uh[:, u % SPLIT, at_], ul[:, u % SPLIT, at_])
                            if u < 8:
                                c, kk = u // 4, 2 * (u % 4) + k
                                mm = three(bank[2 * c + h][:, :], (xh, xl), kk, ws, kk == 0, False)
                            else:
                                kk = 2 * (u - 8) + k
                                mm = three(bank[6 + h][:, :], (ah, al), kk, ws, kk == 0, kk == KT - 1)
                    mm.then_inc(s["unit_used"], 1)

                def bias(c):
                    for h in range(2):
                        mm = pe.matmul(bank[2 * c + h][:, :], ones3[:, :], biasb[:, h * D + c * 512:h * D + (c + 1) * 512],
                                       start=False, stop=True)
                    mm.then_inc(s["up_ready"], 1)

                def body(i):
                    held(pe, None, s["xg_ready"], 2 * i + 2)
                    for u in range(4):
                        unit(i, u)
                    held(pe, None, s["bias_loaded"], 16 * i + 16)
                    bias(0)
                    held(pe, None, s["act_ready"], 2 * i + 2)
                    for u in range(4, 7):
                        unit(i, u)
                    turn_act(i, 0)
                    unit(i, 7)
                    bias(1)
                    held(pe, None, s["actT_ready"], 2 * i + 1)
                    held(pe, None, s["y_kept"], 2 * i + 1)
                    unit(i, 8)
                    unit(i, 9)
                    turn_act(i, 1)
                    turn_rows(i + 1)
                    held(pe, None, s["actT_ready"], 2 * i + 2)
                    unit(i, 10)
                    unit(i, 11)
                pe.wait_ge(s["ones"], 1)
                pe.wait_ge(s["counted"], 2)
                turn_rows(0)
                items(pe, body)

            @block.vector
            def _(dve):
                dve.memset(ones3[:, :], 1.0).then_inc(s["ones"], 1)
                dve.memset(zero_rows[:, :], 0.0).then_inc(s["counted"], 1)
                link = Link(dve, s["dve_link"])

                def low(i, u):
                    held(dve, None, s["high_ready"], UNITS * i + u + 1)
                    dve.tensor_tensor(ul[:, u % SPLIT, :], raw[u % RAW], uh[:, u % SPLIT, :].bitcast(F32), ALU.subtract)\
                       .then_inc(s["split_ready"], 1)

                def rows_low(i):
                    for c in range(2):
                        held(dve, None, s["xg_high"], 2 * i + c + 1)
                        dve.tensor_tensor(xl[:, 4 * c:4 * c + 4, :], four(bank[c]), xh[:, 4 * c:4 * c + 4, :].bitcast(F32),
                                          ALU.subtract).then_inc(s["xg_ready"], 1)

                def act_low(i, c):
                    held(dve, None, s["act_high"], 2 * i + c + 1)
                    dve.tensor_tensor(al[:, 4 * c:4 * c + 4, :], four(bank[4 + c]), ah[:, 4 * c:4 * c + 4, :].bitcast(F32),
                                      ALU.subtract).then_inc(s["actT_ready"], 1)

                def swiglu(i, c):
                    cols = slice(c * 512, (c + 1) * 512)
                    held(dve, None, s["up_ready"], 1 + 2 * i + c + 1)
                    dve.tensor_scalar(gs[:, cols], bank[2 * c][:, :], 7.0, None, ALU.min).then_inc(s["gate_ready"], 1)
                    link(dve.tensor_scalar(ls[:, cols], bank[2 * c + 1][:, :], 7.0, -7.0, ALU.min, ALU.max))
                    link(dve.scalar_tensor_tensor(ls[:, cols], ls[:, cols], 1.0, gs[:, cols], ALU.add, ALU.mult))
                    held(dve, None, s["sigmoid_ready"], 2 * i + c + 1)
                    dve.tensor_tensor(at[:, cols], ls[:, cols], sg[:, cols], ALU.mult).then_inc(s["act_ready"], 1)

                def body(i):
                    link.turn(0, i, 4)
                    for u in range(8):
                        low(i, u)
                    swiglu(i, 0)
                    low(i, 8)
                    act_low(i, 0)
                    low(i, 9)
                    low(i, 10)
                    swiglu(i, 1)
                    low(i, 11)
                    act_low(i, 1)
                    rows_low(i + 1)
                dve.wait_ge(s["counted"], 2)
                rows_low(0)
                items(dve, body)

            @block.scalar
            def _(act):
                def high(i, u):
                    r = u % RAW
                    held(act, None, raw_loaded[r], 64 * i + 32 * (u // RAW) + 32)
                    held(act, None, s["unit_used"], UNITS * i + u + 1)
                    act.activation(uh[:, u % SPLIT, :], raw[r], ACT.Copy).then_inc(s["high_ready"], 1)

                def rows_high(i):
                    held(act, None, s["xg_turned"], i + 1)
                    for c in range(2):
                        act.activation(xh[:, 4 * c:4 * c + 4, :], four(bank[c]), ACT.Copy).then_inc(s["xg_high"], 1)

                def act_high(i, c):
                    held(act, None, s["act_turned"], 2 * i + c + 1)
                    act.activation(ah[:, 4 * c:4 * c + 4, :], four(bank[4 + c]), ACT.Copy).then_inc(s["act_high"], 1)

                def sigmoid(i, c):
                    cols = slice(c * 512, (c + 1) * 512)
                    held(act, None, s["gate_ready"], 2 * i + c + 1)
                    act.activation(sg[:, cols], gs[:, cols], ACT.Sigmoid, scale=1.702).then_inc(s["sigmoid_ready"], 1)

                def keep_rows(i):
                    held(act, None, s["unit_used"], SPLIT + UNITS * i)
                    held(act, None, s["y_written"], 16 * i + 16)
                    for n in range(2):
                        act.activation(y[:, n * 512:(n + 1) * 512], bank[6 + n][:, :], ACT.Copy).then_inc(s["y_kept"], 1)
                    held(act, None, s["y_kept"], 1 + 2 * i + 2)
                    act.dma_start(A["expert_out"][bass.ds(i * P, P), :], y[:, :]).then_inc(s["y_written"], 16)

                def body(i):
                    for u in range(4):
                        high(i, u)
                    keep_rows(i)
                    for u in range(4, 8):
                        high(i, u)
                    sigmoid(i, 0)
                    high(i, 8)
                    high(i, 9)
                    act_high(i, 0)
                    high(i, 10)
                    high(i, 11)
                    sigmoid(i, 1)
                    act_high(i, 1)
                    rows_high(i + 1)

                def skipped(i):
                    act.dma_start(A["expert_out"][bass.ds(i * P + P, P), :], zero_rows[:, :]).then_inc(s["y_written"], 16)
                act.wait_ge(s["counted"], 2)
                for n in range(2):
                    act.activation(bank[6 + n][:, :], zero_rows[:, 0:512], ACT.Copy).then_inc(s["ones"], 1)
                act.wait_ge(s["ones"], 3)
                rows_high(0)
                n = items(act, body, skipped)
                held(act, None, s["unit_used"], n * UNITS + SPLIT)
                act.wait_ge(s["y_written"], ITEMS * 16 + 16)
                for h in range(2):
                    act.activation(y[:, h * 512:(h + 1) * 512], bank[6 + h][:, :], ACT.Copy).then_inc(s["y_kept"], 1)
                held(act, None, s["y_kept"], n * 2 + 3)
                act.dma_start(A["expert_out"][bass.ds(n * P, P), :], y[:, :]).then_inc(s["y_written"], 16)
                act.wait_ge(s["y_written"], ITEMS * 16 + 32)
        sem.over()

    with ExitStack() as st:
        def tb(name, shape, dt=F32):
            return st.enter_context(nc.sbuf_tensor(name, shape, dt))
        back = tb("picked_rows", [P, TT * TOPK, D])
        bd = tb("b_down", [EXPERTS, D])
        sem = PhaseSems(nc)
        b_loaded, b_product, link_sem, added = (sem("combine_" + n) for n in ("b_loaded", "b_product", "link", "added"))
        fetched = [sem(f"combine_fetched{i}") for i in range(TT * TOPK)]
        with nc.Block() as block:
            @block.sync
            def _(sp):
                sp.dma_start(bd[:, :], A["b_down_2"][0]).then_inc(b_loaded, 16)
                sp.wait_ge(fetched[TT * TOPK // 2], 16)
                gemm.load_ahead(sp, block_pieces(ring, A["w_ple_gate_2"][0]))

            @block.gpsimd
            def _(pool):
                for t in range(TT):
                    for k in range(TOPK):
                        j = t * TOPK + k
                        pool.indirect_dma_start(back[:, j, :], None, A["expert_out"],
                                                bass.IndirectOffsetOnAxis(ap=out_row[:, j:j + 1], axis=0))\
                            .then_inc(fetched[j], 16)

            @block.tensor
            def _(pe):
                pe.wait_ge(b_loaded, 16)
                for t in range(TT):
                    for n in range(2):
                        pe.matmul(bank[2 * t + n][:, :], wtT[:, t * P:(t + 1) * P], bd[:, n * 512:(n + 1) * 512],
                                  start=True, stop=True).then_inc(b_product, 1)

            @block.vector
            def _(dve):
                link = Link(dve, link_sem)
                for t in range(TT):
                    for k in range(TOPK):
                        j = t * TOPK + k
                        dve.wait_ge(fetched[j], 16)
                        dve.scalar_tensor_tensor(x[:, t, :], back[:, j, :], wt[:, t, k:k + 1], x[:, t, :],
                                                 ALU.mult, ALU.add).then_inc(added, 1)
                        dve.wait_ge(added, j + 1)
                    for n in range(2):
                        dve.wait_ge(b_product, 2 * t + n + 1)
                        link(dve.tensor_tensor(x[:, t, n * 512:(n + 1) * 512], bank[2 * t + n][:, :],
                                               x[:, t, n * 512:(n + 1) * 512], ALU.add))
        sem.over()
    gemm.ahead = True
    outer.close()


def last_stage(nc, A, sem, sb, bank, ident, vecT, x, hT, ring, gemm, out_rows, out_written):
    with ExitStack() as st:
        def tb(name, shape, dt=F32):
            return st.enter_context(nc.sbuf_tensor(name, shape, dt))
        PD = 256
        pr, pT, wp = tb("ple_input", [P, TT, PD]), tb("ple_T", [P, PD // P, SEQ]), tb("w_ple", [P, PD // P, D])
        gf = tb("ln_f", [P, D])
        s = {n: sem("last_" + n) for n in ("loaded", "turned", "kept", "product", "gated", "link", "squared", "rooted", "scaled")}

        def load_rest(sp):
            sp.dma_start(pr[:, :, :], A["p_2"][0, 0].rearrange("(t q) d -> q t d", q=P)).then_inc(s["loaded"], 16)
            sp.dma_start(wp[:, :, :], A["w_ple_2"][0].rearrange("(k q) n -> q k n", q=P)).then_inc(s["loaded"], 16)
            sp.dma_start(gf[:, :], A["ln_f_2"].unsqueeze(0).broadcast_to([P, D])).then_inc(s["loaded"], 16)
        norm_to_cols(nc, "ple", sem, sb, bank, ident, x, VAT["ln_ple_2"], vecT, hT, meanwhile=load_rest)
        sg = tb("ple_gate", [P, TT, D])
        gemm.phase(1, block_pieces(ring, A["w_ple_gate_2"][0]), rows_of(hT),
                   gemm.drain("act", range(4), lambda eng, p, b, j, bk: eng.activation(sg[:, j, b * 512:(b + 1) * 512], bk[:, :],
                                                                                       ACT.Sigmoid)))
        tmp, stat = tb("ple_tmp", [P, 2, D]), tb("final_stat", [P, 3, TT])
        with nc.Block() as block:
            @block.sync
            def _(sp):
                for t in range(TT):
                    sp.wait_ge(s["scaled"], t + 1)
                    sp.dma_start(out_rows[:, t, :], x[:, t, :]).then_inc(out_written, 16)
                sp.wait_ge(out_written, 16 * TT)

            @block.tensor
            def _(pe):
                pe.wait_ge(s["loaded"], 48)
                for k in range(PD // P):
                    for t in range(TT):
                        mm = pe.transpose(bank[k][:, t * P:(t + 1) * P], pr[:, t, k * P:(k + 1) * P], ident[:, :])
                    mm.then_inc(s["turned"], 1)
                pe.wait_ge(s["kept"], 2)
                for t in range(TT):
                    for n in range(2):
                        for k in range(PD // P):
                            mm = pe.matmul(bank[2 * t + n][:, :], pT[:, k, t * P:(t + 1) * P], wp[:, k, n * 512:(n + 1) * 512],
                                           start=k == 0, stop=k == PD // P - 1)
                        mm.then_inc(s["product"], 1)

            @block.scalar
            def _(act):
                for k in range(2):
                    act.wait_ge(s["turned"], k + 1)
                    act.activation(pT[:, k, :], bank[k][:, :], ACT.Copy).then_inc(s["kept"], 1)
                for t in range(TT):
                    act.wait_ge(s["link"], 4 * t + 4)
                    if t:
                        act.wait_ge(s["squared"], t)
                    act.activation(sg[:, 0, :], x[:, t, :], ACT.Square, accum_out=stat[:, 0, t:t + 1]).then_inc(s["squared"], 1)
                act.wait_ge(s["link"], 4 * TT + 1)
                act.activation(stat[:, 2, :], stat[:, 1, :], ACT.Sqrt).then_inc(s["rooted"], 1)

            @block.vector
            def _(dve):
                link = Link(dve, s["link"])
                for t in range(TT):
                    for n in range(2):
                        dve.wait_ge(s["product"], 2 * t + n + 1)
                        cols = slice(n * 512, (n + 1) * 512)
                        link(dve.tensor_tensor(tmp[:, 0, cols], bank[2 * t + n][:, :], sg[:, t, cols], ALU.mult))
                        link(dve.tensor_tensor(x[:, t, cols], x[:, t, cols], tmp[:, 0, cols], ALU.add))
                dve.wait_ge(s["squared"], TT)
                dve.wait_ge(s["loaded"], 48)
                link(dve.tensor_scalar(stat[:, 1, :], stat[:, 0, :], 1.0 / D, EPS, ALU.mult, ALU.add))
                dve.wait_ge(s["rooted"], 1)
                link(dve.reciprocal(stat[:, 0, :], stat[:, 2, :]))
                for t in range(TT):
                    dve.scalar_tensor_tensor(x[:, t, :], x[:, t, :], stat[:, 0, t:t + 1], gf[:, :], ALU.mult, ALU.mult)\
                       .then_inc(s["scaled"], 1)


def bias_columns():
    import numpy as np
    m = np.zeros((BUCKETS + 1, SHEAR), np.float32)
    half = BUCKETS // 2
    for c in range(SHEAR):
        n = 2 * P - 1 - c
        if n < 0:
            m[BUCKETS, c] = NEG
            continue
        b = n if n < half else min(half + int(math.log(max(n, 1) / half) / math.log(128 / half) * (BUCKETS - half)), BUCKETS - 1)
        m[b, c] += 1.0
        m[BUCKETS - 1, c] -= 1.0
    return m


def build(nc, A, out, stop=None):
    outer = ExitStack()
    with outer:
        def sem(name):
            return outer.enter_context(nc.semaphore(name))

        def sb(name, shape, dt=F32):
            return outer.enter_context(nc.sbuf_tensor(name, shape, dt))

        bank = [outer.enter_context(nc.psum_tensor(f"bank{i}", [P, 512], F32)) for i in range(8)]
        out_rows = out[0].rearrange("(t p) d -> p t d", p=P)

        ident = sb("ident", [P, P])
        vecT = sb("vecT", [P, NVEC])
        x = sb("x_rows", [P, TT, D])
        hT = (sb("hT_high", [P, KT, SEQ], F32R), sb("hT_low", [P, KT, SEQ], F32R))
        gemm = Gemm(nc, sem, sb, bank)
        ring = gemm.ring
        out_written = sem("out_written")

        def finish(rows):
            with nc.Block() as block:
                @block.sync
                def _(sp):
                    sp.dma_start(out_rows, rows).then_inc(out_written, 16)
                    sp.wait_ge(out_written, 16)

        first = ExitStack()
        rnnT = first.enter_context(nc.sbuf_tensor("rnnT", [P, KT, SEQ], F32))
        biasE = first.enter_context(nc.sbuf_tensor("biasE", [P, HEADS, 2 * P], F32))
        neg_lam = first.enter_context(nc.sbuf_tensor("neg_lam", [P, 1], F32))

        w_in = A["w_in"][0]
        QKW = 3 * D
        recurrent = block_pieces(ring, w_in, col0=QKW)

        with ExitStack() as st:
            vec = st.enter_context(nc.sbuf_tensor("vec", [NVEC, P], F32))
            lv = st.enter_context(nc.sbuf_tensor("lambda_vectors", [P, 4, HD], F32))
            lp = st.enter_context(nc.sbuf_tensor("lambda_products", [P, 2, HD], F32))
            ls = st.enter_context(nc.sbuf_tensor("lambda_sums", [P, 4], F32))
            rb = st.enter_context(nc.sbuf_tensor("rel_bias", [BUCKETS + 1, HEADS], F32))
            rbb = st.enter_context(nc.sbuf_tensor("rel_bias_wide", [BUCKETS + 1, HEADS, P], F32))
            cols = st.enter_context(nc.sbuf_tensor("bias_columns", [BUCKETS + 1, SHEAR], F32))
            rep = st.enter_context(nc.sbuf_tensor("bias_rows", [P, HEADS, SHEAR], F32))
            zeroed, ident_ready, vec_loaded, x_loaded, lam_loaded, bias_loaded, ones_ready = (
                sem(n) for n in ("zeroed", "ident_ready", "vec_loaded", "x_loaded", "lam_loaded", "bias_loaded", "ones_ready"))
            vec_turned, rows_product, rows_ready, sheared, lam_summed, lam_exp, dve_link, bias_ready = (
                sem("setup_" + n) for n in ("vec_turned", "rows_product", "rows_ready", "sheared",
                                            "lam_summed", "lam_exp", "dve_link", "bias_ready"))
            flat = A["bias_scratch"]
            nvec_dma = len(VECS) + 4
            with nc.Block() as block:
                @block.sync
                def _(sp):
                    for name, k in VECS:
                        r = VAT[name]
                        sp.dma_start(vec[r:r + k, :], A[name]).then_inc(vec_loaded, 16)
                    for name in ("q_norm_g", "k_norm_g"):
                        for half in range(2):
                            sp.dma_start(vec[VAT[name]:VAT[name] + 1, half * HD:(half + 1) * HD], A[name])\
                              .then_inc(vec_loaded, 16)
                    sp.wait_ge(ones_ready, 1)
                    sp.dma_start(rb[0:BUCKETS, :], A["rel_bias"]).then_inc(bias_loaded, 16)
                    sp.dma_start(cols[:, :], A["bias_columns"]).then_inc(bias_loaded, 16)
                    sp.dma_start(x[:, :, :], A["x"][0].rearrange("(t p) d -> p t d", p=P)).then_inc(x_loaded, 16)
                    for i, n in enumerate(("lambda_q1", "lambda_k1", "lambda_q2", "lambda_k2")):
                        sp.dma_start(lv[:, i, :], A[n].broadcast_to([P, HD])).then_inc(lam_loaded, 16)
                    gemm.load_ahead(sp, recurrent)
                    sp.wait_ge(rows_ready, HEADS)
                    sp.dma_start(flat.rearrange("(h p m) -> p h m", h=HEADS, p=P), rep[:, :, :]).then_inc(sheared, 16)
                    sp.wait_ge(x_loaded, 16)

                @block.gpsimd
                def _(pool):
                    pool.memset(ident[:, :], 0.0).then_inc(zeroed, 1)
                    pool.wait_ge(zeroed, 1)
                    pool.affine_select(out=ident[:, :], in_=ident[:, :], compare_op=ALU.not_equal, fill=1.0, base=0,
                                       pattern=[[-1, P]], channel_multiplier=1).then_inc(ident_ready, 1)

                @block.vector
                def _(dve):
                    link = Link(dve, dve_link)
                    link(dve.memset(rbb[:, :, :], 1.0))
                    dve.memset(rb[:, :], 1.0).then_inc(ones_ready, 1)
                    dve.wait_ge(bias_loaded, 32)
                    for h in range(HEADS):
                        link(dve.tensor_scalar(rbb[:, h, :], rbb[:, h, :], rb[:, h:h + 1], None, ALU.mult))
                    dve.wait_ge(vec_turned, 1)
                    link(dve.tensor_copy(vecT[:, :], bank[0][:, 0:NVEC]))
                    link(dve.tensor_scalar(vecT[:, VAT["k_norm_g"]:VAT["k_norm_g"] + 1],
                                           vecT[:, VAT["k_norm_g"]:VAT["k_norm_g"] + 1], HD ** -0.5, None, ALU.mult))
                    link(dve.tensor_scalar(vecT[:, VAT["subln_g"]:VAT["subln_g"] + 1],
                                           vecT[:, VAT["subln_g"]:VAT["subln_g"] + 1], 1.0 - 0.2, None, ALU.mult))
                    dve.wait_ge(lam_loaded, 64)
                    link(dve.tensor_tensor(lp[:, :, :], lv[:, 0:4:2, :], lv[:, 1:4:2, :], ALU.mult))
                    dve.tensor_reduce(ls[:, 0:2], lp[:, :, :], AX.X, ALU.add).then_inc(lam_summed, 1)
                    dve.wait_ge(lam_exp, 1)
                    dve.scalar_tensor_tensor(neg_lam[:, :], ls[:, 3:4], -0.2, ls[:, 2:3], ALU.add, ALU.subtract)\
                       .then_inc(dve_link, 1)

                @block.scalar
                def _(act):
                    act.wait_ge(lam_summed, 1)
                    act.activation(ls[:, 2:4], ls[:, 0:2], ACT.Exp).then_inc(lam_exp, 1)
                    for h in range(HEADS):
                        act.wait_ge(rows_product, h + 1)
                        act.activation(rep[:, h, :], bank[(h + 1) % 8][:, 0:SHEAR], ACT.Copy).then_inc(rows_ready, 1)

                @block.tensor
                def _(pe):
                    pe.wait_ge(ident_ready, 1)
                    pe.wait_ge(vec_loaded, 16 * nvec_dma)
                    pe.transpose(bank[0][:, 0:NVEC], vec[:, :], ident[0:NVEC, 0:NVEC]).then_inc(vec_turned, 1)
                    pe.wait_ge(dve_link, 1 + HEADS + 1)
                    for h in range(HEADS):
                        pe.matmul(bank[(h + 1) % 8][:, 0:SHEAR], rbb[:, h, :], cols[:, :], start=True, stop=True)\
                          .then_inc(rows_product, 1)

            def read_bias(sp):
                sp.wait_ge(sheared, 16)
                for h in range(HEADS):
                    at = h * P * SHEAR + P - 1
                    sp.dma_start(biasE[:, h, :], flat[at:at + P * (SHEAR - 1)]
                                 .rearrange("(p m) -> p m", p=P)[:, 0:2 * P]).then_inc(bias_ready, 16)
                sp.wait_ge(bias_ready, 16 * HEADS)
            norm_to_cols(nc, "mix", sem, sb, bank, ident, x, VAT["norm_mix_g"], vecT, hT, meanwhile=read_bias)

        gemm.ahead = True

        def copies(dst):
            return (gemm.drain("act", (0, 2), lambda eng, p, b, j, bk: eng.activation(dst(p, b, j), bk[:, :], ACT.Copy)),
                    gemm.drain("dve", (1, 3), lambda eng, p, b, j, bk: eng.tensor_copy(dst(p, b, j), bk[:, :])))
        residual = gemm.drain("dve", range(4), lambda eng, p, b, j, bk: eng.tensor_tensor(
            x[:, j, b * 512:(b + 1) * 512], bk[:, :], x[:, j, b * 512:(b + 1) * 512], ALU.add))

        with ExitStack() as st:
            XG = st.enter_context(nc.sbuf_tensor("XG", [P, 2, KT, SEQ], F32))
            gemm.phase(2, recurrent, cols_of(hT), *copies(lambda p, b, j: XG[:, p, 4 * b + j, :]),
                       following=block_pieces(ring, w_in))
            lru(nc, sem, bank, vecT, XG, A["w_rg_a"][0], A["w_rg_x"][0], rnnT)

        O = first.enter_context(nc.sbuf_tensor("diff_out", [P, TT, D], F32))
        with ExitStack() as st:
            QKV = st.enter_context(nc.sbuf_tensor("QKV", [P, 3, TT, D], F32))
            gates_in = block_pieces(ring, w_in, col0=QKW + 2 * D)
            gemm.phase(3, block_pieces(ring, w_in), rows_of(hT), *copies(lambda p, b, j: QKV[:, p, j, b * 512:(b + 1) * 512]),
                       following=gates_in)
            diff_attention(nc, sem, bank, ident, vecT, QKV, biasE, neg_lam, O)
        mixT = tuple(first.enter_context(nc.sbuf_tensor(n, [P, KT, SEQ], F32R)) for n in ("mixT_high", "mixT_low"))
        with ExitStack() as st:
            sq = st.enter_context(nc.sbuf_tensor("subln_sq", [P, TT, D], F32))
            ss = st.enter_context(nc.sbuf_tensor("subln_stat", [P, TT * HEADS], F32))
            s1, s2, s3, s4 = (sem("subln_" + n) for n in ("squared", "dve_link", "rooted", "normed"))
            grouped = lambda t: t[:, :, :].rearrange("p t (h d) -> p (t h) d", d=P)
            with nc.Block() as block:
                @block.scalar
                def _(act):
                    act.activation(sq[:, :, :], O[:, :, :], ACT.Square).then_inc(s1, 1)
                    act.wait_ge(s2, 2)
                    act.activation(ss[:, :], ss[:, :], ACT.Sqrt).then_inc(s3, 1)

                @block.vector
                def _(dve):
                    link = Link(dve, s2)
                    dve.wait_ge(s1, 1)
                    link(dve.tensor_reduce(ss[:, :], grouped(sq), AX.X, ALU.add))
                    link(dve.tensor_scalar(ss[:, :], ss[:, :], 1.0 / P, EPS, ALU.mult, ALU.add))
                    dve.wait_ge(s3, 1)
                    link(dve.reciprocal(ss[:, :], ss[:, :]))
                    dve.tensor_tensor(grouped(O), grouped(O), ss[:, :].unsqueeze(2).broadcast_to([P, TT * HEADS, P]),
                                      ALU.mult).then_inc(s4, 1)
            transpose_rows(nc, "attn_out", sem, bank, ident, O, KT, mixT, vecT[:, VAT["subln_g"]:VAT["subln_g"] + 1])

        GA = O[:, :, :].rearrange("p t d -> p (t d)").rearrange("p (k s) -> p k s", k=KT)
        with ExitStack() as st:
            GR = st.enter_context(nc.sbuf_tensor("rnn_gateT", [P, KT, SEQ], F32))
            merged = sem("merged")
            both = (GA, GR)

            def gates(act, p, b):
                if p < 2:
                    gemm.drain("act", range(4), lambda eng, p, b, j, bk: eng.activation(both[p][:, 4 * b + j, :], bk[:, :],
                                                                                        ACT.Sigmoid))(act, p, b)

            def gated(dve, p, b):
                if p == 2:
                    if b == 0:
                        for j in range(4):
                            dve.wait_ge(gemm.drained[j], 2 * (p + gemm.done))
                    gemm.drain("dve", range(4), lambda eng, p, b, j, bk: eng.tensor_tensor(
                        GA[:, 4 * b + j, :], bk[:, :], GA[:, 4 * b + j, :], ALU.mult))(dve, p, b)
            gate_pieces, attn_pieces = gates_in, block_pieces(ring, A["w_proj_attn"][0])
            gemm.phase(3, lambda p, b: gate_pieces(p, b) if p < 2 else attn_pieces(0, b),
                       lambda p: cols_of(hT if p < 2 else mixT), gates, gated, unrolled=True,
                       following=block_pieces(ring, A["w_proj_rnn"][0]))
            split_cols(nc, "rnn", sem, rnnT, mixT)

            def gate_and_add(eng, p, b):
                for j in range(4):
                    n = 4 * b + j
                    eng.wait_ge(gemm.product, 4 * (2 * gemm.done + b) + j + 1)
                    eng.tensor_tensor(GR[:, n, :], bank[n][:, :], GR[:, n, :], ALU.mult).then_inc(gemm.drained[j], 1)
                    eng.wait_ge(gemm.drained[j], 2 * gemm.done + b + 1)
                    eng.tensor_tensor(GA[:, n, :], GA[:, n, :], GR[:, n, :], ALU.add).then_inc(merged, 1)
            gemm.phase(1, block_pieces(ring, A["w_proj_rnn"][0]), cols_of(mixT), None, gate_and_add,
                       following=block_pieces(ring, A["w_out"][0]))
            split_cols(nc, "merge", sem, GA, mixT)
            gemm.phase(1, block_pieces(ring, A["w_out"][0]), rows_of(mixT), None, residual,
                       following=block_pieces(ring, A["w_up"][0]))
        first.close()

        norm_to_cols(nc, "mlp", sem, sb, bank, ident, x, VAT["norm_mlp_g"], vecT, hT)
        with ExitStack() as st:
            HALF = FF // 2
            upT = tuple(st.enter_context(nc.sbuf_tensor(n, [P, HALF // P, SEQ], F32R)) for n in ("upT_high", "upT_low"))
            act_in = st.enter_context(nc.sbuf_tensor("up_squares", [P, 4, SEQ], F32))
            squared, high_done, low_done = (sem("up_" + n) for n in ("squared", "high_done", "low_done"))

            def down_pieces(half):
                def pieces(p, b):
                    src = A["w_down"][0][bass.ds(p * D + half * HALF, D), b * 512:(b + 1) * 512]\
                        .rearrange("(k q) n -> q k n", q=P)
                    return [(ring[:, b, 0:4, :], src[:, 0:4, :]), (ring[:, b, 4:8, :], src[:, 4:8, :])]
                return pieces
            pairs = 4 * 2
            is_up, half_of = (lambda p: p % 4 < 2), (lambda p: p // 4)
            up_pieces = [block_pieces(ring, A["w_up"][0], col0=h * HALF) for h in range(2)]
            n_of = lambda p, b: 16 * half_of(p) + 8 * (p % 4) + 4 * b

            def mlp_pieces(p, b):
                return (up_pieces if is_up(p) else [down_pieces(h) for h in range(2)])[half_of(p)](p % 2, b)

            def mlp_operands(p):
                if is_up(p):
                    return cols_of(hT)
                return lambda w, part, j, k: (upT[part][:, 8 * (p % 2) + k, j * P:(j + 1) * P], w)

            def act_drain(act, p, b):
                if not is_up(p):
                    return
                for j in range(4):
                    act.wait_ge(gemm.product, 4 * (2 * (p + gemm.done) + b) + j + 1)
                    if n_of(p, b):
                        act.wait_ge(low_done, n_of(p, b) - 3 + j)
                    if p == 4 and b == 0:
                        act.wait_ge(gemm.drained[j], 2 * (p + gemm.done))
                    act.activation(act_in[:, j, :], bank[4 * b + j][:, :], ACT.Relu).then_inc(gemm.drained[j], 1)
                for j in range(4):
                    act.wait_ge(squared, n_of(p, b) + j + 1)
                    act.activation(upT[0][:, n_of(p, b) % 16 + j, :], act_in[:, j, :], ACT.Copy).then_inc(high_done, 1)

            def dve_drain(dve, p, b):
                if not is_up(p):
                    if p % 2:
                        residual(dve, p, b)
                    return
                for j in range(4):
                    dve.wait_ge(gemm.drained[j], 2 * (p + gemm.done) + b + 1)
                    dve.tensor_tensor(act_in[:, j, :], act_in[:, j, :], act_in[:, j, :], ALU.mult).then_inc(squared, 1)
                for j in range(4):
                    dve.wait_ge(high_done, n_of(p, b) + j + 1)
                    dve.tensor_tensor(upT[1][:, n_of(p, b) % 16 + j, :], act_in[:, j, :],
                                      upT[0][:, n_of(p, b) % 16 + j, :].bitcast(F32), ALU.subtract).then_inc(low_done, 1)
                if p % 2 and b:
                    for j in range(4):
                        dve.sem_inc(gemm.drained[j], 2)

            def up_ready(pe, p):
                if not is_up(p):
                    pe.wait_ge(low_done, 16 * (half_of(p) + 1))
            gemm.phase(pairs, mlp_pieces, mlp_operands, act_drain, dve_drain, unrolled=True, before=up_ready,
                       spans=lambda p: (is_up(p) or p % 2 == 0, is_up(p) or p % 2 == 1),
                       following=second_cols(ring, A["w_in_2"][0]))
        if stop == "first":
            finish(x[:, :, :])
            return
        second_layer(nc, A, outer, sem, sb, bank, ident, vecT, x, hT, gemm, out_rows, out_written, residual, stop)


_OUT_SHAPE = (1, SEQ, D)
_VECTOR = {n for n, _ in VECS}


def kernel(**inputs):
    import numpy as np
    import concourse.bacc as bacc
    from concourse.bass_utils import run_bass_kernel_spmd

    nc = bacc.Bacc("TRN2", target_bir_lowering=False, num_devices=1)
    arrays, A = {}, {}
    inputs = dict(inputs)
    inputs["bias_columns"] = bias_columns()
    for name, value in inputs.items():
        a = np.ascontiguousarray(value)
        if name in _VECTOR:
            a = a.reshape(-1, P)
        arrays[f"in_{name}"] = a
        A[name] = nc.dram_tensor(f"in_{name}", a.shape, mybir.dt.from_np(a.dtype), kind="ExternalInput").ap()
    A["bias_scratch"] = nc.dram_tensor("bias_scratch", (HEADS * P * SHEAR,), F32, kind="Internal").ap()
    A["h2_scratch"] = nc.dram_tensor("h2_scratch", (SEQ, D), F32, kind="Internal").ap()
    A["slot_tokens"] = nc.dram_tensor("slot_tokens", ((ITEMS + 1) * P, 1), I32, kind="Internal").ap()
    A["expert_out"] = nc.dram_tensor("expert_out", ((ITEMS + 1) * P, D), F32, kind="Internal").ap()
    A["bias_parts"] = nc.dram_tensor("bias_parts", (EXPERTS, 3, 2 * D), BF16, kind="Internal").ap()
    out = nc.dram_tensor("out_rows", _OUT_SHAPE, F32, kind="ExternalOutput").ap()
    A["ln2_row"] = A["ln2_2"].rearrange("k p -> (k p)").unsqueeze(0)
    build(nc, A, out, STOP)
    r = run_bass_kernel_spmd(nc, [arrays], core_ids=[0])
    return r.results[0]["out_rows"]


STOP = None
```
